# Optimizing a Trainium2 kernel written in Bass

```python
import math
import jax
import jax.numpy as jnp
from jax import lax
import numpy as np

D_MODEL = 1024
BATCH = 1
SEQ = 256
DEPTH = 2

GRID_W = 64
CTX_LEN = 256

RWKV_HEAD = 64
RWKV_WIDTH = D_MODEL
RWKV_HEADS = RWKV_WIDTH // RWKV_HEAD
LORA_W = 64
LORA_A = 64
LORA_G = 160
GN_EPS = RWKV_HEAD * 1e-5

CONV_CH = D_MODEL
CONV_K = 31

PEER_HEADS = 8
PEER_NKEYS = 128
PEER_EXPERTS = PEER_NKEYS * PEER_NKEYS
PEER_QDIM = 256
PEER_HALF = PEER_QDIM // 2
PEER_TOPK = 16
PEER_CHUNK = 256

N_BRANCH = 2
NORM_EPS = 1e-6
LN_EPS = 1e-5

P_RWKV = 3 * RWKV_WIDTH + 2 * LORA_W + 2 * LORA_A + LORA_G
P_CONV = 2 * CONV_CH
P_GATE = N_BRANCH * D_MODEL
P_IN = P_RWKV + P_CONV + P_GATE
RWKV_SPLITS = (RWKV_WIDTH, 2 * RWKV_WIDTH, 3 * RWKV_WIDTH,
               3 * RWKV_WIDTH + LORA_W, 3 * RWKV_WIDTH + 2 * LORA_W,
               3 * RWKV_WIDTH + 2 * LORA_W + LORA_A, 3 * RWKV_WIDTH + 2 * LORA_W + 2 * LORA_A)


def rmsnorm(x, g):
    xf = x.astype(jnp.float32)
    y = xf * lax.rsqrt(jnp.mean(xf * xf, axis=-1, keepdims=True) + NORM_EPS)
    return (y * g.astype(jnp.float32)).astype(x.dtype)

def layernorm(x, g, b):
    xf = x.astype(jnp.float32)
    mu = jnp.mean(xf, axis=-1, keepdims=True)
    var = jnp.mean(jnp.square(xf - mu), axis=-1, keepdims=True)
    return ((xf - mu) * lax.rsqrt(var + LN_EPS) * g + b).astype(x.dtype)

def modulate(x, g, shift, scale):
    return rmsnorm(x, g) * (1 + scale) + shift

def token_shift(z, mu):
    zp = jnp.pad(z[:, :-1], ((0, 0), (1, 0), (0, 0)))
    zn = jnp.pad(z[:, 1:], ((0, 0), (0, 1), (0, 0)))
    return z + mu[0] * (zp - z) + mu[1] * (zn - z)

def rwkv_scan(decay, k, v, kk, a, r, s0, reverse):
    emit = r is not None
    seq = (decay, k, v, kk, a) + ((r,) if emit else ())
    xs = tuple(jnp.moveaxis(t.astype(jnp.float32), 1, 0) for t in seq)

    def step(S, inp):
        w_t, k_t, v_t, kk_t, a_t = inp[:5]
        sa = jnp.einsum('bhvk,bhk->bhv', S, kk_t)
        S = (S * w_t[:, :, None, :]
             - sa[..., None] * (kk_t * a_t)[:, :, None, :]
             + v_t[..., None] * k_t[:, :, None, :])
        y = jnp.einsum('bhvk,bhk->bhv', S, inp[5]) if emit else None
        return S, y

    S, ys = lax.scan(step, s0, xs, reverse=reverse)
    return S, (jnp.moveaxis(ys, 0, 1) if emit else None)

def rwkv_branch(zr, p, s0, emit):
    B, L, _ = zr.shape
    H, N = RWKV_HEADS, RWKV_HEAD
    r, k, v, w1f, w1b, a1f, a1b, g1 = jnp.split(zr, RWKV_SPLITS, axis=-1)
    heads = lambda t: t.reshape(B, L, H, N)
    kkr = heads(k * p['k_k']).astype(jnp.float32)
    kk = kkr / jnp.maximum(jnp.sqrt(jnp.sum(kkr * kkr, axis=-1, keepdims=True)), 1e-12)
    states, outs, bonus = [], [], []
    for d, (w1d, a1d) in enumerate(((w1f, a1f), (w1b, a1b))):
        wlog = -jax.nn.softplus(-(p['w0'][d] + jnp.tanh(w1d) @ p['w2'][d])) - 0.5
        decay = jnp.exp(-jnp.exp(wlog.astype(jnp.float32)))
        a = jax.nn.sigmoid(a1d @ p['a2'][d] + p['a0'][d])
        kd = k * (1 + (a - 1) * p['k_a'])
        S, y = rwkv_scan(heads(decay), heads(kd), heads(v), kk, heads(a),
                         heads(r) if emit else None, s0[d], reverse=(d == 1))
        states.append(S)
        if emit:
            outs.append(y)
            bonus.append(jnp.sum(heads(r * kd) * p['r_k'], axis=-1, keepdims=True))
    if not emit:
        return None, (states[0], states[1])
    o = outs[0] + outs[1]
    mu = jnp.mean(o, axis=-1, keepdims=True)
    var = jnp.mean(jnp.square(o - mu), axis=-1, keepdims=True)
    o = ((o - mu) * lax.rsqrt(var + GN_EPS)).reshape(B, L, RWKV_WIDTH) * p['lnx_g'] + p['lnx_b']
    o = o + ((bonus[0] + bonus[1]).astype(jnp.float32) * heads(v).astype(jnp.float32)).reshape(B, L, RWKV_WIDTH)
    g = jax.nn.sigmoid(g1) @ p['g2']
    y = (o.astype(zr.dtype) * g) @ p['w_oA']
    return y, (states[0], states[1])

def conv_branch(zc, p, rows):
    B, L, _ = zc.shape
    u = zc[..., :CONV_CH] * jax.nn.sigmoid(zc[..., CONV_CH:])
    img = u.reshape(B, rows, GRID_W, CONV_CH) if rows is not None else u[:, :, None, :]
    rhs = p['conv_w'][:, None, None, :].astype(img.dtype)
    out = lax.conv_general_dilated(img, rhs, window_strides=(1, 1),
                                   padding=((CONV_K // 2, CONV_K // 2), (0, 0)),
                                   dimension_numbers=('NHWC', 'HWIO', 'NHWC'),
                                   feature_group_count=CONV_CH)
    out = layernorm(out.reshape(B, L, CONV_CH), p['cnorm_g'], p['cnorm_b'])
    return jax.nn.silu(out) @ p['w_oB']

def token_mixer(h, p, rows, s0, emit):
    w_in = p['w_in'] if emit else p['w_in'][:, :P_RWKV]
    z = h @ w_in
    zr = token_shift(z[..., :P_RWKV], p['shift_mu'])
    y_a, states = rwkv_branch(zr, p, s0, emit)
    if not emit:
        return None, states
    y_b = conv_branch(z[..., P_RWKV:P_RWKV + P_CONV], p, rows)
    gates = jax.nn.sigmoid(z[..., P_RWKV + P_CONV:] + p['gate_b'])
    m = gates[..., :D_MODEL] * y_a + gates[..., D_MODEL:] * y_b
    return m @ p['w_out'], states

def peer(h, p):
    B, L, D = h.shape
    T = B * L
    chunk = math.gcd(T, PEER_CHUNK)
    hb = h.reshape(T // chunk, chunk, D)

    def block(hc):
        q = (hc @ p['w_q']).reshape(chunk, PEER_HEADS, 2, PEER_HALF)
        s = jnp.einsum('thcd,hcnd->thcn', q, p['sub_keys']).astype(jnp.float32)
        s1, i1 = lax.top_k(s[:, :, 0], PEER_TOPK)
        s2, i2 = lax.top_k(s[:, :, 1], PEER_TOPK)
        cand = (s1[..., :, None] + s2[..., None, :]).reshape(chunk, PEER_HEADS, PEER_TOPK * PEER_TOPK)
        cidx = (i1[..., :, None] * PEER_NKEYS + i2[..., None, :]).reshape(chunk, PEER_HEADS, PEER_TOPK * PEER_TOPK)
        best, pos = lax.top_k(cand, PEER_TOPK)
        eidx = jnp.take_along_axis(cidx, pos, axis=-1)
        gw = jax.nn.softmax(best, axis=-1)
        u = jnp.take(p['peer_u'], eidx, axis=0)
        act = jax.nn.gelu(jnp.einsum('td,thkd->thk', hc, u).astype(jnp.float32), approximate=False) * gw
        v = jnp.take(p['peer_v'], eidx, axis=0)
        return jnp.einsum('thk,thkd->td', act.astype(hc.dtype), v)

    return lax.map(block, hb).reshape(B, L, D)

def first_inputs(seed: int = 0) -> dict:
    key = jax.random.key(seed)
    ks = jax.random.split(key, 40)
    f32 = jnp.float32
    nrm = lambda k, shape, s: jax.random.normal(k, shape, f32) * s
    Ly, D, W, H = DEPTH, D_MODEL, RWKV_WIDTH, RWKV_HEADS
    return {
        'x': nrm(ks[0], (BATCH, SEQ, D), 1.0),
        'c': nrm(ks[1], (BATCH, D), 1.0),
        'ctx': nrm(ks[2], (BATCH, CTX_LEN, D), 1.0),
        'c_ctx': nrm(ks[3], (D,), 1.0),
        'ada_w': nrm(ks[4], (Ly, D, 6 * D), 0.5 * D ** -0.5),
        'ada_b': nrm(ks[5], (Ly, 6 * D), 0.02),
        'norm1_g': 1.0 + nrm(ks[6], (Ly, D), 0.02),
        'norm2_g': 1.0 + nrm(ks[7], (Ly, D), 0.02),
        'w_in': nrm(ks[8], (Ly, D, P_IN), D ** -0.5),
        'shift_mu': jax.random.uniform(ks[9], (Ly, 2, P_RWKV), f32, 0.0, 0.5),
        'w0': jax.random.uniform(ks[10], (Ly, 2, W), f32, -6.0, 1.0),
        'w2': nrm(ks[11], (Ly, 2, LORA_W, W), 0.5 * LORA_W ** -0.5),
        'a0': nrm(ks[12], (Ly, 2, W), 0.5),
        'a2': nrm(ks[13], (Ly, 2, LORA_A, W), 0.5 * LORA_A ** -0.5),
        'g2': nrm(ks[14], (Ly, LORA_G, W), LORA_G ** -0.5),
        'k_k': 0.85 + nrm(ks[15], (Ly, W), 0.05),
        'k_a': 1.0 + nrm(ks[16], (Ly, W), 0.05),
        'r_k': nrm(ks[17], (Ly, H, RWKV_HEAD), 0.1),
        'lnx_g': 1.0 + nrm(ks[18], (Ly, W), 0.02),
        'lnx_b': nrm(ks[19], (Ly, W), 0.02),
        'w_oA': nrm(ks[20], (Ly, W, D), W ** -0.5),
        'conv_w': nrm(ks[21], (Ly, CONV_K, CONV_CH), CONV_K ** -0.5),
        'cnorm_g': 1.0 + nrm(ks[22], (Ly, CONV_CH), 0.02),
        'cnorm_b': nrm(ks[23], (Ly, CONV_CH), 0.02),
        'w_oB': nrm(ks[24], (Ly, CONV_CH, D), CONV_CH ** -0.5),
        'gate_b': nrm(ks[25], (Ly, P_GATE), 0.02),
        'w_out': nrm(ks[26], (Ly, D, D), D ** -0.5),
        'w_q': nrm(ks[27], (Ly, D, PEER_HEADS * PEER_QDIM), D ** -0.5),
        'sub_keys': nrm(ks[28], (Ly, PEER_HEADS, 2, PEER_NKEYS, PEER_HALF), PEER_HALF ** -0.5),
        'peer_u': nrm(ks[29], (Ly, PEER_EXPERTS, D), D ** -0.5),
        'peer_v': nrm(ks[30], (Ly, PEER_EXPERTS, D), 0.5),
        'final_g': 1.0 + nrm(ks[31], (D,), 0.02),
    }

def first_block(x, c, ctx, c_ctx, ada_w, ada_b, norm1_g, norm2_g, w_in, shift_mu, w0, w2, a0, a2, g2,
              k_k, k_a, r_k, lnx_g, lnx_b, w_oA, conv_w, cnorm_g, cnorm_b, w_oB, gate_b, w_out,
              w_q, sub_keys, peer_u, peer_v, final_g):
    B = x.shape[0]
    rows = x.shape[1] // GRID_W
    xc = ctx
    zero_state = jnp.zeros((B, RWKV_HEADS, RWKV_HEAD, RWKV_HEAD), jnp.float32)
    for l in range(DEPTH):
        last = l == DEPTH - 1
        p = dict(w_in=w_in[l], shift_mu=shift_mu[l], w0=w0[l], w2=w2[l], a0=a0[l], a2=a2[l],
                 g2=g2[l], k_k=k_k[l], k_a=k_a[l], r_k=r_k[l], lnx_g=lnx_g[l], lnx_b=lnx_b[l],
                 w_oA=w_oA[l], conv_w=conv_w[l], cnorm_g=cnorm_g[l], cnorm_b=cnorm_b[l],
                 w_oB=w_oB[l], gate_b=gate_b[l], w_out=w_out[l], w_q=w_q[l],
                 sub_keys=sub_keys[l], peer_u=peer_u[l], peer_v=peer_v[l])
        mod = jax.nn.silu(c) @ ada_w[l] + ada_b[l]
        sh1, sc1, gt1, sh2, sc2, gt2 = jnp.split(mod[:, None, :], 6, axis=-1)
        modc = jax.nn.silu(c_ctx) @ ada_w[l] + ada_b[l]
        csh1, csc1, cgt1, csh2, csc2, cgt2 = jnp.split(modc, 6, axis=-1)

        hc = modulate(xc, norm1_g[l], csh1, csc1)
        yc, ctx_states = token_mixer(hc, p, None, (zero_state, zero_state), emit=not last)

        h = modulate(x, norm1_g[l], sh1, sc1)
        y, _ = token_mixer(h, p, rows, ctx_states, emit=True)
        x = x + gt1 * y
        x = x + gt2 * peer(modulate(x, norm2_g[l], sh2, sc2), p)

        if not last:
            xc = xc + cgt1 * yc
            xc = xc + cgt2 * peer(modulate(xc, norm2_g[l], csh2, csc2), p)
    return rmsnorm(x, final_g)


DEPTH_2 = 1

CHUNK = 64
Q_BLOCK = 128
EPS = 1e-6
N_BRANCHES = 4
BRANCH_WIDTH = D_MODEL // 4
HEADS = 4
HEAD_DIM = BRANCH_WIDTH // HEADS
D_FF = 4 * D_MODEL

DN_DK = HEAD_DIM
DN_DV = HEAD_DIM
CONV_K_2 = 4
MLA_NOPE = HEAD_DIM
MLA_ROPE = HEAD_DIM // 2
MLA_V = HEAD_DIM
MLA_Q_LORA = D_MODEL // 4
MLA_KV_LORA = D_MODEL // 8
ROPE_THETA = 10000.0
GLA_DK = HEAD_DIM // 2
GLA_DV = HEAD_DIM
GLA_RANK = 16
GLA_TAU = 16.0
FOX_DH = HEAD_DIM

IN_SIZES = (
    HEADS * (2 * DN_DK + DN_DV), HEADS * DN_DV, HEADS, HEADS,
    MLA_Q_LORA, MLA_KV_LORA, MLA_ROPE,
    HEADS * GLA_DK, HEADS * GLA_DK, HEADS * GLA_DV, HEADS * GLA_DV, GLA_RANK,
    HEADS * FOX_DH, HEADS * FOX_DH, HEADS * FOX_DH, HEADS,
)
IN_WIDTH = sum(IN_SIZES)


def rms_norm(x, gain):
    xf = x.astype(jnp.float32)
    y = xf * lax.rsqrt(jnp.mean(xf * xf, axis=-1, keepdims=True) + EPS)
    return (y * gain.astype(jnp.float32)).astype(x.dtype)

def l2_normalize(x):
    xf = x.astype(jnp.float32)
    return (xf * lax.rsqrt(jnp.sum(xf * xf, axis=-1, keepdims=True) + EPS)).astype(x.dtype)

def causal_depthwise_conv(x, w):
    k = w.shape[0]
    return lax.conv_general_dilated(
        x, w[:, None, :].astype(x.dtype), window_strides=(1,), padding=((k - 1, 0),),
        dimension_numbers=('NWC', 'WIO', 'NWC'), feature_group_count=x.shape[-1])

def to_chunks(t):
    b, s, h, d = t.shape
    return t.reshape(b, s // CHUNK, CHUNK, h, d).transpose(0, 3, 1, 2, 4)

def from_chunks(t):
    b, h, n, c, d = t.shape
    return t.transpose(0, 2, 3, 1, 4).reshape(b, n * c, h, d)

def scalar_chunks(t):
    b, s, h = t.shape
    return t.reshape(b, s // CHUNK, CHUNK, h).transpose(0, 3, 1, 2)

def gated_delta_rule(q, k, v, g, beta):
    out_dtype = v.dtype
    f32 = jnp.float32
    b_sz, s_len, n_h, dk = q.shape
    dv = v.shape[-1]
    qc = to_chunks(q.astype(f32)) * (dk ** -0.5)
    kc = to_chunks(k.astype(f32))
    vc = to_chunks(v.astype(f32))
    gc = jnp.cumsum(scalar_chunks(g.astype(f32)), axis=-1)
    bc = scalar_chunks(beta.astype(f32))
    lower = jnp.tril(jnp.ones((CHUNK, CHUNK), dtype=bool))
    strict = jnp.tril(jnp.ones((CHUNK, CHUNK), dtype=bool), -1)
    diff = gc[..., :, None] - gc[..., None, :]
    decay_ts = jnp.where(lower, jnp.exp(jnp.where(lower, diff, 0.0)), 0.0)
    kk = jnp.einsum('bhncd,bhnsd->bhncs', kc, kc)
    a_strict = jnp.where(strict, bc[..., None] * kk * decay_ts, 0.0)
    eye = jnp.eye(CHUNK, dtype=f32)
    rhs = jnp.concatenate([vc * bc[..., None], kc * (bc * jnp.exp(gc))[..., None]], axis=-1)
    sol = lax.linalg.triangular_solve(a_strict + eye, rhs, left_side=True, lower=True,
                                      unit_diagonal=True)
    u = sol[..., :dv]
    w = sol[..., dv:]
    qk = jnp.einsum('bhncd,bhnsd->bhncs', qc, kc) * decay_ts
    q_decay = qc * jnp.exp(gc)[..., None]
    k_tail = kc * jnp.exp(gc[..., -1:] - gc)[..., None]
    chunk_decay = jnp.exp(gc[..., -1])

    def step(state, inp):
        u_c, w_c, qk_c, qd_c, kt_c, cd_c = inp
        v_new = u_c - jnp.einsum('bhck,bhkv->bhcv', w_c, state)
        o_c = (jnp.einsum('bhck,bhkv->bhcv', qd_c, state)
               + jnp.einsum('bhcs,bhsv->bhcv', qk_c, v_new))
        state = state * cd_c[..., None, None] + jnp.einsum('bhck,bhcv->bhkv', kt_c, v_new)
        return state, o_c

    xs = tuple(jnp.moveaxis(t, 2, 0) for t in (u, w, qk, q_decay, k_tail, chunk_decay))
    s0 = jnp.zeros((b_sz, n_h, dk, dv), f32)
    _, o = lax.scan(step, s0, xs)
    return from_chunks(jnp.moveaxis(o, 0, 2)).astype(out_dtype)

def gla_chunked(q, k, v, log_a):
    out_dtype = v.dtype
    f32 = jnp.float32
    b_sz, s_len, n_h, dk = q.shape
    dv = v.shape[-1]
    qc = to_chunks(q.astype(f32)) * (dk ** -0.5)
    kc = to_chunks(k.astype(f32))
    vc = to_chunks(v.astype(f32))
    bcum = jnp.cumsum(to_chunks(log_a.astype(f32)), axis=3)
    q_in = qc * jnp.exp(bcum)
    k_in = kc * jnp.exp(-bcum)
    lower = jnp.tril(jnp.ones((CHUNK, CHUNK), dtype=bool))
    attn = jnp.where(lower, jnp.einsum('bhncd,bhnsd->bhncs', q_in, k_in), 0.0)
    o_intra = jnp.einsum('bhncs,bhnsv->bhncv', attn, vc)
    b_last = bcum[..., -1:, :]
    k_tail = kc * jnp.exp(b_last - bcum)
    chunk_decay = jnp.exp(b_last[..., 0, :])

    def step(state, inp):
        qi_c, kt_c, v_c, cd_c = inp
        o_c = jnp.einsum('bhck,bhkv->bhcv', qi_c, state)
        state = state * cd_c[..., None] + jnp.einsum('bhck,bhcv->bhkv', kt_c, v_c)
        return state, o_c

    xs = tuple(jnp.moveaxis(t, 2, 0) for t in (q_in, k_tail, vc, chunk_decay))
    s0 = jnp.zeros((b_sz, n_h, dk, dv), f32)
    _, o_inter = lax.scan(step, s0, xs)
    o = o_intra + jnp.moveaxis(o_inter, 0, 2)
    return from_chunks(o).astype(out_dtype)

def rope_cos_sin(seq, dim):
    inv_freq = 1.0 / (ROPE_THETA ** (jnp.arange(0, dim, 2, dtype=jnp.float32) / dim))
    ang = jnp.arange(seq, dtype=jnp.float32)[:, None] * inv_freq[None, :]
    ang = jnp.concatenate([ang, ang], axis=-1)
    return jnp.cos(ang), jnp.sin(ang)

def apply_rope(x, cos, sin):
    xf = x.astype(jnp.float32)
    x1, x2 = jnp.split(xf, 2, axis=-1)
    rot = jnp.concatenate([-x2, x1], axis=-1)
    return (xf * cos[None, :, None, :] + rot * sin[None, :, None, :]).astype(x.dtype)

def block_sweep_attention(q, k, v, scale, forget_cum):
    s_len = q.shape[1]
    outs = []
    for start in range(0, s_len, Q_BLOCK):
        end = start + Q_BLOCK
        logits = jnp.einsum('bqhd,bkhd->bhqk', q[:, start:end], k[:, :end],
                            preferred_element_type=jnp.float32) * scale
        q_pos = jnp.arange(start, end)
        k_pos = jnp.arange(end)
        if forget_cum is None:
            allowed = (k_pos[None, :] // CHUNK) <= (q_pos[:, None] // CHUNK)
        else:
            allowed = k_pos[None, :] <= q_pos[:, None]
            f_q = forget_cum[:, start:end].transpose(0, 2, 1)
            f_k = forget_cum[:, :end].transpose(0, 2, 1)
            logits = logits + (f_q[..., :, None] - f_k[..., None, :])
        logits = jnp.where(allowed, logits, -jnp.inf)
        p = jax.nn.softmax(logits, axis=-1)
        outs.append(jnp.einsum('bhqk,bkhd->bqhd', p.astype(v.dtype), v[:, :end]))
    return jnp.concatenate(outs, axis=1)

def hybrid_layer(x, norm_mix_pre, norm_mix_post, norm_mlp_pre, norm_mlp_post, w_in,
                 dn_conv, dn_a_log, dn_dt_bias, dn_norm,
                 mla_q_norm, mla_w_q_up, mla_kv_norm, mla_w_kv_up,
                 gla_w_gate_up, gla_gate_bias, gla_norm, fox_f_bias,
                 w_branch_up, w_gate, b_gate, w_out, w_mlp_in, w_mlp_out):
    f32 = jnp.float32
    b_sz, s_len, _ = x.shape
    h = rms_norm(x, norm_mix_pre)
    proj = h @ w_in
    split_at = np.cumsum(IN_SIZES)[:-1].tolist()
    (dn_qkv, dn_z, dn_b, dn_a, mla_cq, mla_ckv, mla_kpe,
     gla_q, gla_k, gla_v, gla_g, gla_lr,
     fox_q, fox_k, fox_v, fox_f) = jnp.split(proj, split_at, axis=-1)

    qkv = jax.nn.silu(causal_depthwise_conv(dn_qkv, dn_conv))
    a_q, a_k, a_v = jnp.split(qkv, [HEADS * DN_DK, 2 * HEADS * DN_DK], axis=-1)
    a_q = l2_normalize(a_q.reshape(b_sz, s_len, HEADS, DN_DK))
    a_k = l2_normalize(a_k.reshape(b_sz, s_len, HEADS, DN_DK))
    a_v = a_v.reshape(b_sz, s_len, HEADS, DN_DV)
    beta = jax.nn.sigmoid(dn_b.astype(f32))
    g = -jnp.exp(dn_a_log.astype(f32)) * jax.nn.softplus(dn_a.astype(f32) + dn_dt_bias.astype(f32))
    o_a = gated_delta_rule(a_q, a_k, a_v, g, beta)
    o_a = (rms_norm(o_a, dn_norm) * jax.nn.silu(dn_z.reshape(b_sz, s_len, HEADS, DN_DV))
           ).reshape(b_sz, s_len, BRANCH_WIDTH)

    cq = rms_norm(mla_cq, mla_q_norm)
    b_q = (cq @ mla_w_q_up).reshape(b_sz, s_len, HEADS, MLA_NOPE + MLA_ROPE)
    q_nope, q_pe = jnp.split(b_q, [MLA_NOPE], axis=-1)
    ckv = rms_norm(mla_ckv, mla_kv_norm)
    b_kv = (ckv @ mla_w_kv_up).reshape(b_sz, s_len, HEADS, MLA_NOPE + MLA_V)
    k_nope, b_v = jnp.split(b_kv, [MLA_NOPE], axis=-1)
    cos, sin = rope_cos_sin(s_len, MLA_ROPE)
    q_pe = apply_rope(q_pe, cos, sin)
    k_pe = apply_rope(mla_kpe[:, :, None, :], cos, sin)
    b_qf = jnp.concatenate([q_nope, q_pe], axis=-1)
    b_kf = jnp.concatenate([k_nope, jnp.broadcast_to(k_pe, (b_sz, s_len, HEADS, MLA_ROPE))], axis=-1)
    o_b = block_sweep_attention(b_qf, b_kf, b_v, (MLA_NOPE + MLA_ROPE) ** -0.5, None)
    o_b = o_b.reshape(b_sz, s_len, BRANCH_WIDTH)

    log_a = jax.nn.log_sigmoid((gla_lr @ gla_w_gate_up + gla_gate_bias).astype(f32)) / GLA_TAU
    o_c = gla_chunked(gla_q.reshape(b_sz, s_len, HEADS, GLA_DK),
                      gla_k.reshape(b_sz, s_len, HEADS, GLA_DK),
                      gla_v.reshape(b_sz, s_len, HEADS, GLA_DV),
                      log_a.reshape(b_sz, s_len, HEADS, GLA_DK))
    o_c = (rms_norm(o_c, gla_norm) * jax.nn.silu(gla_g.reshape(b_sz, s_len, HEADS, GLA_DV))
           ).reshape(b_sz, s_len, BRANCH_WIDTH)

    log_f = jax.nn.log_sigmoid((fox_f + fox_f_bias).astype(f32))
    forget_cum = jnp.cumsum(log_f, axis=1)
    o_d = block_sweep_attention(fox_q.reshape(b_sz, s_len, HEADS, FOX_DH),
                                fox_k.reshape(b_sz, s_len, HEADS, FOX_DH),
                                fox_v.reshape(b_sz, s_len, HEADS, FOX_DH),
                                FOX_DH ** -0.5, forget_cum)
    o_d = o_d.reshape(b_sz, s_len, BRANCH_WIDTH)

    branches = (o_a, o_b, o_c, o_d)
    merged = jnp.zeros_like(x)
    for i in range(N_BRANCHES):
        gate = jax.nn.sigmoid(h @ w_gate[i] + b_gate[i])
        merged = merged + gate * (branches[i] @ w_branch_up[i])
    x = x + rms_norm(merged @ w_out, norm_mix_post)

    h2 = rms_norm(x, norm_mlp_pre)
    u = jax.nn.relu(h2 @ w_mlp_in)
    x = x + rms_norm((u * u) @ w_mlp_out, norm_mlp_post)
    return x

def second_inputs(seed: int = 0) -> dict:
    key = jax.random.key(seed)
    ks = jax.random.split(key, 24)
    L, D, f32 = DEPTH_2, D_MODEL, jnp.float32

    def nrm(i, shape, scale):
        return jax.random.normal(ks[i], shape, f32) * scale

    def gain(i, shape):
        return 1.0 + 0.1 * jax.random.normal(ks[i], shape, f32)

    conv_width = HEADS * (2 * DN_DK + DN_DV)
    dt = jnp.exp(jax.random.uniform(ks[7], (L, HEADS), f32, math.log(1e-3), math.log(1e-1)))
    return {
        'x': nrm(0, (BATCH, SEQ, D), 1.0),
        'norm_mix_pre': gain(1, (L, D)),
        'norm_mix_post': gain(2, (L, D)),
        'norm_mlp_pre': gain(3, (L, D)),
        'norm_mlp_post': gain(4, (L, D)),
        'w_in': nrm(5, (L, D, IN_WIDTH), D ** -0.5),
        'dn_conv': nrm(8, (L, CONV_K_2, conv_width), CONV_K_2 ** -0.5),
        'dn_a_log': jnp.log(jax.random.uniform(ks[6], (L, HEADS), f32, 1.0, 16.0)),
        'dn_dt_bias': dt + jnp.log(-jnp.expm1(-dt)),
        'dn_norm': gain(9, (L, DN_DV)),
        'mla_q_norm': gain(10, (L, MLA_Q_LORA)),
        'mla_w_q_up': nrm(11, (L, MLA_Q_LORA, HEADS * (MLA_NOPE + MLA_ROPE)), MLA_Q_LORA ** -0.5),
        'mla_kv_norm': gain(12, (L, MLA_KV_LORA)),
        'mla_w_kv_up': nrm(13, (L, MLA_KV_LORA, HEADS * (MLA_NOPE + MLA_V)), MLA_KV_LORA ** -0.5),
        'gla_w_gate_up': nrm(14, (L, GLA_RANK, HEADS * GLA_DK), GLA_RANK ** -0.5),
        'gla_gate_bias': nrm(15, (L, HEADS * GLA_DK), 0.1),
        'gla_norm': gain(16, (L, GLA_DV)),
        'fox_f_bias': jax.random.uniform(ks[17], (L, HEADS), f32, 1.0, 3.0),
        'w_branch_up': nrm(18, (L, N_BRANCHES, BRANCH_WIDTH, D), BRANCH_WIDTH ** -0.5),
        'w_gate': nrm(19, (L, N_BRANCHES, D, D), D ** -0.5),
        'b_gate': nrm(20, (L, N_BRANCHES, D), 0.1),
        'w_out': nrm(21, (L, D, D), D ** -0.5),
        'w_mlp_in': nrm(22, (L, D, D_FF), D ** -0.5),
        'w_mlp_out': nrm(23, (L, D_FF, D), D_FF ** -0.5),
    }

def second_block(x, norm_mix_pre, norm_mix_post, norm_mlp_pre, norm_mlp_post, w_in,
              dn_conv, dn_a_log, dn_dt_bias, dn_norm,
              mla_q_norm, mla_w_q_up, mla_kv_norm, mla_w_kv_up,
              gla_w_gate_up, gla_gate_bias, gla_norm, fox_f_bias,
              w_branch_up, w_gate, b_gate, w_out, w_mlp_in, w_mlp_out):
    for l in range(DEPTH_2):
        x = hybrid_layer(x, norm_mix_pre[l], norm_mix_post[l], norm_mlp_pre[l], norm_mlp_post[l],
                         w_in[l], dn_conv[l], dn_a_log[l], dn_dt_bias[l], dn_norm[l],
                         mla_q_norm[l], mla_w_q_up[l], mla_kv_norm[l], mla_w_kv_up[l],
                         gla_w_gate_up[l], gla_gate_bias[l], gla_norm[l], fox_f_bias[l],
                         w_branch_up[l], w_gate[l], b_gate[l], w_out[l], w_mlp_in[l], w_mlp_out[l])
    return x


def setup_inputs(seed=0):
    out = dict(first_inputs(seed))
    for name, value in second_inputs(seed + 1).items():
        if name != "x":
            out[name + "_2"] = value
    return out


def reference(
    x, c, ctx, c_ctx, ada_w, ada_b, norm1_g, norm2_g, w_in, shift_mu, w0, w2, a0, a2, g2, k_k,
    k_a, r_k, lnx_g, lnx_b, w_oA, conv_w, cnorm_g, cnorm_b, w_oB, gate_b, w_out, w_q, sub_keys,
    peer_u, peer_v, final_g, norm_mix_pre_2, norm_mix_post_2, norm_mlp_pre_2, norm_mlp_post_2,
    w_in_2, dn_conv_2, dn_a_log_2, dn_dt_bias_2, dn_norm_2, mla_q_norm_2, mla_w_q_up_2,
    mla_kv_norm_2, mla_w_kv_up_2, gla_w_gate_up_2, gla_gate_bias_2, gla_norm_2, fox_f_bias_2,
    w_branch_up_2, w_gate_2, b_gate_2, w_out_2, w_mlp_in_2, w_mlp_out_2,
):
    x = first_block(
        x, c, ctx, c_ctx, ada_w, ada_b, norm1_g, norm2_g, w_in, shift_mu, w0, w2, a0, a2, g2,
        k_k, k_a, r_k, lnx_g, lnx_b, w_oA, conv_w, cnorm_g, cnorm_b, w_oB, gate_b, w_out, w_q,
        sub_keys, peer_u, peer_v, final_g,
    )
    return second_block(
        x, norm_mix_pre_2, norm_mix_post_2, norm_mlp_pre_2, norm_mlp_post_2, w_in_2, dn_conv_2,
        dn_a_log_2, dn_dt_bias_2, dn_norm_2, mla_q_norm_2, mla_w_q_up_2, mla_kv_norm_2,
        mla_w_kv_up_2, gla_w_gate_up_2, gla_gate_bias_2, gla_norm_2, fox_f_bias_2,
        w_branch_up_2, w_gate_2, b_gate_2, w_out_2, w_mlp_in_2, w_mlp_out_2,
    )


_drawn_inputs = setup_inputs


def setup_inputs(seed=0):
    import zlib

    import numpy as np

    out = dict(_drawn_inputs(seed))
    spreads = {}
    factors = {'norm1_g': 3.16,
     'w2': 2.853,
     'lnx_g': 4.673,
     'lnx_b': 5.304,
     'cnorm_g': 4.267,
     'cnorm_b': 4.485,
     'gate_b': 6.142,
     'mla_q_norm_2': 4.373,
     'mla_kv_norm_2': 2.946,
     'gla_gate_bias_2': 10.265,
     'dn_norm_2': 3.524,
     'gla_w_gate_up_2': 2.725,
     'gla_norm_2': 3.364}
    for name, (base, spread) in spreads.items():
        noise = np.random.default_rng([zlib.crc32(name.encode()), seed]).standard_normal(out[name].shape)
        drawn = base * np.exp(spread * noise) if base else spread * noise
        out[name] = jnp.asarray(drawn.astype(out[name].dtype))
    for name, factor in factors.items():
        out[name] = (out[name] * factor).astype(out[name].dtype)
    return out
```

```python
import math
from contextlib import ExitStack, contextmanager

import numpy as np

import concourse.bass as bass
from concourse import mybir

F32 = mybir.dt.float32
U32 = mybir.dt.uint32
ACT = mybir.ActivationFunctionType
ALU = mybir.AluOpType
AXX = mybir.AxisListType.X
P = 128


def names(**values):
    return type("Names", (), values)()


class Signal:

    def __init__(self, sem):
        self.sem, self.count, self.mark = sem, 0, 0

    def up(self, by=1):
        self.count += by
        return self.sem

    def at(self, n):
        return self.mark + n


class Core:

    def __init__(self, nc, ctx):
        self.nc, self.ctx = nc, ctx
        self.signals, self.made = [], 0
        self.psum = ctx.enter_context(nc.psum_tensor("psum", [P, 4096], F32))
        self.weights = [self.counter(f"weights_loaded{i}") for i in range(2)]
        self.multiplied = self.counter("multiplied")
        self.evacuated = self.counter("evacuated")
        self.vec_step = self.counter("vec_step")
        self.act_step = self.counter("act_step")
        self.pool_step = self.counter("pool_step")
        self.staged = self.counter("numbers_staged")
        self.weights_staged = self.counter("weights_staged")
        self.slot_free = self.counter("slot_free")
        self.row_used = self.counter("row_used")
        self.dots_kept = self.counter("dots_kept")
        self.weighted = self.counter("weighted")
        self.gathered = [self.counter(f"row_gathered{j}") for j in range(8)]
        self.loaded = self.counter("loaded")
        self.stored = self.counter("stored")

    def sbuf(self, name, shape, dtype=F32):
        self.made += 1
        return self.nc.sbuf_tensor(f"{name}_{self.made}", [P, *shape], dtype)

    def counter(self, name):
        s = Signal(self.ctx.enter_context(self.nc.semaphore(name)))
        self.signals.append(s)
        return s

    @contextmanager
    def stage(self):
        for s in self.signals:
            s.mark = s.count
        with self.nc.Block(no_gpsimd_drain=True) as block:
            yield block

    def bank(self, i, n=512):
        return self.psum[:, 512 * i:512 * i + n]


def bc(ap, *shape):
    return ap.broadcast_to([P, *shape])


def gemm(k, w, blocks, kt, cols, rhs, dst, tokens):
    nc = k.nc
    sub = cols // P
    with k.sbuf("weight_ring", [2, kt * cols]) as ring, k.stage() as block:
        pairs = blocks // 2
        wl, mu, ev = k.weights, k.multiplied, k.evacuated

        def half(n_slot, width=sub * tokens):
            return k.psum[:, n_slot * 1024:n_slot * 1024 + width]

        @block.sync
        def _(sp):
            for n in range(min(2, blocks)):
                sp.dma_start(ring[:, n, :], w[n]).then_inc(wl[n].sem, 16)

            def load(n, slot):
                sp.wait_ge(mu.sem, mu.at(n - 1))
                sp.dma_start(ring[:, slot, :], w[n]).then_inc(wl[slot].sem, 16)

            if pairs > 1:
                with sp.Fori(1, pairs) as i:
                    for slot in range(2):
                        load(i * 2 + slot, slot)
            if blocks % 2 and blocks > 1:
                load(blocks - 1, 0)

        @block.tensor
        def _(pe):
            def multiply(i, slot, first):
                pe.wait_ge(wl[slot].sem, wl[slot].at(16) + i * 16)
                if not first:
                    pe.wait_ge(ev.sem, ev.at(slot - 1) + i * 2)
                for s in range(sub):
                    for j in range(kt):
                        at = j * cols + s * P
                        mm = pe.matmul(half(slot)[:, s * tokens:(s + 1) * tokens], ring[:, slot, at:at + P], rhs(j),
                                       start=(j == 0), stop=(j == kt - 1))
                mm.then_inc(mu.sem, 1)

            for slot in range(min(2, blocks)):
                multiply(0, slot, True)
            if pairs > 1:
                with pe.Fori(1, pairs) as i:
                    for slot in range(2):
                        multiply(i, slot, False)
            if blocks % 2 and blocks > 1:
                multiply(pairs, 0, False)

        @block.scalar
        def _(act):
            def copy_out(n, slot):
                act.wait_ge(mu.sem, mu.at(1) + n)
                act.activation(dst[:, bass.ds(n * sub, sub), :],
                               half(slot).rearrange("p (s t) -> p s t", s=sub), ACT.Copy).then_inc(ev.sem, 1)

            if pairs:
                with act.Fori(0, pairs) as i:
                    for slot in range(2):
                        copy_out(i * 2 + slot, slot)
            if blocks % 2:
                copy_out(blocks - 1, 0)

        for n in range(blocks):
            wl[n % 2].up(16)
            mu.up()
            ev.up()


def chained(k, dve):
    step = k.vec_step

    def chain(instruction):
        instruction.then_inc(step.up(), 1)
        dve.wait_ge(step.sem, step.count)

    return chain


def over_tokens(column, tiles, tokens):
    return column.unsqueeze(2).broadcast_to([P, tiles, tokens])


def over_tiles(row, tiles, tokens):
    return row.unsqueeze(1).broadcast_to([P, tiles, tokens])


def load(k, *pairs):
    with k.stage() as block:

        @block.sync
        def _(sp):
            for dst, src in pairs:
                sp.dma_start(dst, src).then_inc(k.loaded.up(16), 16)
            sp.wait_ge(k.loaded.sem, k.loaded.count)


def channel_norm(k, src, dst, tiles, width, eps, mul=None, add=None, center=False, tokens=256):
    nc = k.nc
    with (
        k.sbuf("squares", [tiles, tokens]) as squares,
        k.sbuf("row", [tokens]) as row,
        k.stage() as block,
    ):
        total, mean = k.bank(0, tokens), k.bank(1, tokens)
        marks = {}

        @block.vector
        def _(dve):
            chain = chained(k, dve)
            base = src
            if center:
                dve.wait_ge(k.multiplied.sem, k.multiplied.at(1))
                chain(dve.tensor_scalar(row[:], mean, 1.0 / width, None, ALU.mult))
                chain(dve.tensor_tensor(dst, src, over_tiles(row[:], tiles, tokens), ALU.subtract))
                base = dst
            marks["centered"] = k.vec_step.count
            n = 2 if center else 1
            dve.wait_ge(k.multiplied.sem, k.multiplied.at(n))
            chain(dve.tensor_scalar(row[:], total, 1.0 / width, eps, ALU.mult, ALU.add))
            marks["variance"] = k.vec_step.count
            dve.wait_ge(k.act_step.sem, k.act_step.at(2))
            chain(dve.reciprocal(row[:], row[:]))
            chain(dve.tensor_tensor(dst, base, over_tiles(row[:], tiles, tokens), ALU.mult))
            if mul is not None:
                chain(dve.tensor_tensor(dst, dst, over_tokens(mul, tiles, tokens), ALU.mult))
            if add is not None:
                chain(dve.tensor_tensor(dst, dst, over_tokens(add, tiles, tokens), ALU.add))

        @block.scalar
        def _(act):
            if center:
                act.wait_ge(k.vec_step.sem, marks["centered"])
            act.activation(squares[:], dst if center else src, ACT.Square).then_inc(k.act_step.up(), 1)
            act.wait_ge(k.vec_step.sem, marks["variance"])
            act.activation(row[:], row[:], ACT.Sqrt).then_inc(k.act_step.up(), 1)

        @block.tensor
        def _(pe):
            if center:
                for j in range(tiles):
                    mm = pe.matmul(mean, k.ones, src[:, j, :], start=(j == 0), stop=(j == tiles - 1))
                mm.then_inc(k.multiplied.up(), 1)
            pe.wait_ge(k.act_step.sem, k.act_step.at(1))
            for j in range(tiles):
                mm = pe.matmul(total, k.ones, squares[:, j, :], start=(j == 0), stop=(j == tiles - 1))
            mm.then_inc(k.multiplied.up(), 1)


def invert_unit_lower(k, groups, Ld, LdT, NT, temps, TT):
    E1, E2, E3, X = temps
    ident = k.ident

    def grp(t, g):
        return t[:, g]

    steps = [
        (LdT, Ld, None, E1),
        (Ld, LdT, None, E2),
        (E1, E2, None, E3),
        (E2, X, X, X),
        (E3, X, X, X),
        (X, None, None, TT),
        (NT, X, None, E1),
        (X, NT, None, E2),
        (E2, E1, None, E3),
        (E1, E2, None, Ld),
        (Ld, E3, None, LdT),
        (E1, TT, TT, TT),
        (E3, TT, TT, TT),
        (LdT, TT, TT, TT),
    ]
    with k.stage() as block:

        @block.vector
        def _(dve):
            for g in range(groups):
                dve.tensor_tensor(grp(X, g), grp(Ld, g), k.ident.unsqueeze(1).broadcast_to([P, 4, P]),
                                  ALU.add).then_inc(k.vec_step.up(), 1)
            for q, (_, _, _, out) in enumerate(steps):
                dve.wait_ge(k.multiplied.sem, k.multiplied.at(groups * q + 1))
                dve.tensor_copy(grp(out, 0), k.bank((groups * q) % 4).rearrange("p (h c) -> p h c", h=4)
                                ).then_inc(k.vec_step.up(), 1)

        @block.scalar
        def _(act):
            if groups > 1:
                for q, (_, _, _, out) in enumerate(steps):
                    act.wait_ge(k.multiplied.sem, k.multiplied.at(2 * q + 2))
                    act.activation(grp(out, 1), k.bank((2 * q + 1) % 4).rearrange("p (h c) -> p h c", h=4), ACT.Copy
                                   ).then_inc(k.act_step.up(), 1)

        @block.tensor
        def _(pe):
            for q, (left, right, added, _) in enumerate(steps):
                for g in range(groups):
                    if g == 0:
                        pe.wait_ge(k.vec_step.sem, k.vec_step.at(groups + q))
                    else:
                        if q == 0:
                            pe.wait_ge(k.vec_step.sem, k.vec_step.at(groups))
                        else:
                            pe.wait_ge(k.act_step.sem, k.act_step.at(q))
                    bank = k.bank((groups * q + g) % 4)
                    for h in range(4):
                        out = bank[:, h * P:(h + 1) * P]
                        if right is None:
                            mm = pe.transpose(out, grp(left, g)[:, h, :], ident)
                        else:
                            mm = pe.matmul(out, grp(left, g)[:, h, :], grp(right, g)[:, h, :], start=True,
                                           stop=added is None)
                            if added is not None:
                                mm = pe.matmul(out, ident, grp(added, g)[:, h, :], start=False, stop=True)
                    mm.then_inc(k.multiplied.up(), 1)


def rwkv_unit(k, b, L, half, d, tile, first, emit):
    nc = k.nc
    z, S = b.z, b.states[d]
    toks = slice(tile * P, (tile + 1) * P)
    kts = slice(4 * half, 4 * half + 4)
    lo, hi = 64 * d, 64 * d + 64
    C = math.exp(-0.5)
    strict, incl, near, far, back = ((k.up, k.up_incl, k.up8, k.up_far, k.lo8) if d == 0 else
                                     (k.lo, k.lo_incl, k.lo8, k.lo_far, k.up8))

    def r3(bank):
        return bank.rearrange("p (j t) -> p j t", j=4)

    def masked(m, n):
        return m.unsqueeze(1).broadcast_to([P, n, P])

    r, kz, vz = z[:, kts, toks], z[:, slice(8 + 4 * half, 12 + 4 * half), toks], z[:, slice(16 + 4 * half, 20 + 4 * half), toks]
    kk = b.kk[:, kts, toks]
    marks = {}
    with k.stage() as block:

        @block.vector
        def _(dve):
            chain = chained(k, dve)
            dve.wait_ge(k.act_step.sem, k.act_step.at(1))
            chain(dve.tensor_tensor_scan(b.cum.rearrange("p j t -> p (j t)"), k.segments, b.sg.rearrange("p j t -> p (j t)"),
                                         0.0, ALU.mult, ALU.add))
            chain(dve.tensor_copy(b.tot[:], b.cum[:, :, 63::64]))
            if d == 0:
                chain(dve.tensor_tensor(b.excl, b.cum, b.sg, ALU.subtract))
                cum_incl = b.cum
            else:
                for c in range(2):
                    s = slice(64 * c, 64 * c + 64)
                    chain(dve.tensor_tensor(b.excl[:, :, s], b.tot[:, :, c:c + 1].broadcast_to([P, 4, 64]), b.cum[:, :, s],
                                            ALU.subtract))
                chain(dve.tensor_tensor(b.cum, b.excl, b.sg, ALU.add))
                cum_incl = b.cum
            marks["sums"] = k.vec_step.count
            ka = L.k_a[:, kts].unsqueeze(2).broadcast_to([P, 4, P])
            chain(dve.scalar_tensor_tensor(b.kd, b.a, 1.0, ka, ALU.subtract, ALU.mult))
            chain(dve.scalar_tensor_tensor(b.kd, b.kd, 1.0, kz, ALU.add, ALU.mult))
            chain(dve.scalar_tensor_tensor(b.a, b.a, -1.0, kk, ALU.mult, ALU.mult))
            if emit:
                ks = b.kdsum[:, kts, toks]
                if d == 0:
                    chain(dve.tensor_copy(ks, b.kd))
                else:
                    chain(dve.tensor_tensor(ks, ks, b.kd, ALU.add))
            dve.wait_ge(k.act_step.sem, k.act_step.at(3))
            chain(dve.tensor_tensor(b.kh[:], b.kd, b.eN, ALU.mult))
            marks["kh"] = k.vec_step.count
            chain(dve.tensor_tensor(b.nb[:], b.a, b.eN, ALU.mult))
            marks["nb"] = k.vec_step.count
            chain(dve.tensor_tensor(b.kt[:], kk, b.eX, ALU.mult))
            for hh in range(2):
                chain(dve.tensor_scalar(b.rhs4[:, :, hh, :], b.kt[:], k.half_mask[hh], None, ALU.mult))
            if emit:
                chain(dve.tensor_tensor(b.rt[:], r, b.eP, ALU.mult))
                for hh in range(2):
                    chain(dve.tensor_scalar(b.rhs4[:, :, 2 + hh, :], b.rt[:], k.half_mask[hh], None, ALU.mult))
            dve.wait_ge(k.act_step.sem, k.act_step.at(2))
            for c in range(2):
                chain(dve.tensor_scalar(b.Vc[:, c, :], b.V[:], k.half_mask[c], None, ALU.mult))

        @block.scalar
        def _(act):
            act.wait_ge(k.multiplied.sem, k.multiplied.at(1))
            for j in range(4):
                act.activation(b.sg[:, j, :], k.bank(0)[:, j * P:(j + 1) * P], ACT.Sigmoid,
                               bias=L.w0[:, 8 * d + 4 * half + j:8 * d + 4 * half + j + 1])
                last = act.activation(b.a[:, j, :], k.bank(1)[:, j * P:(j + 1) * P], ACT.Sigmoid,
                                      bias=L.a0[:, 8 * d + 4 * half + j:8 * d + 4 * half + j + 1])
            last.then_inc(k.act_step.up(), 1)
            act.wait_ge(k.multiplied.sem, k.multiplied.at(2))
            act.activation(b.V[:], k.bank(2), ACT.Copy).then_inc(k.act_step.up(), 1)
            act.wait_ge(k.vec_step.sem, marks["sums"])
            if emit:
                act.activation(b.eP, b.cum, ACT.Exp, scale=-C)
            act.activation(b.eN, b.cum, ACT.Exp, scale=C)
            act.activation(b.eX, b.excl, ACT.Exp, scale=-C)
            act.activation(b.pc[:], b.tot[:], ACT.Exp, scale=-C).then_inc(k.act_step.up(), 1)
            act.wait_ge(k.multiplied.sem, k.multiplied.at(3))
            act.activation(b.khT[:], k.bank(3), ACT.Copy).then_inc(k.act_step.up(), 1)
            act.wait_ge(k.multiplied.sem, k.multiplied.at(4))
            act.activation(b.nbT[:], k.bank(4), ACT.Copy).then_inc(k.act_step.up(), 1)

        @block.tensor
        def _(pe):
            for j in range(4):
                c = slice((4 * half + j) * P, (4 * half + j + 1) * P)
                pe.matmul(k.bank(0)[:, j * P:(j + 1) * P], L.w2[lo:hi, c], z[lo:hi, 24, toks], start=True, stop=True)
                mm = pe.matmul(k.bank(1)[:, j * P:(j + 1) * P], L.a2[lo:hi, c], z[lo:hi, 25, toks], start=True, stop=True)
            mm.then_inc(k.multiplied.up(), 1)
            for j in range(4):
                mm = pe.transpose(k.bank(2)[:, j * P:(j + 1) * P], vz[:, j, :], k.ident)
            mm.then_inc(k.multiplied.up(), 1)
            pe.wait_ge(k.vec_step.sem, marks["kh"])
            for j in range(4):
                mm = pe.transpose(k.bank(3)[:, j * P:(j + 1) * P], b.kh[:, j, :], k.ident)
            mm.then_inc(k.multiplied.up(), 1)
            pe.wait_ge(k.vec_step.sem, marks["nb"])
            for j in range(4):
                mm = pe.transpose(k.bank(4)[:, j * P:(j + 1) * P], b.nb[:, j, :], k.ident)
            mm.then_inc(k.multiplied.up(), 1)

    width = 512 if emit else 256
    with k.stage() as block:

        @block.tensor
        def _(pe):
            for j in range(4):
                three = [k.bank(3 * (j % 2) + i) for i in range(3)]
                if j >= 2:
                    pe.wait_ge(k.vec_step.sem, k.vec_step.at(j - 1))
                rhs = b.rhs4[:, j].rearrange("p a t -> p (a t)")[:, 0:width]
                pe.matmul(three[0][:, 0:width], b.kh[:, j, :], rhs, start=True, stop=True)
                pe.matmul(three[1][:, 0:width], b.nb[:, j, :], rhs, start=True, stop=True)
                for hh in range(2):
                    mm = pe.matmul(three[2][:, hh * P:(hh + 1) * P], b.rhs4[:, j, hh, :], b.nb[:, j, :], start=True, stop=True)
                mm.then_inc(k.multiplied.up(), 1)

        @block.vector
        def _(dve):
            for j in range(4):
                dve.wait_ge(k.multiplied.sem, k.multiplied.at(j + 1))
                g, h0 = j // 2, 2 * (j % 2)
                three = [k.bank(3 * (j % 2) + i).rearrange("p (h t) -> p h t", h=4) for i in range(3)]
                hs = slice(h0, h0 + 2)
                dve.tensor_tensor(b.MT[:, g, hs, :], three[0][:, 0:2, :], masked(strict, 2), ALU.mult)
                dve.tensor_tensor(b.LdT[:, g, hs, :], three[1][:, 0:2, :], masked(near, 2), ALU.mult)
                dve.tensor_tensor(b.NT[:, g, hs, :], three[1][:, 0:2, :], masked(far, 2), ALU.mult)
                if emit:
                    dve.tensor_tensor(b.ArT[:, g, hs, :], three[0][:, 2:4, :], masked(incl, 2), ALU.mult)
                    dve.tensor_tensor(b.AbT[:, g, hs, :], three[1][:, 2:4, :], masked(incl, 2), ALU.mult)
                dve.tensor_tensor(b.Ld[:, g, hs, :], three[2][:, 0:2, :], masked(back, 2), ALU.mult).then_inc(k.vec_step.up(), 1)

    invert_unit_lower(k, 2, b.Ld, b.LdT, b.NT, (b.E1, b.E2, b.E3, b.X), b.TT)

    def head(t, h):
        return t[:, h // 4, h % 4, :]

    St = S[:, kts, :]
    bR, bU, bS, bY = (k.bank(i) for i in range(4))
    with k.stage() as block:
        order = (0, 1) if d == 0 else (1, 0)

        @block.vector
        def _(dve):
            chain = chained(k, dve)
            for n, c in enumerate(order):
                m = 3 * n
                dve.wait_ge(k.multiplied.sem, k.multiplied.at(m + 1))
                chain(dve.tensor_copy(b.R[:], bR))
                marks["R", n] = k.vec_step.count
                if emit:
                    y = b.Y[:, tile, 512 * half:512 * half + 512]
                    if first and n == 0:
                        chain(dve.tensor_scalar(y, bY, k.half_mask[c], None, ALU.mult))
                    else:
                        chain(dve.scalar_tensor_tensor(y, bY, k.half_mask[c], y, ALU.mult, ALU.add))
                dve.wait_ge(k.multiplied.sem, k.multiplied.at(m + 2))
                chain(dve.tensor_scalar(b.U[:, n, :], bU, k.half_mask[c], None, ALU.mult))
                marks["U", n] = k.vec_step.count
                dve.wait_ge(k.multiplied.sem, k.multiplied.at(m + 3))
                chain(dve.tensor_tensor(St, St, r3(bS), ALU.add))
                chain(dve.tensor_tensor(St, St, masked(k.blocks64, 4), ALU.mult))
                chain(dve.tensor_tensor(St, St, b.pc[:, :, c:c + 1].broadcast_to([P, 4, P]), ALU.mult))
                marks["S", n] = k.vec_step.count
            if emit:
                chain(dve.tensor_tensor(b.U[:, 0, :], b.U[:, 0, :], b.U[:, 1, :], ALU.add))
                marks["Usum"] = k.vec_step.count
                dve.wait_ge(k.multiplied.sem, k.multiplied.at(7))
                chain(dve.tensor_tensor(y, y, bY, ALU.add))

        @block.tensor
        def _(pe):
            for n, c in enumerate(order):
                if n:
                    pe.wait_ge(k.vec_step.sem, marks["S", n - 1])
                for j in range(4):
                    js = slice(j * P, (j + 1) * P)
                    if emit:
                        pe.matmul(bY[:, js], b.rt[:, j, :], St[:, j, :], start=True, stop=True)
                    pe.matmul(bR[:, js], b.kt[:, j, :], St[:, j, :], start=True, stop=False, skip_group_check=True)
                    for hh in range(2):
                        h = 2 * j + hh
                        mm = pe.matmul(bR[:, 64 * h:64 * h + 64], head(b.MT, h), b.V[:, 64 * h:64 * h + 64], start=False,
                                       stop=True, skip_group_check=True)
                mm.then_inc(k.multiplied.up(), 1)
                pe.wait_ge(k.vec_step.sem, marks["R", n])
                for h in range(8):
                    hs = slice(64 * h, 64 * h + 64)
                    mm = pe.matmul(bU[:, hs], head(b.TT, h), b.R[:, hs], start=True, stop=True)
                mm.then_inc(k.multiplied.up(), 1)
                pe.wait_ge(k.vec_step.sem, marks["U", n])
                for j in range(4):
                    js = slice(j * P, (j + 1) * P)
                    pe.matmul(bS[:, js], b.khT[:, js], b.Vc[:, c, js], start=True, stop=False)
                    mm = pe.matmul(bS[:, js], b.nbT[:, js], b.U[:, n, js], start=False, stop=True)
                mm.then_inc(k.multiplied.up(), 1)
            if emit:
                pe.wait_ge(k.vec_step.sem, marks["Usum"])
                for h in range(8):
                    hs = slice(64 * h, 64 * h + 64)
                    pe.matmul(bY[:, hs], head(b.ArT, h), b.V[:, hs], start=True, stop=False)
                    mm = pe.matmul(bY[:, hs], head(b.AbT, h), b.U[:, 0, hs], start=False, stop=True)
                mm.then_inc(k.multiplied.up(), 1)


def buffers(k, mem, **shapes):
    return names(**{name: mem.enter_context(k.sbuf(name, shape)) for name, shape in shapes.items()})


def rwkv(k, L, z, states, emit, o):
    nc = k.nc
    with ExitStack() as mem:
        b = buffers(k, mem, kk=[8, 256])
        t0 = 0 if emit else 8
        with buffers_scope(k, before=[14, 256], after=[14, 256]) as s, k.stage() as block:

            @block.vector
            def _(dve):
                chain = chained(k, dve)
                for a in range(t0, 28, 14 if emit else 10):
                    n = 14 if emit else 10
                    zz = z[:, a:a + n, :]
                    bef, aft = s.before[:, 0:n, :], s.after[:, 0:n, :]
                    chain(dve.tensor_tensor(bef[:, :, 1:256], zz[:, :, 0:255], zz[:, :, 1:256], ALU.subtract))
                    chain(dve.tensor_scalar(bef[:, :, 0:1], zz[:, :, 0:1], -1.0, None, ALU.mult))
                    chain(dve.tensor_tensor(aft[:, :, 0:255], zz[:, :, 1:256], zz[:, :, 0:255], ALU.subtract))
                    chain(dve.tensor_scalar(aft[:, :, 255:256], zz[:, :, 255:256], -1.0, None, ALU.mult))
                    chain(dve.tensor_tensor(bef, bef, over_tokens(L.mu[:, 0, a:a + n], n, 256), ALU.mult))
                    chain(dve.tensor_tensor(aft, aft, over_tokens(L.mu[:, 1, a:a + n], n, 256), ALU.mult))
                    chain(dve.tensor_tensor(zz, zz, bef, ALU.add))
                    chain(dve.tensor_tensor(zz, zz, aft, ALU.add))

        kz = z[:, 8:16, :]
        with buffers_scope(k, squares=[8, 256], norm=[8, 256]) as s, k.stage() as block:

            @block.vector
            def _(dve):
                chain = chained(k, dve)
                chain(dve.tensor_tensor(b.kk[:], kz, over_tokens(L.k_k, 8, 256), ALU.mult))
                dve.wait_ge(k.act_step.sem, k.act_step.at(3 if emit else 2))
                chain(dve.tensor_scalar(s.norm[:], s.norm[:], 1e-12, None, ALU.max))
                chain(dve.reciprocal(s.norm[:], s.norm[:]))
                chain(dve.tensor_tensor(b.kk[:], b.kk[:], s.norm[:], ALU.mult))

            @block.scalar
            def _(act):
                act.wait_ge(k.vec_step.sem, k.vec_step.at(1))
                act.activation(s.squares[:], b.kk[:], ACT.Square).then_inc(k.act_step.up(), 1)
                act.activation(z[:, 24, :], z[:, 24, :], ACT.Tanh)
                if emit:
                    act.activation(z[:, 26:28, :], z[:, 26:28, :], ACT.Sigmoid).then_inc(k.act_step.up(), 1)
                act.wait_ge(k.multiplied.sem, k.multiplied.at(1))
                act.activation(s.norm[:], k.psum[:, 0:2048].rearrange("p (j t) -> p j t", j=8), ACT.Sqrt).then_inc(k.act_step.up(), 1)

            @block.tensor
            def _(pe):
                pe.wait_ge(k.act_step.sem, k.act_step.at(1))
                for j in range(8):
                    mm = pe.matmul(k.psum[:, 256 * j:256 * j + 256], k.blocks64, s.squares[:, j, :], start=True, stop=True)
                mm.then_inc(k.multiplied.up(), 1)

        if emit:
            o_sum = buffers(k, mem, Y=[2, 1024], kdsum=[8, 256])
            b.Y, b.kdsum = o_sum.Y, o_sum.kdsum
        with ExitStack() as inner:
            u = buffers(k, inner, tot=[4, 2], pc=[4, 2], kh=[4, P], nb=[4, P], kt=[4, P], rt=[4, P], rhs4=[4, 4, P], V=[512], Vc=[2, 512],
                        khT=[512], nbT=[512], MT=[2, 4, P], LdT=[2, 4, P], NT=[2, 4, P], ArT=[2, 4, P], AbT=[2, 4, P],
                        Ld=[2, 4, P], E1=[2, 4, P], E2=[2, 4, P], E3=[2, 4, P], X=[2, 4, P], TT=[2, 4, P], R=[512], U=[2, 512])
            u.z, u.states, u.kk = z, states, b.kk
            if emit:
                u.Y, u.kdsum = b.Y, b.kdsum
            u.sg, u.a, u.cum, u.excl, u.eP, u.eN, u.eX, u.kd = (t[:, n] for t in (u.E1, u.E2, u.E3, u.X) for n in range(2))
            for half in range(2):
                for d in range(2):
                    for tile in ((0, 1) if d == 0 else (1, 0)):
                        rwkv_unit(k, u, L, half, d, tile, d == 0, emit)
        if not emit:
            return
        heads, marks = 32, []
        with buffers_scope(k, squares=[heads, 64], row=[heads]) as s, k.stage() as block:

            @block.vector
            def _(dve):
                chain = chained(k, dve)
                y = b.Y[:].rearrange("p i (h v) -> p (i h) v", v=64)
                row = s.row[:].unsqueeze(2).broadcast_to([P, heads, 64])
                chain(dve.tensor_reduce(s.row[:], y, AXX, ALU.add))
                chain(dve.tensor_scalar(s.row[:], s.row[:], 1.0 / 64, None, ALU.mult))
                chain(dve.tensor_tensor(y, y, row, ALU.subtract))
                chain(dve.tensor_tensor(s.squares[:], y, y, ALU.mult))
                chain(dve.tensor_reduce(s.row[:], s.squares[:], AXX, ALU.add))
                chain(dve.tensor_scalar(s.row[:], s.row[:], 1.0 / 64, 64e-5, ALU.mult, ALU.add))
                variance = k.vec_step.count
                dve.wait_ge(k.act_step.sem, k.act_step.at(1))
                chain(dve.reciprocal(s.row[:], s.row[:]))
                chain(dve.tensor_tensor(y, y, row, ALU.mult))
                marks.append(variance)

            @block.scalar
            def _(act):
                act.wait_ge(k.vec_step.sem, marks[0])
                act.activation(s.row[:], s.row[:], ACT.Sqrt).then_inc(k.act_step.up(), 1)

        with k.stage() as block:

            @block.tensor
            def _(pe):
                for j in range(8):
                    for i in range(2):
                        mm = pe.transpose(k.psum[:, 256 * j + P * i:256 * j + P * i + P], b.Y[:, i, P * j:P * j + P], k.ident)
                mm.then_inc(k.multiplied.up(), 1)
                pe.wait_ge(k.vec_step.sem, k.vec_step.at(2))
                for j in range(8):
                    mm = pe.matmul(k.psum[:, 2048 + 256 * j:2304 + 256 * j], k.blocks64, b.kdsum[:, j, :], start=True, stop=True)
                mm.then_inc(k.multiplied.up(), 1)
                pe.wait_ge(k.vec_step.sem, k.vec_step.at(3))
                for j in range(8):
                    out = k.psum[:, 256 * j:256 * j + 256]
                    pe.matmul(out, L.g2[:, 0, P * j:P * j + P], z[:, 26, :], start=True, stop=False)
                    mm = pe.matmul(out, L.g2[0:32, 1, P * j:P * j + P], z[0:32, 27, :], start=False, stop=True)
                mm.then_inc(k.multiplied.up(), 1)

            @block.vector
            def _(dve):
                chain = chained(k, dve)
                lower = k.psum[:, 0:2048].rearrange("p (j t) -> p j t", j=8)
                upper = k.psum[:, 2048:4096].rearrange("p (j t) -> p j t", j=8)
                chain(dve.tensor_tensor(b.kdsum[:], b.kdsum[:], z[:, 0:8, :], ALU.mult))
                chain(dve.tensor_tensor(b.kdsum[:], b.kdsum[:], over_tokens(L.r_k, 8, 256), ALU.mult))
                dve.wait_ge(k.multiplied.sem, k.multiplied.at(1))
                chain(dve.tensor_tensor(o, lower, over_tokens(L.lnx_g, 8, 256), ALU.mult))
                chain(dve.tensor_tensor(o, o, over_tokens(L.lnx_b, 8, 256), ALU.add))
                dve.wait_ge(k.multiplied.sem, k.multiplied.at(2))
                chain(dve.tensor_tensor(b.kk[:], upper, z[:, 16:24, :], ALU.mult))
                chain(dve.tensor_tensor(o, o, b.kk[:], ALU.add))
                dve.wait_ge(k.multiplied.sem, k.multiplied.at(3))
                chain(dve.tensor_tensor(o, o, lower, ALU.mult))


@contextmanager
def buffers_scope(k, **shapes):
    with ExitStack() as mem:
        yield buffers(k, mem, **shapes)


def conv_branch(k, L, zc, out, taps):
    reach = max(abs(s) for _, s in taps)
    with buffers_scope(k, u=[8, 256 + 2 * reach], conv=[8, 256]) as s:
        with k.stage() as block:

            @block.scalar
            def _(act):
                act.activation(zc[:, 8:16, :], zc[:, 8:16, :], ACT.Sigmoid).then_inc(k.act_step.up(), 1)

            @block.gpsimd
            def _(pool):
                pool.memset(s.u[:, :, 0:reach], 0.0).then_inc(k.pool_step.up(), 1)
                pool.memset(s.u[:, :, 256 + reach:256 + 2 * reach], 0.0).then_inc(k.pool_step.up(), 1)

            @block.vector
            def _(dve):
                dve.wait_ge(k.act_step.sem, k.act_step.at(1))
                dve.tensor_tensor(s.u[:, :, reach:reach + 256], zc[:, 0:8, :], zc[:, 8:16, :], ALU.mult).then_inc(k.vec_step.up(), 1)
                dve.wait_ge(k.vec_step.sem, k.vec_step.at(1))
                dve.wait_ge(k.pool_step.sem, k.pool_step.at(2))
                for n, (row, shift) in enumerate(taps):
                    for j in range(8):
                        src = s.u[:, j, reach + shift:reach + shift + 256]
                        w = L.conv_w[:, 8 * row + j:8 * row + j + 1]
                        if n:
                            dve.wait_ge(k.vec_step.sem, k.vec_step.count - 7)
                            ins = dve.scalar_tensor_tensor(s.conv[:, j, :], src, w, s.conv[:, j, :], ALU.mult, ALU.add)
                        else:
                            ins = dve.tensor_scalar(s.conv[:, j, :], src, w, None, ALU.mult)
                        ins.then_inc(k.vec_step.up(), 1)

        channel_norm(k, s.conv[:], out, 8, 1024, 1e-5, L.cnorm_g, L.cnorm_b, center=True)
        with k.stage() as block:

            @block.scalar
            def _(act):
                act.activation(s.conv[:], out, ACT.Sigmoid).then_inc(k.act_step.up(), 1)

            @block.vector
            def _(dve):
                dve.wait_ge(k.act_step.sem, k.act_step.at(1))
                dve.tensor_tensor(out, out, s.conv[:], ALU.mult).then_inc(k.vec_step.up(), 1)


def token_mixer(k, L, l, dram, x, mod, states, taps, emit):
    nc = k.nc
    with ExitStack() as mem:
        h = buffers(k, mem, h=[8, 256]).h
        channel_norm(k, x, h[:], 8, 1024, 1e-6, mod.scale1, mod.shift1)

        def rhs(t):
            return lambda j: t[:, j, :]

        if not emit:
            with buffers_scope(k, z=[28, 256]) as s:
                gemm(k, dram.w_in[l, 2:7], 5, 8, 512, rhs(h), s.z[:, 8:28, :], 256)
                rwkv(k, L, s.z, states, False, None)
            return
        m = buffers(k, mem, m=[8, 256]).m
        ga = buffers(k, mem, g=[8, 256]).g
        with buffers_scope(k, gb=[8, 256], zc=[16, 256], y=[8, 256]) as s:
            gemm(k, dram.w_in[l, 7:11], 4, 8, 512, rhs(h), s.zc[:], 256)
            conv_branch(k, L, s.zc[:], m[:], taps)
            gemm(k, dram.w_oB[l], 2, 8, 512, rhs(m), s.y[:], 256)
            gemm(k, dram.w_in[l, 11:13], 2, 8, 512, rhs(h), ga[:], 256)
            gemm(k, dram.w_in[l, 13:15], 2, 8, 512, rhs(h), s.gb[:], 256)
            with k.stage() as block:

                @block.scalar
                def _(act):
                    for g, t in enumerate((ga, s.gb)):
                        for j in range(8):
                            ins = act.activation(t[:, j, :], t[:, j, :], ACT.Sigmoid, bias=L.gate_b[:, 8 * g + j:8 * g + j + 1])
                    ins.then_inc(k.act_step.up(), 1)

                @block.vector
                def _(dve):
                    dve.wait_ge(k.act_step.sem, k.act_step.at(1))
                    dve.tensor_tensor(m[:], s.gb[:], s.y[:], ALU.mult).then_inc(k.vec_step.up(), 1)
        with buffers_scope(k, z=[28, 256]) as s:
            gemm(k, dram.w_in[l, 0:7], 7, 8, 512, rhs(h), s.z[:], 256)
            rwkv(k, L, s.z, states, True, h[:])
        with buffers_scope(k, y=[8, 256]) as s:
            gemm(k, dram.w_oA[l], 2, 8, 512, rhs(h), s.y[:], 256)
            with k.stage() as block:

                @block.vector
                def _(dve):
                    chain = chained(k, dve)
                    chain(dve.tensor_tensor(s.y[:], s.y[:], ga[:], ALU.mult))
                    chain(dve.tensor_tensor(m[:], m[:], s.y[:], ALU.add))

            gemm(k, dram.w_out[l], 2, 8, 512, rhs(m), s.y[:], 256)
            with k.stage() as block:

                @block.vector
                def _(dve):
                    chain = chained(k, dve)
                    chain(dve.tensor_tensor(s.y[:], s.y[:], over_tokens(mod.gate1, 8, 256), ALU.mult))
                    chain(dve.tensor_tensor(x, x, s.y[:], ALU.add))


HEADS, KEYS, TOPK, SLOTS = 8, 128, 16, 128
RING = 8
LOWEST = -3.0e38


def top16(k, dve, lists, values, work, best, index):
    up = k.vec_step

    def settled():
        dve.wait_ge(up.sem, up.count)

    for n in lists:
        dve.max(best[:, n, 0:8], values(n)).then_inc(up.up(), 1)
    settled()
    for n in lists:
        dve.max_index(index[:, n, 0:8], best[:, n, 0:8], values(n)).then_inc(up.up(), 1)
    for n in lists:
        dve.match_replace(work(n), best[:, n, 0:8], values(n), LOWEST).then_inc(up.up(), 1)
    settled()
    for n in lists:
        dve.max(best[:, n, 8:16], work(n)).then_inc(up.up(), 1)
    settled()
    for n in lists:
        dve.max_index(index[:, n, 8:16], best[:, n, 8:16], work(n)).then_inc(up.up(), 1)
    settled()


def peer(k, l, dram, x, mod):
    nc = k.nc
    with ExitStack() as mem:
        b = buffers(k, mem, h=[8, 256], htok=[2, 1024], gw=[2, SLOTS], dots=[2, SLOTS])
        eidx = mem.enter_context(k.sbuf("expert", [2 * SLOTS + RING], U32))
        channel_norm(k, x, b.h[:], 8, 1024, 1e-6, mod.scale2, mod.shift2)
        with buffers_scope(k, q=[16, 256], keys=[16, P], s=[16, P], work=[16, P], best1=[16, 16], cand=[HEADS, 256],
                           cand2=[HEADS, 256], best=[HEADS, 16], i12=[16, 16], pf=[2, HEADS, 16], hot=[HEADS, 16, 16],
                           e12=[2, HEADS, 16], row=[HEADS]) as s, \
                k.sbuf("idx1", [16, 16], U32) as idx1, k.sbuf("pos", [HEADS, 16], U32) as pos, \
                k.sbuf("posab", [2, HEADS, 16], U32) as posab:
            load(k, (s.keys[:], dram.sub_keys[l]))
            gemm(k, dram.w_q[l], 4, 8, 512, lambda j: b.h[:, j, :], s.q[:], 256)
            for tile in range(2):
                toks = slice(tile * P, tile * P + P)
                with k.stage() as block:

                    @block.tensor
                    def _(pe):
                        for n in range(16):
                            mm = pe.matmul(k.psum[:, n * P:n * P + P], s.q[:, n, toks], s.keys[:, n, :], start=True, stop=True)
                        mm.then_inc(k.multiplied.up(), 1)
                        for j in range(8):
                            mm = pe.transpose(k.psum[:, 2048 + j * P:2048 + j * P + P], b.h[:, j, toks], k.ident)
                        mm.then_inc(k.multiplied.up(), 1)

                    @block.scalar
                    def _(act):
                        act.wait_ge(k.multiplied.sem, k.multiplied.at(1))
                        act.activation(s.s[:], k.psum[:, 0:2048].rearrange("p (n c) -> p n c", n=16), ACT.Copy).then_inc(k.act_step.up(), 1)
                        act.wait_ge(k.multiplied.sem, k.multiplied.at(2))
                        act.activation(b.htok[:, tile, :], k.psum[:, 2048:3072], ACT.Copy).then_inc(k.act_step.up(), 1)

                    @block.vector
                    def _(dve):
                        chain = chained(k, dve)
                        dve.wait_ge(k.act_step.sem, k.act_step.at(1))
                        top16(k, dve, range(16), lambda n: s.s[:, n, :], lambda n: s.work[:, n, :], s.best1, idx1)
                        two = s.best1[:].rearrange("p (h c) j -> p h c j", c=2)
                        chain(dve.tensor_tensor(s.cand[:].rearrange("p h (a b) -> p h a b", b=16),
                                                two[:, :, 0, :].unsqueeze(3).broadcast_to([P, HEADS, 16, 16]),
                                                two[:, :, 1, :].unsqueeze(2).broadcast_to([P, HEADS, 16, 16]), ALU.add))
                        top16(k, dve, range(HEADS), lambda n: s.cand[:, n, :], lambda n: s.cand2[:, n, :], s.best, pos)
                        chain(dve.tensor_scalar(posab[:, 0], pos[:], 4, None, ALU.logical_shift_right))
                        chain(dve.tensor_scalar(posab[:, 1], pos[:], 15, None, ALU.bitwise_and))
                        chain(dve.tensor_copy(s.pf[:], posab[:]))
                        chain(dve.tensor_copy(s.i12[:], idx1[:]))
                        i2 = s.i12[:].rearrange("p (h c) j -> p h c j", c=2)
                        iota = k.iota16.unsqueeze(1).unsqueeze(1).broadcast_to([P, HEADS, 16, 16])
                        for c in range(2):
                            chain(dve.tensor_tensor(s.hot[:], s.pf[:, c].unsqueeze(3).broadcast_to([P, HEADS, 16, 16]), iota, ALU.is_equal))
                            chain(dve.tensor_tensor(s.hot[:], s.hot[:], i2[:, :, c, :].unsqueeze(2).broadcast_to([P, HEADS, 16, 16]), ALU.mult))
                            chain(dve.tensor_reduce(s.e12[:, c], s.hot[:], AXX, ALU.add))
                        chain(dve.scalar_tensor_tensor(s.e12[:, 0], s.e12[:, 0], float(KEYS), s.e12[:, 1], ALU.mult, ALU.add))
                        chain(dve.tensor_scalar(eidx[:, tile * SLOTS:(tile + 1) * SLOTS], s.e12[:, 0].rearrange("p h j -> p (h j)"), float(l * KEYS * KEYS), None, ALU.add))
                        gw = b.gw[:, tile, :].rearrange("p (h j) -> p h j", j=16)
                        chain(dve.tensor_tensor(gw, s.best[:], s.best[:, :, 0:1].broadcast_to([P, HEADS, 16]), ALU.subtract))

                with k.stage() as block:

                    @block.scalar
                    def _(act):
                        act.activation(b.gw[:, tile, :], b.gw[:, tile, :], ACT.Exp).then_inc(k.act_step.up(), 1)

                    @block.vector
                    def _(dve):
                        chain = chained(k, dve)
                        dve.wait_ge(k.act_step.sem, k.act_step.at(1))
                        gw = b.gw[:, tile, :].rearrange("p (h j) -> p h j", j=16)
                        chain(dve.tensor_reduce(s.row[:], gw, AXX, ALU.add))
                        chain(dve.reciprocal(s.row[:], s.row[:]))
                        chain(dve.tensor_tensor(gw, gw, s.row[:].unsqueeze(2).broadcast_to([P, HEADS, 16]), ALU.mult))

        with ExitStack() as inner:
            r = buffers(k, inner, ring=[RING, 1024], acc=[2, 1024], dot8=[2, RING], act8=[2, RING])
            idx8 = [inner.enter_context(k.sbuf("expert_group", [RING], U32)) for _ in range(2)]
            groups = SLOTS // RING
            rounds = groups // 2
            passes = [(dram.peer_u, 0), (dram.peer_u, 1), (dram.peer_v, 0), (dram.peer_v, 1)]
            with k.stage() as block:
                def turn(n, i, part):
                    return i * 2 + (n * groups + part)

                @block.gpsimd
                def _(pool):
                    for n, (table, tile) in enumerate(passes):
                        def gather(i, part, first=False):
                            g = turn(n, i, part)
                            pool.wait_ge(k.staged.sem, g + k.staged.at(1))
                            pool.sem_inc(k.slot_free.sem, 1)
                            for j in range(RING):
                                if not first:
                                    pool.wait_ge(k.row_used.sem, g * RING + (k.row_used.at(1) + j - RING))
                                    pool.sem_inc(k.slot_free.sem, 1)
                                pool.indirect_dma_start(
                                    r.ring[:, j, :], None, table,
                                    bass.IndirectOffsetOnAxis(ap=idx8[part][:, j:j + 1], axis=0),
                                ).then_inc(k.gathered[j].sem, 16)

                        start = 0
                        if n == 0:
                            gather(0, 0, True)
                            gather(0, 1)
                            start = 1
                        with pool.Fori(start, rounds) as i:
                            gather(i, 0)
                            gather(i, 1)

                @block.vector
                def _(dve):
                    dve.memset(r.acc[:], 0.0).then_inc(k.vec_step.up(), 1)
                    dve.tensor_copy(eidx[:, 2 * SLOTS:2 * SLOTS + RING], eidx[:, 0:RING]).then_inc(k.vec_step.up(), 1)
                    dve.tensor_copy(idx8[0][:], eidx[:, 0:RING]).then_inc(k.staged.sem, 1)
                    dve.wait_ge(k.vec_step.sem, k.vec_step.count)
                    for n, (_, tile) in enumerate(passes):
                        if n >= 2:
                            dve.wait_ge(k.act_step.sem, k.act_step.at(tile + 1))
                            dve.tensor_tensor(b.dots[:, tile, :], b.dots[:, tile, :], b.gw[:, tile, :], ALU.mult).then_inc(k.weighted.up(), 1)
                            dve.wait_ge(k.weighted.sem, k.weighted.count)

                        def use(i, part):
                            g = turn(n, i, part)
                            at = i * (2 * RING) + part * RING
                            dve.tensor_copy(idx8[1 - part][:], eidx[:, bass.ds(at + (tile * SLOTS + RING), RING)]).then_inc(k.staged.sem, 1)
                            if n >= 2:
                                dve.tensor_copy(r.act8[:, part, :], b.dots[:, tile, bass.ds(at, RING)]).then_inc(k.weights_staged.sem, 1)
                                dve.wait_ge(k.weights_staged.sem, i * 2 + (k.weights_staged.at(1) + (n - 2) * groups + part))
                            for j in range(RING):
                                dve.wait_ge(k.gathered[j].sem, g * 16 + k.gathered[j].at(16))
                                if n < 2:
                                    dve.tensor_tensor_reduce(r.ring[:, j, :], r.ring[:, j, :], b.htok[:, tile, :], 1.0, 0.0, ALU.mult,
                                                             ALU.add, r.dot8[:, part, j:j + 1]).then_inc(k.row_used.sem, 1)
                                else:
                                    dve.wait_ge(k.row_used.sem, g * RING + (k.row_used.at(0) + j))
                                    dve.scalar_tensor_tensor(r.acc[:, tile, :], r.ring[:, j, :], r.act8[:, part, j:j + 1],
                                                             r.acc[:, tile, :], ALU.mult, ALU.add).then_inc(k.row_used.sem, 1)
                            if n < 2:
                                dve.wait_ge(k.row_used.sem, g * RING + k.row_used.at(RING))
                                dve.tensor_copy(b.dots[:, tile, bass.ds(at, RING)], r.dot8[:, part, :]).then_inc(k.dots_kept.sem, 1)

                        with dve.Fori(0, rounds) as i:
                            use(i, 0)
                            use(i, 1)

                @block.scalar
                def _(act):
                    for tile in range(2):
                        act.wait_ge(k.dots_kept.sem, k.dots_kept.at((tile + 1) * groups))
                        act.activation(b.dots[:, tile, :], b.dots[:, tile, :], ACT.Gelu).then_inc(k.act_step.up(), 1)

                k.staged.up(4 * groups + 1)
                k.row_used.up(4 * SLOTS)
                k.dots_kept.up(2 * groups)
                k.weights_staged.up(2 * groups)
                for j in range(RING):
                    k.gathered[j].up(16 * 4 * groups)

            with k.stage() as block:

                @block.tensor
                def _(pe):
                    for j in range(8):
                        for i in range(2):
                            mm = pe.transpose(k.psum[:, 256 * j + P * i:256 * j + P * i + P], r.acc[:, i, P * j:P * j + P], k.ident)
                    mm.then_inc(k.multiplied.up(), 1)

                @block.vector
                def _(dve):
                    dve.wait_ge(k.multiplied.sem, k.multiplied.at(1))
                    for j in range(8):
                        dve.scalar_tensor_tensor(x[:, j, :], k.psum[:, 256 * j:256 * j + 256], mod.gate2[:, j:j + 1], x[:, j, :],
                                                 ALU.mult, ALU.add).then_inc(k.vec_step.up(), 1)



DN_Q, DN_K, DN_V, DN_Z, CQ, CKV, KPE, GLA_Q, GLA_K, GLA_V, GLA_G, GLA_LR, FOX_Q, FOX_K, FOX_V, SMALL = (
    0, 2, 4, 6, 8, 10, 11, 12, 13, 14, 16, 18, 19, 21, 23, 25)
VECTORS2 = {"norm_mix_pre_2": 8, "norm_mix_post_2": 8, "norm_mlp_pre_2": 8, "norm_mlp_post_2": 8, "dn_conv_2": 24, "mla_q_norm_2": 2,
            "mla_kv_norm_2": 1, "gla_gate_bias_2": 1, "b_gate_2": 32, "dn_norm_2": 1, "gla_norm_2": 1}
ROWS2 = ("dn_dt_bias_2", "fox_f_bias_2", "dn_a_log_2")


def per_head(column, n):
    return column.unsqueeze(2).broadcast_to([P, 4, n])


def heads4(t):
    return t.rearrange("p (h c) -> p h c", h=4)


def for_heads(mask, n):
    return mask.unsqueeze(1).broadcast_to([P, n, mask.shape[1]])


def to_tokens(k, pairs):
    with k.stage() as block:

        @block.tensor
        def _(pe):
            for n, (src, _) in enumerate(pairs):
                for i in range(2):
                    mm = pe.transpose(k.psum[:, 256 * n + P * i:256 * n + P * i + P], src[:, P * i:P * i + P], k.ident)
            mm.then_inc(k.multiplied.up(), 1)

        @block.scalar
        def _(act):
            act.wait_ge(k.multiplied.sem, k.multiplied.at(1))
            for n, (_, dst) in enumerate(pairs):
                act.activation(dst, k.psum[:, 256 * n:256 * n + 256].rearrange("p (i c) -> p i c", i=2), ACT.Copy
                               ).then_inc(k.act_step.up(), 1)


def to_channels(k, y, out, gain=None, gate=None):
    with k.stage() as block:

        @block.tensor
        def _(pe):
            for j in range(2):
                for i in range(2):
                    mm = pe.transpose(k.psum[:, 256 * j + P * i:256 * j + P * i + P], y[:, i, P * j:P * j + P], k.ident)
            mm.then_inc(k.multiplied.up(), 1)

        @block.vector
        def _(dve):
            dve.wait_ge(k.multiplied.sem, k.multiplied.at(1))
            turned = k.psum[:, 0:512].rearrange("p (j t) -> p j t", j=2)
            if gate is None:
                dve.tensor_copy(out, turned).then_inc(k.vec_step.up(), 1)
            else:
                dve.scalar_tensor_tensor(out, turned, gain, gate, ALU.mult, ALU.mult).then_inc(k.vec_step.up(), 1)


def silu(k, t, tmp):
    with k.stage() as block:

        @block.scalar
        def _(act):
            act.activation(tmp, t, ACT.Sigmoid).then_inc(k.act_step.up(), 1)

        @block.vector
        def _(dve):
            dve.wait_ge(k.act_step.sem, k.act_step.at(1))
            dve.tensor_tensor(t, t, tmp, ALU.mult).then_inc(k.vec_step.up(), 1)


def softplus(k, y, tmp, out, scale):
    with k.stage() as block:

        @block.vector
        def _(dve):
            chain = chained(k, dve)
            chain(dve.scalar_tensor_tensor(tmp, y, -1.0, y, ALU.mult, ALU.min))
            dve.wait_ge(k.act_step.sem, k.act_step.at(2))
            chain(dve.scalar_tensor_tensor(out, y, 0.0, tmp, ALU.max, ALU.add))
            chain(dve.tensor_scalar(out, out, scale, None, ALU.mult))

        @block.scalar
        def _(act):
            act.wait_ge(k.vec_step.sem, k.vec_step.at(1))
            act.activation(tmp, tmp, ACT.Exp).then_inc(k.act_step.up(), 1)
            act.wait_ge(k.act_step.sem, k.act_step.at(1))
            act.activation(tmp, tmp, ACT.Ln, bias=1.0).then_inc(k.act_step.up(), 1)


def head_norm(k, y, squares, row):
    with k.stage() as block:
        marks = []

        @block.vector
        def _(dve):
            chain = chained(k, dve)
            chain(dve.tensor_tensor(squares, y, y, ALU.mult))
            chain(dve.tensor_reduce(row, squares, AXX, ALU.add))
            chain(dve.tensor_scalar(row, row, 1.0 / 64, 1e-6, ALU.mult, ALU.add))
            marks.append(k.vec_step.count)
            dve.wait_ge(k.act_step.sem, k.act_step.at(1))
            chain(dve.reciprocal(row, row))
            chain(dve.tensor_tensor(y, y, row.unsqueeze(2).broadcast_to([P, 8, 64]), ALU.mult))

        @block.scalar
        def _(act):
            act.wait_ge(k.vec_step.sem, marks[0])
            act.activation(row, row, ACT.Sqrt).then_inc(k.act_step.up(), 1)


def delta_branch(k, V, z, small, out):
    with buffers_scope(k, conv=[6, 256], tmp=[6, 256], ktok=[2, 256], vtok=[2, 256], km=[4, 256], qm=[4, 256], row=[8],
                       gcol=[2, 4], eg=[2, 4], bne=[2, 4], etail=[2, 4], eT=[2, 2, 4], D=[2, 4, P], L=[2, 4, P], Aq=[2, 4, P],
                       AqT=[2, 4, P], Ld=[2, 4, P], LdT=[2, 4, P], NT=[2, 4, P], E1=[2, 4, P], E2=[2, 4, P], E3=[2, 4, P],
                       X=[2, 4, P], TT=[2, 4, P], S=[2, P], R=[256], U=[2, 256], Y=[2, 256], inc=[2, P]) as b:
        beta, g = small.beta, small.g
        conv = b.conv
        with k.stage() as block:

            @block.vector
            def _(dve):
                chain = chained(k, dve)
                w = V.dn_conv_2.rearrange("p (r j) -> p r j", r=4)
                chain(dve.tensor_tensor(conv[:], z[:, 0:6, :], over_tokens(w[:, 3, :], 6, 256), ALU.mult))
                for r in range(3):
                    late = 3 - r
                    chain(dve.tensor_tensor(b.tmp[:, :, late:256], z[:, 0:6, 0:256 - late], over_tokens(w[:, r, :], 6, 256 - late), ALU.mult))
                    chain(dve.tensor_tensor(conv[:, :, late:256], conv[:, :, late:256], b.tmp[:, :, late:256], ALU.add))

        silu(k, conv[:], b.tmp[:])
        with k.stage() as block:

            @block.scalar
            def _(act):
                act.activation(b.tmp[:, 0:4, :], conv[:, 0:4, :], ACT.Square).then_inc(k.act_step.up(), 1)
                act.wait_ge(k.vec_step.sem, k.vec_step.at(1))
                act.activation(b.tmp[:, 0:4, :], b.tmp[:, 0:4, :], ACT.Sqrt).then_inc(k.act_step.up(), 1)

            @block.tensor
            def _(pe):
                pe.wait_ge(k.act_step.sem, k.act_step.at(1))
                for j in range(4):
                    mm = pe.matmul(k.psum[:, 256 * j:256 * j + 256], k.blocks64, b.tmp[:, j, :], start=True, stop=True)
                mm.then_inc(k.multiplied.up(), 1)

            @block.vector
            def _(dve):
                chain = chained(k, dve)
                dve.wait_ge(k.multiplied.sem, k.multiplied.at(1))
                t = b.tmp[:, 0:4, :]
                chain(dve.tensor_scalar(t, k.psum[:, 0:1024].rearrange("p (j t) -> p j t", j=4), 1e-6, None, ALU.add))
                dve.wait_ge(k.act_step.sem, k.act_step.at(2))
                chain(dve.reciprocal(t, t))
                chain(dve.tensor_tensor(conv[:, 0:4, :], conv[:, 0:4, :], t, ALU.mult))
                chain(dve.tensor_scalar(conv[:, 0:2, :], conv[:, 0:2, :], 64 ** -0.5, None, ALU.mult))
                for h in range(4):
                    chain(dve.tensor_scalar(b.qm[:, h, :], conv[:, h // 2, :], k.half_mask[h % 2], None, ALU.mult))
                    chain(dve.tensor_scalar(b.km[:, h, :], conv[:, 2 + h // 2, :], k.half_mask[h % 2], None, ALU.mult))
                chain(dve.memset(b.S[:], 0.0))

        to_tokens(k, [(conv[:, 2 + j, :], b.ktok[:, :, P * j:P * j + P]) for j in range(2)]
                  + [(conv[:, 4 + j, :], b.vtok[:, :, P * j:P * j + P]) for j in range(2)])
        for i in range(2):
            toks = slice(P * i, P * i + P)
            with k.stage() as block:

                @block.tensor
                def _(pe):
                    gi = g[:, i, :]
                    for n, m in enumerate((k.up_incl, k.blocks64, k.chunk0, k.chunk1)):
                        pe.matmul(k.bank(0)[:, 4 * n:4 * n + 4], m, gi, start=True, stop=True)
                    for h in range(4):
                        hs = slice(P * h, P * h + P)
                        pe.matmul(k.bank(1)[:, hs], g[:, i, h:h + 1].broadcast_to([P, P]), k.up_incl, start=True, stop=True)
                        pe.matmul(k.bank(2)[:, hs], b.km[:, h, toks], conv[:, 2 + h // 2, toks], start=True, stop=True)
                        mm = pe.matmul(k.bank(3)[:, hs], b.qm[:, h, toks], conv[:, 2 + h // 2, toks], start=True, stop=True)
                    mm.then_inc(k.multiplied.up(), 1)

                @block.vector
                def _(dve):
                    chain = chained(k, dve)
                    dve.wait_ge(k.multiplied.sem, k.multiplied.at(1))
                    sums = k.bank(0)
                    chain(dve.tensor_copy(b.gcol[:, i, :], sums[:, 0:4]))
                    chain(dve.tensor_tensor(b.etail[:, i, :], sums[:, 4:8], b.gcol[:, i, :], ALU.subtract))
                    chain(dve.tensor_copy(b.eT[:, i], sums[:, 8:16].rearrange("p (c h) -> p c h", c=2)))
                    for h in range(4):
                        chain(dve.tensor_scalar(b.D[:, i, h, :], k.bank(1)[:, P * h:P * h + P], -1.0, b.gcol[:, i, h:h + 1], ALU.mult, ALU.add))
                    chain(dve.tensor_tensor(b.D[:, i], b.D[:, i], for_heads(k.lo_incl, 4), ALU.mult))

            with k.stage() as block:

                @block.scalar
                def _(act):
                    act.activation(b.D[:, i], b.D[:, i], ACT.Exp).then_inc(k.act_step.up(), 1)
                    act.activation(b.eg[:, i, :], b.gcol[:, i, :], ACT.Exp).then_inc(k.act_step.up(), 1)
                    act.activation(b.etail[:, i, :], b.etail[:, i, :], ACT.Exp).then_inc(k.act_step.up(), 1)
                    act.activation(b.eT[:, i], b.eT[:, i], ACT.Exp).then_inc(k.act_step.up(), 1)

                @block.vector
                def _(dve):
                    chain = chained(k, dve)
                    dve.wait_ge(k.act_step.sem, k.act_step.at(4))
                    chain(dve.scalar_tensor_tensor(b.bne[:, i, :], b.eg[:, i, :], -1.0, beta[:, i, :], ALU.mult, ALU.mult))
                    chain(dve.tensor_tensor(b.D[:, i], b.D[:, i], for_heads(k.lo_incl, 4), ALU.mult))
                    chain(dve.scalar_tensor_tensor(b.L[:, i], heads4(k.bank(2)), -1.0, b.D[:, i], ALU.mult, ALU.mult))
                    chain(dve.tensor_tensor(b.L[:, i], b.L[:, i], for_heads(k.lo, 4), ALU.mult))
                    chain(dve.tensor_tensor(b.L[:, i], b.L[:, i], per_head(beta[:, i, :], P), ALU.mult))
                    chain(dve.tensor_tensor(b.Aq[:, i], heads4(k.bank(3)), b.D[:, i], ALU.mult))
                    chain(dve.tensor_tensor(b.Ld[:, i], b.L[:, i], for_heads(k.lo8, 4), ALU.mult))
                    chain(dve.tensor_tensor(heads4(b.vtok[:, i, :]), heads4(b.vtok[:, i, :]), per_head(beta[:, i, :], 64), ALU.mult))
                    chain(dve.tensor_tensor(heads4(b.ktok[:, i, :]), heads4(b.ktok[:, i, :]), per_head(b.etail[:, i, :], 64), ALU.mult))

            with k.stage() as block:

                @block.tensor
                def _(pe):
                    for h in range(4):
                        pe.transpose(k.bank(4)[:, P * h:P * h + P], b.L[:, i, h, :], k.ident)
                        mm = pe.transpose(k.bank(5)[:, P * h:P * h + P], b.Aq[:, i, h, :], k.ident)
                    mm.then_inc(k.multiplied.up(), 1)

                @block.vector
                def _(dve):
                    dve.wait_ge(k.multiplied.sem, k.multiplied.at(1))
                    dve.tensor_tensor(b.LdT[:, i], heads4(k.bank(4)), for_heads(k.up8, 4), ALU.mult).then_inc(k.vec_step.up(), 1)
                    dve.tensor_tensor(b.NT[:, i], heads4(k.bank(4)), for_heads(k.up_far, 4), ALU.mult).then_inc(k.vec_step.up(), 1)
                    dve.tensor_copy(b.AqT[:, i], heads4(k.bank(5))).then_inc(k.vec_step.up(), 1)

        invert_unit_lower(k, 2, b.Ld, b.LdT, b.NT, (b.E1, b.E2, b.E3, b.X), b.TT)
        for i in range(2):
            toks = slice(P * i, P * i + P)
            bK, bQ, bU, bS, bY = (k.bank(n, 256) for n in range(5))
            y = b.Y[:, i, :]
            with k.stage() as block:
                marks = {}

                @block.vector
                def _(dve):
                    chain = chained(k, dve)
                    for c in range(2):
                        dve.wait_ge(k.multiplied.sem, k.multiplied.at(3 * c + 1))
                        chain(dve.tensor_tensor(heads4(b.R[:]), heads4(bK), per_head(b.bne[:, i, :], 64), ALU.mult))
                        chain(dve.tensor_tensor(b.R[:], b.R[:], b.vtok[:, i, :], ALU.add))
                        marks["R", c] = k.vec_step.count
                        if c == 0:
                            chain(dve.tensor_scalar(y, bQ, k.half_mask[0], None, ALU.mult))
                        else:
                            chain(dve.scalar_tensor_tensor(y, bQ, k.half_mask[1], y, ALU.mult, ALU.add))
                        dve.wait_ge(k.multiplied.sem, k.multiplied.at(3 * c + 2))
                        chain(dve.tensor_scalar(b.U[:, c, :], bU, k.half_mask[c], None, ALU.mult))
                        marks["U", c] = k.vec_step.count
                        dve.wait_ge(k.multiplied.sem, k.multiplied.at(3 * c + 3))
                        chain(dve.tensor_tensor(b.inc[:], bS.rearrange("p (j v) -> p j v", j=2), for_heads(k.blocks64, 2), ALU.mult))
                        S4 = b.S[:].rearrange("p j (h v) -> p (j h) v", h=2)
                        chain(dve.tensor_tensor(S4, S4, per_head(b.eT[:, i, c, :], 64), ALU.mult))
                        chain(dve.tensor_tensor(b.S[:], b.S[:], b.inc[:], ALU.add))
                        marks["S", c] = k.vec_step.count
                    chain(dve.tensor_tensor(heads4(y), heads4(y), per_head(b.eg[:, i, :], 64), ALU.mult))
                    chain(dve.tensor_tensor(b.U[:, 0, :], b.U[:, 0, :], b.U[:, 1, :], ALU.add))
                    marks["Usum"] = k.vec_step.count
                    dve.wait_ge(k.multiplied.sem, k.multiplied.at(7))
                    chain(dve.tensor_tensor(y, y, bY, ALU.add))

                @block.tensor
                def _(pe):
                    for c in range(2):
                        if c:
                            pe.wait_ge(k.vec_step.sem, marks["S", 0])
                        for j in range(2):
                            js = slice(P * j, P * j + P)
                            pe.matmul(bK[:, js], conv[:, 2 + j, toks], b.S[:, j, :], start=True, stop=True)
                            mm = pe.matmul(bQ[:, js], conv[:, j, toks], b.S[:, j, :], start=True, stop=True)
                        mm.then_inc(k.multiplied.up(), 1)
                        pe.wait_ge(k.vec_step.sem, marks["R", c])
                        for h in range(4):
                            hs = slice(64 * h, 64 * h + 64)
                            mm = pe.matmul(bU[:, hs], b.TT[:, i, h, :], b.R[:, hs], start=True, stop=True)
                        mm.then_inc(k.multiplied.up(), 1)
                        pe.wait_ge(k.vec_step.sem, marks["U", c])
                        for j in range(2):
                            js = slice(P * j, P * j + P)
                            mm = pe.matmul(bS[:, js], b.ktok[:, i, js], b.U[:, c, js], start=True, stop=True)
                        mm.then_inc(k.multiplied.up(), 1)
                    pe.wait_ge(k.vec_step.sem, marks["Usum"])
                    for h in range(4):
                        hs = slice(64 * h, 64 * h + 64)
                        mm = pe.matmul(bY[:, hs], b.AqT[:, i, h, :], b.U[:, 0, hs], start=True, stop=True)
                    mm.then_inc(k.multiplied.up(), 1)

        head_norm(k, b.Y[:].rearrange("p i (h v) -> p (i h) v", v=64), b.tmp[:, 0:2, :].rearrange("p i (h v) -> p (i h) v", v=64), b.row[:])
        silu(k, z[:, DN_Z:DN_Z + 2, :], b.tmp[:, 0:2, :])
        to_channels(k, b.Y, out, V.dn_norm_2, z[:, DN_Z:DN_Z + 2, :])


def gla_branch(k, V, z, gate_up, out):
    with buffers_scope(k, w=[256], tmp=[256], cum=[256], tot=[4], pc=[4], dist=[256], qin=[256], kin=[256], ktail=[256], qm=[4, 256],
                       ktok=[2, P], vtok=[2, 256], Vc=[2, 2, 256], AT=[2, 4, P], S=[256], inc=[256], Y=[2, 256], squares=[8, 64],
                       row=[8], tmp2=[2, 256]) as b:
        with k.stage() as block:

            @block.tensor
            def _(pe):
                pe.matmul(k.bank(0, 256), gate_up, z[0:16, GLA_LR, :], start=True, stop=True).then_inc(k.multiplied.up(), 1)

            @block.vector
            def _(dve):
                dve.wait_ge(k.multiplied.sem, k.multiplied.at(1))
                dve.tensor_scalar(b.w[:], k.bank(0, 256), V.gla_gate_bias_2, -1.0, ALU.add, ALU.mult).then_inc(k.vec_step.up(), 1)

        softplus(k, b.w[:], b.tmp[:], b.w[:], -1.0 / 16.0)
        with k.stage() as block:

            @block.vector
            def _(dve):
                chain = chained(k, dve)
                chain(dve.tensor_tensor_scan(b.cum[:], k.segments[:, 0:256], b.w[:], 0.0, ALU.mult, ALU.add))
                chain(dve.tensor_copy(b.tot[:], b.cum[:, 63::64]))
                chain(dve.tensor_tensor(b.dist[:].rearrange("p (c t) -> p c t", c=4), b.tot[:].unsqueeze(2).broadcast_to([P, 4, 64]),
                                        b.cum[:].rearrange("p (c t) -> p c t", c=4), ALU.subtract))
                dve.wait_ge(k.act_step.sem, k.act_step.at(4))
                chain(dve.scalar_tensor_tensor(b.qin[:], b.qin[:], 32 ** -0.5, z[:, GLA_Q, :], ALU.mult, ALU.mult))
                chain(dve.tensor_tensor(b.kin[:], b.kin[:], z[:, GLA_K, :], ALU.mult))
                chain(dve.tensor_tensor(b.ktail[:], b.dist[:], z[:, GLA_K, :], ALU.mult))
                for h in range(4):
                    chain(dve.tensor_scalar(b.qm[:, h, :], b.qin[:], k.quarter_mask[h], None, ALU.mult))
                chain(dve.memset(b.S[:], 0.0))
                chain(dve.memset(b.AT[:], 0.0))

            @block.scalar
            def _(act):
                act.wait_ge(k.vec_step.sem, k.vec_step.at(3))
                act.activation(b.qin[:], b.cum[:], ACT.Exp).then_inc(k.act_step.up(), 1)
                act.activation(b.kin[:], b.cum[:], ACT.Exp, scale=-1.0).then_inc(k.act_step.up(), 1)
                act.activation(b.pc[:], b.tot[:], ACT.Exp).then_inc(k.act_step.up(), 1)
                act.activation(b.dist[:], b.dist[:], ACT.Exp).then_inc(k.act_step.up(), 1)

        to_tokens(k, [(b.ktail[:], b.ktok[:])] + [(z[:, GLA_V + j, :], b.vtok[:, :, P * j:P * j + P]) for j in range(2)])
        with k.stage() as block:
            marks = {}

            @block.vector
            def _(dve):
                chain = chained(k, dve)
                for i in range(2):
                    for c in range(2):
                        chain(dve.tensor_scalar(b.Vc[:, i, c, :], b.vtok[:, i, :], k.half_mask[c], None, ALU.mult))
                marks["V"] = k.vec_step.count
                allowed = for_heads(k.up_incl, 4).bitcast(U32)
                for i in range(2):
                    dve.wait_ge(k.multiplied.sem, k.multiplied.at(i + 1))
                    chain(dve.copy_predicated(b.AT[:, i], allowed, heads4(k.bank(i))))
                marks["A"] = k.vec_step.count
                for n in range(4):
                    i, c = n // 2, n % 2
                    y = b.Y[:, i, :]
                    dve.wait_ge(k.multiplied.sem, k.multiplied.at(3 + n))
                    if c == 0:
                        chain(dve.tensor_scalar(y, k.bank(2, 256), k.half_mask[0], None, ALU.mult))
                    else:
                        chain(dve.scalar_tensor_tensor(y, k.bank(2, 256), k.half_mask[1], y, ALU.mult, ALU.add))
                    chain(dve.tensor_tensor(heads4(b.inc[:]), heads4(k.bank(3, 256)), per_head(k.quarters, 64), ALU.mult))
                    chain(dve.scalar_tensor_tensor(b.S[:], b.S[:], b.pc[:, n:n + 1], b.inc[:], ALU.mult, ALU.add))
                    marks["S", n] = k.vec_step.count
                dve.wait_ge(k.multiplied.sem, k.multiplied.at(7))
                chain(dve.tensor_tensor(b.Y[:], b.Y[:], k.bank(4).rearrange("p (i v) -> p i v", i=2), ALU.add))

            @block.tensor
            def _(pe):
                for i in range(2):
                    toks = slice(P * i, P * i + P)
                    pe.matmul(heads4(k.bank(i)), b.kin[:, toks], b.qm[:, :, toks], start=True, stop=True).then_inc(k.multiplied.up(), 1)
                pe.wait_ge(k.vec_step.sem, marks["V"])
                for n in range(4):
                    i, c = n // 2, n % 2
                    if n:
                        pe.wait_ge(k.vec_step.sem, marks["S", n - 1])
                    pe.matmul(k.bank(2, 256), b.qin[:, P * i:P * i + P], b.S[:], start=True, stop=True)
                    pe.matmul(k.bank(3, 256), b.ktok[:, i, :], b.Vc[:, i, c, :], start=True, stop=True).then_inc(k.multiplied.up(), 1)
                for i in range(2):
                    for h in range(4):
                        at = 256 * i + 64 * h
                        mm = pe.matmul(k.bank(4)[:, at:at + 64], b.AT[:, i, h, :], b.vtok[:, i, 64 * h:64 * h + 64], start=True, stop=True)
                mm.then_inc(k.multiplied.up(), 1)

        head_norm(k, b.Y[:].rearrange("p i (h v) -> p (i h) v", v=64), b.squares[:], b.row[:])
        silu(k, z[:, GLA_G:GLA_G + 2, :], b.tmp2[:])
        to_channels(k, b.Y, out, V.gla_norm_2, z[:, GLA_G:GLA_G + 2, :])


def attention(k, products, scale, mask, v, forget, out):
    with buffers_scope(k, vtok=[2, 256], F=[4, 256], lg=[4, 256], top=[4], total=[4], PT=[2, 4, P], Y=[2, 256]) as b:
        to_tokens(k, [(v[:, j, :], b.vtok[:, :, P * j:P * j + P]) for j in range(2)])
        if forget is not None:
            with k.stage() as block:

                @block.tensor
                def _(pe):
                    for h in range(4):
                        for m in range(2):
                            at = 256 * h + P * m
                            for i in range(m + 1):
                                mm = pe.matmul(k.psum[:, at:at + P], forget[:, i, h:h + 1].broadcast_to([P, P]),
                                               k.upto if i == m else k.ones, start=(i == 0), stop=(i == m))
                    mm.then_inc(k.multiplied.up(), 1)

                @block.vector
                def _(dve):
                    dve.wait_ge(k.multiplied.sem, k.multiplied.at(1))
                    dve.tensor_copy(b.F[:], heads4(k.psum[:, 0:1024])).then_inc(k.vec_step.up(), 1)

        for i in range(2):
            n = P * (i + 1)
            toks, keys = slice(P * i, n), slice(0, n)
            with k.stage() as block:
                logits = k.psum[:, 0:4 * 256].rearrange("p (h s) -> p h s", h=4)[:, :, 0:n]
                lg = b.lg[:, :, 0:n]
                marks = {}

                @block.vector
                def _(dve):
                    chain = chained(k, dve)
                    dve.wait_ge(k.multiplied.sem, k.multiplied.at(1))
                    if forget is None:
                        chain(dve.tensor_scalar(lg, logits, scale, None, ALU.mult))
                    else:
                        chain(dve.scalar_tensor_tensor(lg, logits, scale, b.F[:, :, 0:n], ALU.mult, ALU.subtract))
                    chain(dve.tensor_tensor(b.lg[:, :, toks], b.lg[:, :, toks], for_heads(mask, 4), ALU.add))
                    chain(dve.tensor_reduce(b.top[:], lg, AXX, ALU.max))
                    chain(dve.tensor_tensor(lg, lg, per_head(b.top[:], n), ALU.subtract))
                    marks["less"] = k.vec_step.count
                    dve.wait_ge(k.act_step.sem, k.act_step.at(1))
                    chain(dve.tensor_reduce(b.total[:], lg, AXX, ALU.add))
                    chain(dve.reciprocal(b.total[:], b.total[:]))
                    dve.wait_ge(k.multiplied.sem, k.multiplied.at(3))
                    y = heads4(b.Y[:, i, :])
                    chain(dve.tensor_tensor(y, heads4(k.bank(4, 256)), per_head(b.total[:], 64), ALU.mult))

                @block.scalar
                def _(act):
                    act.wait_ge(k.vec_step.sem, marks["less"])
                    act.activation(lg, lg, ACT.Exp).then_inc(k.act_step.up(), 1)
                    act.wait_ge(k.multiplied.sem, k.multiplied.at(2))
                    act.activation(b.PT[:, 0:i + 1], k.psum[:, 1024:1024 + 512 * (i + 1)].rearrange("p (m h t) -> p m h t", h=4, t=P),
                                   ACT.Copy).then_inc(k.act_step.up(), 1)

                @block.tensor
                def _(pe):
                    for h in range(4):
                        pairs = products(h, toks, keys)
                        for a, (q, kk) in enumerate(pairs):
                            mm = pe.matmul(logits[:, h, :], q, kk, start=(a == 0), stop=(a == len(pairs) - 1))
                    mm.then_inc(k.multiplied.up(), 1)
                    pe.wait_ge(k.act_step.sem, k.act_step.at(1))
                    for m in range(i + 1):
                        for h in range(4):
                            at = 1024 + 512 * m + P * h
                            mm = pe.transpose(k.psum[:, at:at + P], b.lg[:, h, P * m:P * m + P], k.ident)
                    mm.then_inc(k.multiplied.up(), 1)
                    pe.wait_ge(k.act_step.sem, k.act_step.at(2))
                    for h in range(4):
                        for m in range(i + 1):
                            mm = pe.matmul(k.bank(4)[:, 64 * h:64 * h + 64], b.PT[:, m, h, :], b.vtok[:, m, 64 * h:64 * h + 64],
                                           start=(m == 0), stop=(m == i))
                    mm.then_inc(k.multiplied.up(), 1)

        to_channels(k, b.Y, out)


def fox_branch(k, z, forget, out):
    with buffers_scope(k, qm=[4, 256]) as b:
        with k.stage() as block:

            @block.vector
            def _(dve):
                for h in range(4):
                    dve.tensor_scalar(b.qm[:, h, :], z[:, FOX_Q + h // 2, :], k.half_mask[h % 2], None, ALU.mult).then_inc(k.vec_step.up(), 1)

        attention(k, lambda h, toks, keys: [(b.qm[:, h, toks], z[:, FOX_K + h // 2, keys])], 64 ** -0.5, k.causal,
                  z[:, FOX_V:FOX_V + 2, :], forget, out)


def mla_branch(k, V, z, dram, out):
    with buffers_scope(k, cq=[2, 256], ckv=[1, 256], q=[4, 256], kv=[4, 256], rot=[256], qm=[4, 256], qpm=[4, 256]) as b:
        channel_norm(k, z[:, CQ:CQ + 2, :], b.cq[:], 2, 256, 1e-6, V.mla_q_norm_2)
        channel_norm(k, z[:, CKV:CKV + 1, :], b.ckv[:], 1, 128, 1e-6, V.mla_kv_norm_2)
        gemm(k, dram.mla_q_up, 1, 2, 512, lambda j: b.cq[:, j, :], b.q[:], 256)
        gemm(k, dram.mla_kv_up, 1, 1, 512, lambda j: b.ckv[:, j, :], b.kv[:], 256)
        with k.stage() as block:

            @block.tensor
            def _(pe):
                pe.matmul(k.bank(0, 256), k.turn, b.q[:, 2, :], start=True, stop=True)
                pe.matmul(k.bank(1, 256), k.turn, z[:, KPE, :], start=True, stop=True).then_inc(k.multiplied.up(), 1)

            @block.vector
            def _(dve):
                chain = chained(k, dve)
                dve.wait_ge(k.multiplied.sem, k.multiplied.at(1))
                for n, t in enumerate((b.q[:, 2, :], z[:, KPE, :])):
                    chain(dve.tensor_tensor(b.rot[:], k.bank(n, 256), k.sin, ALU.mult))
                    chain(dve.tensor_tensor(t, t, k.cos, ALU.mult))
                    chain(dve.tensor_tensor(t, t, b.rot[:], ALU.add))
                for h in range(4):
                    chain(dve.tensor_scalar(b.qm[:, h, :], b.q[:, h // 2, :], k.half_mask[h % 2], None, ALU.mult))
                    chain(dve.tensor_scalar(b.qpm[:, h, :], b.q[:, 2, :], k.quarter_mask[h], None, ALU.mult))

        attention(k, lambda h, toks, keys: [(b.qm[:, h, toks], b.kv[:, h // 2, keys]), (b.qpm[:, h, toks], z[:, KPE, keys])],
                  96 ** -0.5, k.chunk_causal, b.kv[:, 2:4, :], None, out)


def second_block(k, dram, x):
    with ExitStack() as mem:
        lay = Layout(VECTORS2)
        c = buffers(k, mem, vec=[lay.width], rows=[12], gate_up=[P], h=[8, 256], branches=[4, 2, 256])
        load(k, (c.vec[:], dram.vectors2), (c.rows[:], dram.rows2), (c.gate_up[0:16, :], dram.gate_up))
        V = names(**{name: c.vec[:, a:z] for name, (a, z) in lay.at.items()})
        channel_norm(k, x[:], c.h[:], 8, 1024, 1e-6, V.norm_mix_pre_2)

        def rhs(t):
            return lambda j: t[:, j, :]

        with buffers_scope(k, z=[28, 256], rates=[2, 12], beta=[2, 4], y=[2, 8], tmp=[2, 8], ea=[4]) as s:
            gemm(k, dram.w_in_2, 7, 8, 512, rhs(c.h), s.z[:], 256)
            with k.stage() as block:

                @block.tensor
                def _(pe):
                    for i in range(2):
                        mm = pe.transpose(k.psum[:, P * i:P * i + P], s.z[:, SMALL, P * i:P * i + P], k.ident)
                    mm.then_inc(k.multiplied.up(), 1)

                @block.scalar
                def _(act):
                    act.wait_ge(k.vec_step.sem, k.vec_step.at(1))
                    turned = k.psum[:, 0:256].rearrange("p (i c) -> p i c", i=2)
                    act.activation(s.beta[:], turned[:, :, 0:4], ACT.Sigmoid).then_inc(k.act_step.up(), 1)
                    act.activation(s.ea[:], c.rows[:, 8:12], ACT.Exp).then_inc(k.act_step.up(), 1)

                @block.vector
                def _(dve):
                    chain = chained(k, dve)
                    dve.wait_ge(k.multiplied.sem, k.multiplied.at(1))
                    turned = k.psum[:, 0:256].rearrange("p (i c) -> p i c", i=2)
                    bias = c.rows[:, 0:8].unsqueeze(1).broadcast_to([P, 2, 8])
                    chain(dve.tensor_tensor(s.y[:], turned[:, :, 4:12], bias, ALU.add))
                    chain(dve.tensor_scalar(s.y[:, :, 4:8], s.y[:, :, 4:8], -1.0, None, ALU.mult))

            softplus(k, s.y[:], s.tmp[:], s.y[:], -1.0)
            with k.stage() as block:

                @block.vector
                def _(dve):
                    g = s.y[:, :, 0:4]
                    dve.tensor_tensor(g, g, s.ea[:].unsqueeze(1).broadcast_to([P, 2, 4]), ALU.mult).then_inc(k.vec_step.up(), 1)

            small = names(beta=s.beta, g=s.y[:, :, 0:4])
            delta_branch(k, V, s.z, small, c.branches[:, 0])
            mla_branch(k, V, s.z, dram, c.branches[:, 1])
            gla_branch(k, V, s.z, c.gate_up[0:16, :], c.branches[:, 2])
            fox_branch(k, s.z, s.y[:, :, 4:8], c.branches[:, 3])
        with buffers_scope(k, merged=[8, 256], gate=[8, 256], up=[8, 256]) as s:
            for i in range(4):
                gemm(k, dram.w_gate_2[i], 2, 8, 512, rhs(c.h), s.gate[:], 256)
                gemm(k, dram.w_branch_up_2[i], 2, 2, 512, lambda j: c.branches[:, i, j, :], s.up[:], 256)
                with k.stage() as block:

                    @block.scalar
                    def _(act):
                        for j in range(8):
                            ins = act.activation(s.gate[:, j, :], s.gate[:, j, :], ACT.Sigmoid, bias=V.b_gate_2[:, 8 * i + j:8 * i + j + 1])
                        ins.then_inc(k.act_step.up(), 1)

                    @block.vector
                    def _(dve):
                        chain = chained(k, dve)
                        dve.wait_ge(k.act_step.sem, k.act_step.at(1))
                        if i == 0:
                            chain(dve.tensor_tensor(s.merged[:], s.gate[:], s.up[:], ALU.mult))
                        else:
                            chain(dve.tensor_tensor(s.up[:], s.gate[:], s.up[:], ALU.mult))
                            chain(dve.tensor_tensor(s.merged[:], s.merged[:], s.up[:], ALU.add))

            gemm(k, dram.w_out_2, 2, 8, 512, rhs(s.merged), s.up[:], 256)
            channel_norm(k, s.up[:], s.gate[:], 8, 1024, 1e-6, V.norm_mix_post_2)
            add_to(k, x[:], s.gate[:])
        channel_norm(k, x[:], c.h[:], 8, 1024, 1e-6, V.norm_mlp_pre_2)
        with buffers_scope(k, u=[32, 256], y=[8, 256], n=[8, 256]) as s:
            gemm(k, dram.w_mlp_in_2, 8, 8, 512, rhs(c.h), s.u[:], 256)
            with k.stage() as block:

                @block.vector
                def _(dve):
                    dve.scalar_tensor_tensor(s.u[:], s.u[:], 0.0, s.u[:], ALU.max, ALU.mult).then_inc(k.vec_step.up(), 1)

            gemm(k, dram.w_mlp_out_2, 8, 32, P, rhs(s.u), s.y[:], 256)
            channel_norm(k, s.y[:], s.n[:], 8, 1024, 1e-6, V.norm_mlp_post_2)
            add_to(k, x[:], s.n[:])


def add_to(k, x, y):
    with k.stage() as block:

        @block.vector
        def _(dve):
            dve.tensor_tensor(x, x, y, ALU.add).then_inc(k.vec_step.up(), 1)


def layout_second(i):
    i = {n: a[0] for n, a in i.items() if n.endswith("_2")}
    a = {}
    at = np.cumsum([0, 768, 256, 4, 4, 256, 128, 32, 128, 128, 256, 256, 16, 256, 256, 256, 4])
    part = [i["w_in_2"][:, at[n]:at[n + 1]] for n in range(16)]
    qkv, dz, db, da, cq, ckv, kpe, gq, gk, gv, gg, lr, fq, fk, fv, ff = part
    w = np.concatenate([qkv, dz, cq, ckv, np.tile(kpe, (1, 4)), gq, gk, gv, gg, padded_to(lr, P), fq, fk, fv,
                        padded_to(np.concatenate([db, da, ff], axis=1), 3 * P)], axis=1)
    a["w_in_2"] = blocked(w, 512)
    a["vectors2"] = np.concatenate([columns(np.tile(i[n], 2) if n in ("dn_norm_2", "gla_norm_2") else i[n]) for n in VECTORS2], axis=1)
    a["rows2"] = np.ascontiguousarray(np.broadcast_to(np.concatenate([i[n] for n in ROWS2])[None, :], (P, 12)))
    a["gate_up"] = i["gla_w_gate_up_2"]
    q = i["mla_w_q_up_2"].reshape(256, 4, 96)
    a["mla_q_up"] = blocked(padded_to(np.concatenate([q[:, :, :64].reshape(256, 256), q[:, :, 64:].reshape(256, 128)], axis=1), 512), 512)
    kv = i["mla_w_kv_up_2"].reshape(128, 4, 128)
    a["mla_kv_up"] = blocked(np.concatenate([kv[:, :, :64].reshape(128, 256), kv[:, :, 64:].reshape(128, 256)], axis=1), 512)
    a["w_gate_2"] = np.stack([blocked(w, 512) for w in i["w_gate_2"]])
    a["w_branch_up_2"] = np.stack([blocked(w, 512) for w in i["w_branch_up_2"]])
    a["w_out_2"] = blocked(i["w_out_2"], 512)
    a["w_mlp_in_2"] = blocked(i["w_mlp_in_2"], 512)
    a["w_mlp_out_2"] = blocked(i["w_mlp_out_2"], P)
    return a


def constants():
    p, f = np.arange(P)[:, None], np.arange(P)[None, :]
    same, same8 = p // 64 == f // 64, p // 8 == f // 8
    t = np.arange(512)[None, :]
    freq = 1.0 / (10000.0 ** (np.arange(0, 32, 2, dtype=np.float32) / np.float32(32)))
    angle = (np.arange(256, dtype=np.float32)[:, None] * freq[None, :].astype(np.float32)).astype(np.float32)
    angle = np.concatenate([angle, angle], axis=1).T
    turn = np.zeros((P, P))
    for i in range(P):
        turn[i + 16 if i % 32 < 16 else i - 16, i] = -1.0 if i % 32 < 16 else 1.0
    table = {
        "ident": p == f, "ones": p * f >= 0, "blocks64": same,
        "up": same & (p < f), "lo": same & (p > f), "up_incl": same & (p <= f), "lo_incl": same & (p >= f),
        "up8": same8 & (p < f), "lo8": same8 & (p > f), "up_far": same & ~same8 & (p < f), "lo_far": same & ~same8 & (p > f),
        "upto": p <= f, "chunk0": (p < 64) & (f >= 0), "chunk1": (p >= 64) & (f >= 0),
        "causal": np.where(f <= p, 0.0, -1e30), "chunk_causal": np.where(f // 64 <= p // 64, 0.0, -1e30),
        "turn": turn, "halves": np.concatenate([p < 64, p >= 64], axis=1),
        "quarters": np.concatenate([p // 32 == i for i in range(4)], axis=1),
        "segments": np.broadcast_to(t % 64 != 0, (P, 512)), "iota16": np.broadcast_to(np.arange(16)[None, :], (P, 16)),
        "cos": np.tile(np.cos(angle), (4, 1)), "sin": np.tile(np.sin(angle), (4, 1)),
    }
    return {n: np.asarray(a, np.float32) for n, a in table.items()}


class Layout:

    def __init__(self, widths):
        self.at, n = {}, 0
        for name, w in widths.items():
            self.at[name] = (n, n + w)
            n += w
        self.width = n


VECTORS = {"norm1_g": 8, "norm2_g": 8, "shift_mu": 56, "w0": 16, "a0": 16, "k_k": 8, "k_a": 8, "r_k": 8, "lnx_g": 8, "lnx_b": 8,
           "conv_w": 248, "cnorm_g": 8, "cnorm_b": 8, "gate_b": 16, "ada_b": 48}


def load_layer(k, mem, l, dram):
    lay = Layout(VECTORS)
    b = buffers(k, mem, vec=[lay.width], w2=[1024], a2=[1024], g2=[2, 1024])
    load(k, (b.vec[:], dram.vectors[l]), (b.w2[:], dram.w2[l]), (b.a2[:], dram.a2[l]), (b.g2[:], dram.g2[l]))
    L = names(**{name: b.vec[:, a:z] for name, (a, z) in lay.at.items()})
    L.mu = L.shift_mu.rearrange("p (d j) -> p d j", d=2)
    L.w2, L.a2, L.g2 = b.w2, b.a2, b.g2
    return L


def first_block(k, dram, x, xc):
    nc = k.nc
    with ExitStack() as mem:
        mods = buffers(k, mem, mods=[2, 48, 2]).mods
        with buffers_scope(k, c=[8, 2], sig=[8, 2]) as s:
            load(k, (s.c[:], dram.c))
            with k.stage() as block:

                @block.scalar
                def _(act):
                    act.activation(s.sig[:], s.c[:], ACT.Sigmoid).then_inc(k.act_step.up(), 1)

                @block.vector
                def _(dve):
                    dve.wait_ge(k.act_step.sem, k.act_step.at(1))
                    dve.tensor_tensor(s.c[:], s.c[:], s.sig[:], ALU.mult).then_inc(k.vec_step.up(), 1)

            gemm(k, dram.ada_w, 24, 8, 512, lambda j: s.c[:, j, :], mods[:].rearrange("p l j c -> p (l j) c"), 2)
        states = [buffers(k, mem, state=[8, P]).state for d in range(2)]
        for l in range(2):
            with ExitStack() as layer_mem:
                L = load_layer(k, layer_mem, l, dram)
                m = buffers(k, layer_mem, mod=[2, 48])
                with k.stage() as block:

                    @block.vector
                    def _(dve):
                        chain = chained(k, dve)
                        for d in range(2):
                            chain(dve.memset(states[d][:], 0.0))
                        for c in range(2):
                            chain(dve.tensor_tensor(m.mod[:, c, :], mods[:, l, :, c], L.ada_b, ALU.add))
                            for at, gain in ((8, L.norm1_g), (32, L.norm2_g)):
                                part = m.mod[:, c, at:at + 8]
                                chain(dve.scalar_tensor_tensor(part, part, 1.0, gain, ALU.add, ALU.mult))


                def modulation(c):
                    shift1, scale1, gate1, shift2, scale2, gate2 = (m.mod[:, c, 8 * i:8 * i + 8] for i in range(6))
                    return names(shift1=shift1, scale1=scale1, gate1=gate1, shift2=shift2, scale2=scale2, gate2=gate2)

                last = l == 1
                token_mixer(k, L, l, dram, xc[:], modulation(1), states, [(15, 0)] + [(r, r - 15) for r in range(31) if r != 15],
                            not last)
                k.dump(f"xc_mix{l}", xc[:])
                token_mixer(k, L, l, dram, x[:], modulation(0), states, [(15, 0)] + [(r, 64 * (r - 15)) for r in range(12, 19) if r != 15],
                            True)
                k.dump(f"x_mix{l}", x[:])
                mx, mc = modulation(0), modulation(1)
                peer(k, l, dram, x[:], mx)
                k.dump(f"x_peer{l}", x[:])
                if not last:
                    peer(k, l, dram, xc[:], mc)


def program(nc, dram, dump=None):
    with ExitStack() as ctx:
        k = Core(nc, ctx)
        k.dump = dump(k) if dump else lambda name, ap: None
        lay = Layout({n: a.shape[1] for n, a in constants().items()})
        table = ctx.enter_context(nc.sbuf_tensor("constants", [P, lay.width], F32))
        (k.ident, k.ones, k.blocks64, k.up, k.lo, k.up_incl, k.lo_incl, k.up8, k.lo8, k.up_far, k.lo_far, k.upto, k.chunk0, k.chunk1,
         k.causal, k.chunk_causal, k.turn, k.halves, k.quarters, k.segments, k.iota16, k.cos, k.sin) = (
            table[:, a:z] for a, z in lay.at.values())
        k.half_mask = [k.halves[:, i:i + 1] for i in range(2)]
        k.quarter_mask = [k.quarters[:, i:i + 1] for i in range(4)]
        x = ctx.enter_context(nc.sbuf_tensor("x_tokens", [P, 8, 256], F32))
        with nc.sbuf_tensor("context_tokens", [P, 8, 256], F32) as xc:
            load(k, (table[:], dram.constants), (x[:], dram.x), (xc[:], dram.ctx))
            first_block(k, dram, x, xc)
        channel_norm(k, x[:], x[:], 8, 1024, 1e-6, k_final(k, ctx, dram))
        k.dump("x_first", x[:])
        second_block(k, dram, x)
        with buffers_scope(k, rows=[2, 1024]) as s, k.stage() as block:

            @block.tensor
            def _(pe):
                for i in range(2):
                    for j in range(8):
                        mm = pe.transpose(k.psum[:, 1024 * i + P * j:1024 * i + P * j + P], x[:, j, P * i:P * i + P], k.ident)
                mm.then_inc(k.multiplied.up(), 1)

            @block.scalar
            def _(act):
                act.wait_ge(k.multiplied.sem, k.multiplied.at(1))
                act.activation(s.rows[:], k.psum[:, 0:2048].rearrange("p (i c) -> p i c", i=2), ACT.Copy).then_inc(k.act_step.up(), 1)

            @block.sync
            def _(sp):
                sp.wait_ge(k.act_step.sem, k.act_step.at(1))
                sp.dma_start(dram.out.rearrange("b (i p) c -> p (b i) c", p=P), s.rows[:]).then_inc(k.stored.up(16), 16)
                sp.wait_ge(k.stored.sem, k.stored.count)


def k_final(k, ctx, dram):
    g = ctx.enter_context(k.nc.sbuf_tensor("final_g", [P, 8], F32))
    load(k, (g[:], dram.final_g))
    return g[:]




def columns(v):
    v = np.asarray(v)
    n = -(-v.shape[-1] // P) * P
    out = np.zeros((*v.shape[:-1], n), v.dtype)
    out[..., :v.shape[-1]] = v
    return np.ascontiguousarray(out.reshape(-1, P).T)


def blocked(w, cols):
    w = np.asarray(w)
    k, n = w.shape
    kt = -(-k // P)
    padded = np.zeros((kt * P, -(-n // cols) * cols), w.dtype)
    padded[:k, :n] = w
    return np.ascontiguousarray(padded.reshape(kt, P, -1, cols).transpose(2, 1, 0, 3).reshape(-1, P, kt * cols))


def padded_to(w, n):
    out = np.zeros((w.shape[0], n), w.dtype)
    out[:, :w.shape[1]] = w
    return out


def layout(i):
    i = {n: np.asarray(a) for n, a in i.items()}
    a = {}
    a["x"] = np.ascontiguousarray(i["x"][0].T.reshape(8, P, 256).transpose(1, 0, 2))
    a["ctx"] = np.ascontiguousarray(i["ctx"][0].T.reshape(8, P, 256).transpose(1, 0, 2))
    a["c"] = np.ascontiguousarray(np.stack([columns(i["c"][0]), columns(i["c_ctx"])], axis=2))
    a["constants"] = np.concatenate(list(constants().values()), axis=1)
    a["final_g"] = columns(i["final_g"])
    a["vectors"] = np.stack([np.concatenate([columns(i[n][l].reshape(-1) if n == "r_k" else i[n][l]) for n in VECTORS], axis=1) for l in range(2)])
    a["ada_w"] = np.concatenate([blocked(i["ada_w"][l], 512) for l in range(2)])
    a["w_in"] = np.stack([np.concatenate([blocked(i["w_in"][l][:, :3488], 512), blocked(i["w_in"][l][:, 3488:], 512)]) for l in range(2)])
    a["w2"] = np.ascontiguousarray(i["w2"].reshape(2, P, 1024))
    a["a2"] = np.ascontiguousarray(i["a2"].reshape(2, P, 1024))
    g2 = np.zeros((2, 256, 1024), np.float32)
    g2[:, :160] = i["g2"]
    a["g2"] = np.ascontiguousarray(g2.reshape(2, 2, P, 1024).transpose(0, 2, 1, 3))
    for n in ("w_oA", "w_oB", "w_out", "w_q"):
        a[n] = np.stack([blocked(i[n][l], 512) for l in range(2)])
    a["sub_keys"] = np.ascontiguousarray(i["sub_keys"].transpose(0, 4, 1, 2, 3).reshape(2, P, 16, P))
    a["peer_u"] = i["peer_u"].reshape(-1, 1024)
    a["peer_v"] = i["peer_v"].reshape(-1, 1024)
    a.update(layout_second(i))
    return a


def kernel(**inputs):
    import concourse.bacc as bacc
    from concourse.bass_utils import run_bass_kernel_spmd

    nc = bacc.Bacc("TRN2", target_bir_lowering=False, num_devices=1)
    arrays = {f"in_{n}": a for n, a in layout(inputs).items()}
    dram = names(**{n[3:]: nc.dram_tensor(n, a.shape, mybir.dt.from_np(a.dtype), kind="ExternalInput").ap()
                              for n, a in arrays.items()})
    dram.out = nc.dram_tensor("out_tokens", (1, 256, 1024), F32, kind="ExternalOutput").ap()
    program(nc, dram)
    return run_bass_kernel_spmd(nc, [arrays], core_ids=[0]).results[0]["out_tokens"]
```

```python
import math
from contextlib import ExitStack, contextmanager

import numpy as np

import concourse.bass as bass
from concourse import mybir

F32 = mybir.dt.float32
U32 = mybir.dt.uint32
ACT = mybir.ActivationFunctionType
ALU = mybir.AluOpType
AXX = mybir.AxisListType.X
P = 128


def names(**values):
    return type("Names", (), values)()


class Signal:

    def __init__(self, sem):
        self.sem, self.count, self.mark = sem, 0, 0

    def up(self, by=1):
        self.count += by
        return self.sem

    def at(self, n):
        return self.mark + n


class Core:

    def __init__(self, nc, ctx):
        self.nc, self.ctx = nc, ctx
        self.signals, self.made = [], 0
        self.fetched = False
        self.psum = ctx.enter_context(nc.psum_tensor("psum", [P, 4096], F32))
        self.weights = [self.counter(f"weights_loaded{i}") for i in range(SLOTS_W)]
        self.multiplied = self.counter("multiplied")
        self.evacuated = self.counter("evacuated")
        self.vec_step = self.counter("vec_step")
        self.act_step = self.counter("act_step")
        self.pool_step = self.counter("pool_step")
        self.staged = self.counter("numbers_staged")
        self.weights_staged = self.counter("weights_staged")
        self.slot_free = self.counter("slot_free")
        self.row_used = self.counter("row_used")
        self.dots_kept = self.counter("dots_kept")
        self.weighted = self.counter("weighted")
        self.gathered = [self.counter(f"row_gathered{j}") for j in range(8)]
        self.loaded = self.counter("loaded")
        self.stored = self.counter("stored")

    def sbuf(self, name, shape, dtype=F32):
        self.made += 1
        return self.nc.sbuf_tensor(f"{name}_{self.made}", [P, *shape], dtype)

    def counter(self, name):
        s = Signal(self.ctx.enter_context(self.nc.semaphore(name)))
        self.signals.append(s)
        return s

    @contextmanager
    def stage(self):
        for s in self.signals:
            s.mark = s.count
        with self.nc.Block(no_gpsimd_drain=True) as block:
            yield block

    def bank(self, i, n=512):
        return self.psum[:, 512 * i:512 * i + n]


SLOTS_W = 4


def fetch(k, sp, w, n, ring):
    slot = n % SLOTS_W
    sp.dma_start(ring[:, slot, 0:w.kt * P], w.ap[n]).then_inc(k.weights[slot].sem, 16)


def weight(ap, kt):
    return names(ap=ap, blocks=ap.shape[0], kt=kt)


def gemm(k, w, rhs, dst, then=None, own_ring=False, tokens=256):
    rounds, extra = divmod(w.blocks, SLOTS_W)
    assert extra == 0
    with ExitStack() as mem:
        ring = mem.enter_context(k.sbuf("weight_ring", [SLOTS_W, w.kt * P])) if own_ring else k.ring
        fetched = not own_ring and k.fetched
        wl, mu, ev = k.weights, k.multiplied, k.evacuated
        with k.stage() as block:
            landed = [s.at(0) if fetched else s.at(16) for s in wl]

            @block.sync
            def _(sp):
                if not fetched:
                    for n in range(SLOTS_W):
                        fetch(k, sp, w, n, ring)
                        wl[n].up(16)
                if rounds > 1:
                    with sp.Fori(1, rounds) as i:
                        for slot in range(SLOTS_W):
                            sp.wait_ge(mu.sem, i * SLOTS_W + (mu.at(slot + 1) - SLOTS_W))
                            sp.dma_start(ring[:, slot, 0:w.kt * P], w.ap[i * SLOTS_W + slot]).then_inc(wl[slot].sem, 16)
                for slot in range(SLOTS_W):
                    wl[slot].up(16 * (rounds - 1))
                if then is not None:
                    for slot in range(SLOTS_W):
                        sp.wait_ge(mu.sem, mu.at((rounds - 1) * SLOTS_W + slot + 1))
                        fetch(k, sp, then, slot, ring)
                        wl[slot].up(16)

            @block.tensor
            def _(pe):
                def multiply(i, slot, first):
                    pe.wait_ge(wl[slot].sem, i * 16 + landed[slot])
                    if not first:
                        pe.wait_ge(ev.sem, i * SLOTS_W + (ev.at(slot + 1) - SLOTS_W))
                    for j in range(w.kt):
                        mm = pe.matmul(k.bank(slot, tokens), ring[:, slot, j * P:j * P + P], rhs(j), start=(j == 0), stop=(j == w.kt - 1))
                    mm.then_inc(mu.sem, 1)

                for slot in range(SLOTS_W):
                    multiply(0, slot, True)
                if rounds > 1:
                    with pe.Fori(1, rounds) as i:
                        for slot in range(SLOTS_W):
                            multiply(i, slot, False)

            @block.scalar
            def _(act):
                with act.Fori(0, rounds) as i:
                    for slot in range(SLOTS_W):
                        act.wait_ge(mu.sem, i * SLOTS_W + mu.at(slot + 1))
                        act.activation(dst[:, bass.ds(i * SLOTS_W + slot, 1), :], k.bank(slot, tokens).unsqueeze(1), ACT.Copy
                                       ).then_inc(ev.sem, 1)

            mu.up(w.blocks)
            ev.up(w.blocks)
            if not own_ring:
                k.fetched = then is not None


def modulation_rows(k, w, c, out):
    blocks, depth = w.shape[0], 4
    with k.sbuf("ada_ring", [depth, 4096]) as ring, k.sbuf("ada_rows", [blocks * 512]) as rows:
        mu, ev, wl = k.multiplied, k.evacuated, k.weights
        rounds = blocks // depth
        with k.stage() as block:

            @block.sync
            def _(sp):
                for slot in range(depth):
                    sp.dma_start(ring[:, slot, :], w[slot]).then_inc(wl[slot].sem, 16)
                with sp.Fori(1, rounds) as i:
                    for slot in range(depth):
                        sp.wait_ge(mu.sem, i * depth + (mu.at(slot + 1) - depth))
                        sp.dma_start(ring[:, slot, :], w[i * depth + slot]).then_inc(wl[slot].sem, 16)

            @block.tensor
            def _(pe):
                def multiply(i, slot, first):
                    pe.wait_ge(wl[slot].sem, i * 16 + wl[slot].at(16))
                    if not first:
                        pe.wait_ge(ev.sem, i * depth + (ev.at(slot + 1) - depth))
                    for j in range(8):
                        mm = pe.matmul(k.bank(slot)[0:2, :], c[:, j, :], ring[:, slot, 512 * j:512 * j + 512], start=(j == 0), stop=(j == 7))
                    mm.then_inc(mu.sem, 1)

                for slot in range(depth):
                    multiply(0, slot, True)
                with pe.Fori(1, rounds) as i:
                    for slot in range(depth):
                        multiply(i, slot, False)

            @block.scalar
            def _(act):
                with act.Fori(0, rounds) as i:
                    for slot in range(depth):
                        act.wait_ge(mu.sem, i * depth + mu.at(slot + 1))
                        act.activation(rows[0:2, bass.ds((i * depth + slot) * 512, 512)], k.bank(slot)[0:2, :], ACT.Copy).then_inc(ev.sem, 1)

            for slot in range(depth):
                wl[slot].up(16 * rounds)
            mu.up(blocks)
            ev.up(blocks)

        with k.stage() as block:

            @block.tensor
            def _(pe):
                for n in range(blocks * 4):
                    mm = pe.transpose(k.bank(0)[:, 2 * n:2 * n + 2], rows[0:2, P * n:P * n + P], k.ident[0:2, 0:2])
                mm.then_inc(mu.up(), 1)

            @block.vector
            def _(dve):
                dve.wait_ge(mu.sem, mu.at(1))
                dve.tensor_copy(out, k.bank(0, blocks * 8).rearrange("p (n c) -> p n c", c=2)).then_inc(k.vec_step.up(), 1)


def chained(k, dve):
    step = k.vec_step

    def chain(instruction):
        instruction.then_inc(step.up(), 1)
        dve.wait_ge(step.sem, step.count)

    return chain


def over_tokens(column, tiles, tokens):
    return column.unsqueeze(2).broadcast_to([P, tiles, tokens])


def over_tiles(row, tiles, tokens):
    return row.unsqueeze(1).broadcast_to([P, tiles, tokens])


def load(k, *pairs):
    with k.stage() as block:

        @block.sync
        def _(sp):
            for dst, src in pairs:
                sp.dma_start(dst, src).then_inc(k.loaded.up(16), 16)
            sp.wait_ge(k.loaded.sem, k.loaded.count)


def channel_norm(k, src, dst, tiles, width, eps, mul=None, add=None, center=False, tokens=256):
    nc = k.nc
    with (
        k.sbuf("squares", [tiles, tokens]) as squares,
        k.sbuf("row", [tokens]) as row,
        k.stage() as block,
    ):
        total, mean = k.bank(0, tokens), k.bank(1, tokens)
        marks = {}

        @block.vector
        def _(dve):
            chain = chained(k, dve)
            base = src
            if center:
                dve.wait_ge(k.multiplied.sem, k.multiplied.at(1))
                chain(dve.tensor_scalar(row[:], mean, 1.0 / width, None, ALU.mult))
                chain(dve.tensor_tensor(dst, src, over_tiles(row[:], tiles, tokens), ALU.subtract))
                base = dst
            marks["centered"] = k.vec_step.count
            n = 2 if center else 1
            dve.wait_ge(k.multiplied.sem, k.multiplied.at(n))
            chain(dve.tensor_scalar(row[:], total, 1.0 / width, eps, ALU.mult, ALU.add))
            marks["variance"] = k.vec_step.count
            dve.wait_ge(k.act_step.sem, k.act_step.at(2))
            chain(dve.reciprocal(row[:], row[:]))
            chain(dve.tensor_tensor(dst, base, over_tiles(row[:], tiles, tokens), ALU.mult))
            if mul is not None:
                chain(dve.tensor_tensor(dst, dst, over_tokens(mul, tiles, tokens), ALU.mult))
            if add is not None:
                chain(dve.tensor_tensor(dst, dst, over_tokens(add, tiles, tokens), ALU.add))

        @block.scalar
        def _(act):
            if center:
                act.wait_ge(k.vec_step.sem, marks["centered"])
            act.activation(squares[:], dst if center else src, ACT.Square).then_inc(k.act_step.up(), 1)
            act.wait_ge(k.vec_step.sem, marks["variance"])
            act.activation(row[:], row[:], ACT.Sqrt).then_inc(k.act_step.up(), 1)

        @block.tensor
        def _(pe):
            if center:
                for j in range(tiles):
                    mm = pe.matmul(mean, k.ones, src[:, j, :], start=(j == 0), stop=(j == tiles - 1))
                mm.then_inc(k.multiplied.up(), 1)
            pe.wait_ge(k.act_step.sem, k.act_step.at(1))
            for j in range(tiles):
                mm = pe.matmul(total, k.ones, squares[:, j, :], start=(j == 0), stop=(j == tiles - 1))
            mm.then_inc(k.multiplied.up(), 1)


def invert_unit_lower(k, groups, Ld, LdT, NT, temps, TT):
    E1, E2, E3, X = temps
    ident = k.ident


    def grp(t, g):
        return t[:, g]

    steps = [
        (LdT, Ld, None, E1),
        (Ld, LdT, None, E2),
        (E1, E2, None, E3),
        (E2, X, X, X),
        (E3, X, X, X),
        (X, None, None, TT),
        (NT, X, None, E1),
        (X, NT, None, E2),
        (E2, E1, None, E3),
        (E1, E2, None, Ld),
        (Ld, E3, None, LdT),
        (E1, TT, TT, TT),
        (E3, TT, TT, TT),
        (LdT, TT, TT, TT),
    ]

    def product(q, g):
        return k.bank((groups * q + g) % 4).rearrange("p (h c) -> p h c", h=4)

    copied = {}
    with k.stage() as block:

        @block.vector
        def _(dve):
            for g in range(groups):
                dve.tensor_tensor(grp(X, g), grp(Ld, g), k.ident.unsqueeze(1).broadcast_to([P, 4, P]),
                                  ALU.add).then_inc(k.vec_step.up(), 1)
                copied[-1, g] = k.vec_step.sem, k.vec_step.count
            for q, (_, _, added, out) in enumerate(steps):
                for g in range(groups):
                    if g and added is None:
                        continue
                    dve.wait_ge(k.multiplied.sem, k.multiplied.at(groups * q + g + 1))
                    if added is None:
                        ins = dve.tensor_copy(grp(out, g), product(q, g))
                    else:
                        ins = dve.tensor_tensor(grp(out, g), product(q, g), grp(added, g), ALU.add)
                    ins.then_inc(k.vec_step.up(), 1)
                    copied[q, g] = k.vec_step.sem, k.vec_step.count

        @block.scalar
        def _(act):
            for q, (_, _, added, out) in enumerate(steps):
                if groups > 1 and added is None:
                    act.wait_ge(k.multiplied.sem, k.multiplied.at(groups * q + 2))
                    act.activation(grp(out, 1), product(q, 1), ACT.Copy).then_inc(k.act_step.up(), 1)
                    copied[q, 1] = k.act_step.sem, k.act_step.count

        @block.tensor
        def _(pe):
            for q, (left, right, _, _) in enumerate(steps):
                for g in range(groups):
                    sem, value = copied[q - 1, g]
                    pe.wait_ge(sem, value)
                    for h in range(4):
                        out = product(q, g)[:, h, :]
                        if right is None:
                            mm = pe.transpose(out, grp(left, g)[:, h, :], ident)
                        else:
                            mm = pe.matmul(out, grp(left, g)[:, h, :], grp(right, g)[:, h, :], start=True, stop=True)
                    mm.then_inc(k.multiplied.up(), 1)


def rwkv_unit(k, b, L, quarter, sweep, emit):
    z = b.z
    ways = [i ^ sweep for i in range(2)]
    kts = slice(2 * quarter, 2 * quarter + 2)
    C = math.exp(-0.5)
    masks = [(k.up, k.up_incl, k.up8, k.up_far, k.lo8), (k.lo, k.lo_incl, k.lo8, k.lo_far, k.up8)]

    def masked(m, n):
        return m.unsqueeze(1).broadcast_to([P, n, P])

    def tiles(t, first=0):
        return t[:, first + 2 * quarter:first + 2 * quarter + 2, :]

    def tokens(i):
        return slice(i * P, (i + 1) * P)

    kz, vz, kk = tiles(z, 8), tiles(z, 16), tiles(b.kk)
    marks = {}
    with k.stage() as block:

        @block.vector
        def _(dve):
            chain = chained(k, dve)
            dve.wait_ge(k.act_step.sem, k.act_step.at(1))
            chain(dve.tensor_tensor_scan(b.cum.rearrange("p j t -> p (j t)"), k.segments, b.sg.rearrange("p j t -> p (j t)"),
                                         0.0, ALU.mult, ALU.add))
            chain(dve.tensor_copy(b.tot[:], b.cum[:, :, 63::64]))
            for i in range(2):
                if ways[i] == 0:
                    chain(dve.tensor_tensor(b.excl[:, :, tokens(i)], b.cum[:, :, tokens(i)], b.sg[:, :, tokens(i)], ALU.subtract))
                else:
                    by_chunk = [t[:, :, tokens(i)].rearrange("p j (c t) -> p j c t", c=2) for t in (b.excl, b.cum)]
                    chain(dve.tensor_tensor(by_chunk[0], b.tot[:, :, 2 * i:2 * i + 2].unsqueeze(3).broadcast_to([P, 2, 2, 64]), by_chunk[1], ALU.subtract))
                    chain(dve.tensor_tensor(b.cum[:, :, tokens(i)], b.excl[:, :, tokens(i)], b.sg[:, :, tokens(i)], ALU.add))
            marks["sums"] = k.vec_step.count
            ka = L.k_a[:, kts].unsqueeze(2).broadcast_to([P, 2, 256])
            chain(dve.scalar_tensor_tensor(b.kd, b.a, 1.0, ka, ALU.subtract, ALU.mult))
            chain(dve.scalar_tensor_tensor(b.kd, b.kd, 1.0, kz, ALU.add, ALU.mult))
            chain(dve.scalar_tensor_tensor(b.a, b.a, -1.0, kk, ALU.mult, ALU.mult))
            if emit:
                ks = tiles(b.kdsum)
                if sweep == 0:
                    chain(dve.tensor_copy(ks, b.kd))
                else:
                    chain(dve.tensor_tensor(ks, ks, b.kd, ALU.add))
            dve.wait_ge(k.act_step.sem, k.act_step.at(3))
            chain(dve.tensor_tensor(b.kh[:], b.kd, b.eN, ALU.mult))
            marks["kh"] = k.vec_step.count
            chain(dve.tensor_tensor(b.nb[:], b.a, b.eN, ALU.mult))
            marks["nb"] = k.vec_step.count
            chain(dve.tensor_tensor(b.kt[:], kk, b.eX, ALU.mult))
            marks["kt"] = k.vec_step.count
            if emit:
                chain(dve.tensor_tensor(b.rt[:], tiles(z), b.eP, ALU.mult))
                marks["rt"] = k.vec_step.count

        @block.scalar
        def _(act):
            act.wait_ge(k.multiplied.sem, k.multiplied.at(1))
            for i in range(2):
                for j in range(2):
                    at, col = (2 * i + j) * P, 8 * ways[i] + 2 * quarter + j
                    act.activation(b.sg[:, j, tokens(i)], k.bank(5 * i)[:, at:at + P], ACT.Sigmoid, bias=L.w0[:, col:col + 1])
                    last = act.activation(b.a[:, j, tokens(i)], k.bank(5 * i + 1)[:, at:at + P], ACT.Sigmoid, bias=L.a0[:, col:col + 1])
            last.then_inc(k.act_step.up(), 1)
            act.wait_ge(k.multiplied.sem, k.multiplied.at(2))
            act.activation(b.V[:], k.bank(2).rearrange("p (i c) -> p i c", i=2), ACT.Copy).then_inc(k.act_step.up(), 1)
            act.wait_ge(k.vec_step.sem, marks["sums"])
            act.activation(b.eN, b.cum, ACT.Exp, scale=C)
            act.activation(b.eX, b.excl, ACT.Exp, scale=-C)
            if emit:
                act.activation(b.eP, b.cum, ACT.Exp, scale=-C)
            act.activation(b.pc[:], b.tot[:], ACT.Exp, scale=-C).then_inc(k.act_step.up(), 1)
            act.wait_ge(k.multiplied.sem, k.multiplied.at(3))
            act.activation(b.khT[:], k.bank(3).rearrange("p (i c) -> p i c", i=2), ACT.Copy).then_inc(k.act_step.up(), 1)
            act.wait_ge(k.multiplied.sem, k.multiplied.at(4))
            act.activation(b.nbT[:], k.bank(4).rearrange("p (i c) -> p i c", i=2), ACT.Copy).then_inc(k.act_step.up(), 1)
            for n, (name, t) in enumerate((("kt", b.kt), ("rt", b.rt)) if emit else (("kt", b.kt),)):
                act.wait_ge(k.vec_step.sem, marks[name])
                for hh in range(2):
                    act.activation(b.rhs4[:, :, :, 2 * n + hh, :], t[:].rearrange("p j (i t) -> p j i t", i=2), ACT.Copy, scale=k.half_mask[hh]).then_inc(k.act_step.up(), 1)

        @block.tensor
        def _(pe):
            for i in range(2):
                rows = slice(64 * ways[i], 64 * ways[i] + 64)
                for j in range(2):
                    at, c = (2 * i + j) * P, slice((2 * quarter + j) * P, (2 * quarter + j + 1) * P)
                    pe.matmul(k.bank(5 * i)[:, at:at + P], L.w2[rows, c], z[rows, 24, tokens(i)], start=True, stop=True)
                    mm = pe.matmul(k.bank(5 * i + 1)[:, at:at + P], L.a2[rows, c], z[rows, 25, tokens(i)], start=True, stop=True)
            mm.then_inc(k.multiplied.up(), 1)
            for i in range(2):
                for j in range(2):
                    at = (2 * i + j) * P
                    mm = pe.transpose(k.bank(2)[:, at:at + P], vz[:, j, tokens(i)], k.ident)
            mm.then_inc(k.multiplied.up(), 1)
            for bank, name, t in ((3, "kh", b.kh), (4, "nb", b.nb)):
                pe.wait_ge(k.vec_step.sem, marks[name])
                for i in range(2):
                    for j in range(2):
                        at = (2 * i + j) * P
                        mm = pe.transpose(k.bank(bank)[:, at:at + P], t[:, j, tokens(i)], k.ident)
                mm.then_inc(k.multiplied.up(), 1)

    width = 512 if emit else 256
    with k.stage() as block:

        @block.tensor
        def _(pe):
            for n in range(4):
                three = [k.bank(3 * (n % 2) + m) for m in range(3)]
                if n >= 2:
                    pe.wait_ge(k.vec_step.sem, k.vec_step.at(n - 1))
                i, j = n // 2, n % 2
                kh, nb = b.kh[:, j, tokens(i)], b.nb[:, j, tokens(i)]
                rhs = b.rhs4[:, j, i].rearrange("p a t -> p (a t)")[:, 0:width]
                pe.matmul(three[0][:, 0:width], kh, rhs, start=True, stop=True)
                pe.matmul(three[1][:, 0:width], nb, rhs, start=True, stop=True)
                for hh in range(2):
                    mm = pe.matmul(three[2][:, hh * P:(hh + 1) * P], b.rhs4[:, j, i, hh, :], nb, start=True, stop=True)
                mm.then_inc(k.multiplied.up(), 1)

        @block.vector
        def _(dve):
            for n in range(4):
                dve.wait_ge(k.multiplied.sem, k.multiplied.at(n + 1))
                i, hs = n // 2, slice(2 * (n % 2), 2 * (n % 2) + 2)
                strict, incl, near, far, back = masks[ways[i]]
                three = [k.bank(3 * (n % 2) + m).rearrange("p (h t) -> p h t", h=4) for m in range(3)]
                dve.tensor_tensor(b.MT[:, i, hs, :], three[0][:, 0:2, :], masked(strict, 2), ALU.mult)
                dve.tensor_tensor(b.LdT[:, i, hs, :], three[1][:, 0:2, :], masked(near, 2), ALU.mult)
                dve.tensor_tensor(b.NT[:, i, hs, :], three[1][:, 0:2, :], masked(far, 2), ALU.mult)
                if emit:
                    dve.tensor_tensor(b.ArT[:, i, hs, :], three[0][:, 2:4, :], masked(incl, 2), ALU.mult)
                    dve.tensor_tensor(b.AbT[:, i, hs, :], three[1][:, 2:4, :], masked(incl, 2), ALU.mult)
                dve.tensor_tensor(b.Ld[:, i, hs, :], three[2][:, 0:2, :], masked(back, 2), ALU.mult).then_inc(k.vec_step.up(), 1)

    invert_unit_lower(k, 2, b.Ld, b.LdT, b.NT, (b.E1, b.E2, b.E3, b.X), b.TT)

    states = [b.states[ways[i]][:, kts, :] for i in range(2)]
    chunk = [[0, 1] if ways[i] == 0 else [1, 0] for i in range(2)]
    bR, bU, bS, bY = ([k.bank(4 * i + n, 256) for i in range(2)] for n in range(4))
    R, U = b.R, b.U

    def rows(n, i):
        return slice(64 * chunk[i][n], 64 * chunk[i][n] + 64)

    def summed(n, i):
        return k.multiplied.at(6 * n + i + 1)

    def solved(n, i):
        return k.multiplied.at(6 * n + 2 + i + 1)

    def stated(n, i):
        return k.multiplied.at(6 * n + 4 + i + 1)

    with k.stage() as block:

        @block.vector
        def _(dve):
            for n in range(2):
                for i in range(2):
                    if emit:
                        dve.wait_ge(k.multiplied.sem, summed(n, i))
                        y = b.Y[rows(n, i), i, 256 * quarter:256 * quarter + 256]
                        if sweep == 0:
                            ins = dve.tensor_copy(y, bY[i][rows(n, i), :])
                        else:
                            ins = dve.tensor_tensor(y, y, bY[i][rows(n, i), :], ALU.add)
                        ins.then_inc(k.vec_step.up(), 1)
                        marks["y", n, i] = k.vec_step.count
                for i in range(2):
                    dve.wait_ge(k.multiplied.sem, stated(n, i))
                    for j in range(2):
                        c = chunk[i][n]
                        dve.scalar_tensor_tensor(states[i][:, j, :], bS[i][:, j * P:(j + 1) * P], b.pc[:, j, 2 * i + c:2 * i + c + 1], k.blocks64,
                                                 ALU.mult, ALU.mult).then_inc(k.vec_step.up(), 1)
                    marks["S", n, i] = k.vec_step.count
            if emit:
                for i in range(2):
                    dve.wait_ge(k.multiplied.sem, k.multiplied.at(12 + i + 1))
                    dve.wait_ge(k.vec_step.sem, marks["y", 1, i])
                    y = b.Y[:, i, 256 * quarter:256 * quarter + 256]
                    dve.tensor_tensor(y, y, bY[i], ALU.add).then_inc(k.vec_step.up(), 1)

        @block.scalar
        def _(act):
            for n in range(2):
                for i in range(2):
                    act.wait_ge(k.multiplied.sem, summed(n, i))
                    act.activation(R[:, i, :], bR[i], ACT.Copy).then_inc(k.act_step.up(), 1)
                    marks["R", n, i] = k.act_step.count
                for i in range(2):
                    act.wait_ge(k.multiplied.sem, solved(n, i))
                    act.activation(U[rows(n, i), i, :], bU[i][rows(n, i), :], ACT.Copy).then_inc(k.act_step.up(), 1)
                    marks["U", n, i] = k.act_step.count

        @block.tensor
        def _(pe):
            for n in range(2):
                for i in range(2):
                    if n:
                        pe.wait_ge(k.vec_step.sem, marks["S", 0, i])
                    for j in range(2):
                        js = slice(j * P, (j + 1) * P)
                        if emit:
                            pe.matmul(bY[i][:, js], b.rt[:, j, tokens(i)], states[i][:, j, :], start=True, stop=True)
                        pe.matmul(bR[i][:, js], b.kt[:, j, tokens(i)], states[i][:, j, :], start=True, stop=False, skip_group_check=True)
                        for hh in range(2):
                            h = 2 * j + hh
                            mm = pe.matmul(bR[i][:, 64 * h:64 * h + 64], b.MT[:, i, h, :], b.V[:, i, 64 * h:64 * h + 64], start=False,
                                           stop=True, skip_group_check=True)
                    mm.then_inc(k.multiplied.up(), 1)
                for i in range(2):
                    pe.matmul(bS[i], k.ident, states[i].rearrange("p j c -> p (j c)"), start=True, stop=False, skip_group_check=True)
                    for j in range(2):
                        js = slice(j * P, (j + 1) * P)
                        pe.matmul(bS[i][:, js], b.khT[rows(n, i), i, js], b.V[rows(n, i), i, js], start=False, stop=False, skip_group_check=True)
                for i in range(2):
                    pe.wait_ge(k.act_step.sem, marks["R", n, i])
                    for h in range(4):
                        hs = slice(64 * h, 64 * h + 64)
                        mm = pe.matmul(bU[i][:, hs], b.TT[:, i, h, :], R[:, i, hs], start=True, stop=True)
                    mm.then_inc(k.multiplied.up(), 1)
                for i in range(2):
                    pe.wait_ge(k.act_step.sem, marks["U", n, i])
                    for j in range(2):
                        js = slice(j * P, (j + 1) * P)
                        mm = pe.matmul(bS[i][:, js], b.nbT[rows(n, i), i, js], U[rows(n, i), i, js], start=False, stop=True, skip_group_check=True)
                    mm.then_inc(k.multiplied.up(), 1)
            if emit:
                for i in range(2):
                    pe.wait_ge(k.vec_step.sem, marks["y", 1, i])
                    for h in range(4):
                        hs = slice(64 * h, 64 * h + 64)
                        pe.matmul(bY[i][:, hs], b.ArT[:, i, h, :], b.V[:, i, hs], start=True, stop=False)
                        mm = pe.matmul(bY[i][:, hs], b.AbT[:, i, h, :], U[:, i, hs], start=False, stop=True)
                    mm.then_inc(k.multiplied.up(), 1)


def buffers(k, mem, **shapes):
    return names(**{name: mem.enter_context(k.sbuf(name, shape)) for name, shape in shapes.items()})


def rwkv(k, L, z, states, emit, o=None, spare=None):
    nc = k.nc
    with ExitStack() as mem:
        b = buffers(k, mem, kk=[8, 256])
        t0 = 0 if emit else 8
        with buffers_scope(k, before=[14, 256], after=[14, 256]) as s, k.stage() as block:

            @block.vector
            def _(dve):
                chain = chained(k, dve)
                for a in range(t0, 28, 14 if emit else 10):
                    n = 14 if emit else 10
                    zz = z[:, a:a + n, :]
                    bef, aft = s.before[:, 0:n, :], s.after[:, 0:n, :]
                    chain(dve.tensor_tensor(bef[:, :, 1:256], zz[:, :, 0:255], zz[:, :, 1:256], ALU.subtract))
                    chain(dve.tensor_scalar(bef[:, :, 0:1], zz[:, :, 0:1], -1.0, None, ALU.mult))
                    chain(dve.tensor_tensor(aft[:, :, 0:255], zz[:, :, 1:256], zz[:, :, 0:255], ALU.subtract))
                    chain(dve.tensor_scalar(aft[:, :, 255:256], zz[:, :, 255:256], -1.0, None, ALU.mult))
                    chain(dve.tensor_tensor(bef, bef, over_tokens(L.mu[:, 0, a:a + n], n, 256), ALU.mult))
                    chain(dve.tensor_tensor(aft, aft, over_tokens(L.mu[:, 1, a:a + n], n, 256), ALU.mult))
                    chain(dve.tensor_tensor(zz, zz, bef, ALU.add))
                    chain(dve.tensor_tensor(zz, zz, aft, ALU.add))

        kz = z[:, 8:16, :]
        with buffers_scope(k, squares=[8, 256], norm=[8, 256]) as s, k.stage() as block:

            @block.vector
            def _(dve):
                chain = chained(k, dve)
                chain(dve.tensor_tensor(b.kk[:], kz, over_tokens(L.k_k, 8, 256), ALU.mult))
                dve.wait_ge(k.act_step.sem, k.act_step.at(3 if emit else 2))
                chain(dve.tensor_scalar(s.norm[:], s.norm[:], 1e-12, None, ALU.max))
                chain(dve.reciprocal(s.norm[:], s.norm[:]))
                chain(dve.tensor_tensor(b.kk[:], b.kk[:], s.norm[:], ALU.mult))

            @block.scalar
            def _(act):
                act.wait_ge(k.vec_step.sem, k.vec_step.at(1))
                act.activation(s.squares[:], b.kk[:], ACT.Square).then_inc(k.act_step.up(), 1)
                act.activation(z[:, 24, :], z[:, 24, :], ACT.Tanh)
                if emit:
                    act.activation(z[:, 26:28, :], z[:, 26:28, :], ACT.Sigmoid).then_inc(k.act_step.up(), 1)
                act.wait_ge(k.multiplied.sem, k.multiplied.at(1))
                act.activation(s.norm[:], k.psum[:, 0:2048].rearrange("p (j t) -> p j t", j=8), ACT.Sqrt).then_inc(k.act_step.up(), 1)

            @block.tensor
            def _(pe):
                pe.wait_ge(k.act_step.sem, k.act_step.at(1))
                for j in range(8):
                    mm = pe.matmul(k.psum[:, 256 * j:256 * j + 256], k.blocks64, s.squares[:, j, :], start=True, stop=True)
                mm.then_inc(k.multiplied.up(), 1)

        if emit:
            b.Y, b.kdsum = o.rearrange("p j t -> p (j t)").rearrange("p (i c) -> p i c", i=2), spare
        with ExitStack() as inner:
            u = buffers(k, inner, tot=[2, 4], pc=[2, 4], kh=[2, 256], nb=[2, 256], kt=[2, 256], rt=[2, 256], rhs4=[2, 2, 4, P], V=[2, 256],
                        khT=[2, 256], nbT=[2, 256], MT=[2, 4, P], LdT=[2, 4, P], NT=[2, 4, P], ArT=[2, 4, P], AbT=[2, 4, P],
                        Ld=[2, 4, P], E1=[2, 4, P], E2=[2, 4, P], E3=[2, 4, P], X=[2, 4, P], R=[2, 256], U=[2, 256])
            u.TT = u.rhs4[:, 0]
            u.z, u.states, u.kk = z, states, b.kk
            if emit:
                u.Y, u.kdsum = b.Y, b.kdsum
            u.sg, u.a, u.cum, u.excl, u.eP, u.eN, u.eX, u.kd = (
                t[:, n].rearrange("p (j i) t -> p j (i t)", j=2) for t in (u.E1, u.E2, u.E3, u.X) for n in range(2))
            for quarter in range(4):
                for sweep in range(2):
                    rwkv_unit(k, u, L, quarter, sweep, emit)
        if not emit:
            return
        heads, marks = 32, []
        with buffers_scope(k, squares=[heads, 64], row=[heads]) as s, k.stage() as block:

            @block.vector
            def _(dve):
                chain = chained(k, dve)
                y = b.Y.rearrange("p i (h v) -> p (i h) v", v=64)
                row = s.row[:].unsqueeze(2).broadcast_to([P, heads, 64])
                chain(dve.tensor_reduce(s.row[:], y, AXX, ALU.add))
                chain(dve.tensor_scalar(s.row[:], s.row[:], 1.0 / 64, None, ALU.mult))
                chain(dve.tensor_tensor(y, y, row, ALU.subtract))
                chain(dve.tensor_tensor(s.squares[:], y, y, ALU.mult))
                chain(dve.tensor_reduce(s.row[:], s.squares[:], AXX, ALU.add))
                chain(dve.tensor_scalar(s.row[:], s.row[:], 1.0 / 64, 64e-5, ALU.mult, ALU.add))
                variance = k.vec_step.count
                dve.wait_ge(k.act_step.sem, k.act_step.at(1))
                chain(dve.reciprocal(s.row[:], s.row[:]))
                chain(dve.tensor_tensor(y, y, row, ALU.mult))
                marks.append(variance)

            @block.scalar
            def _(act):
                act.wait_ge(k.vec_step.sem, marks[0])
                act.activation(s.row[:], s.row[:], ACT.Sqrt).then_inc(k.act_step.up(), 1)

        with k.stage() as block:

            @block.tensor
            def _(pe):
                for j in range(8):
                    for i in range(2):
                        mm = pe.transpose(k.psum[:, 256 * j + P * i:256 * j + P * i + P], b.Y[:, i, P * j:P * j + P], k.ident)
                mm.then_inc(k.multiplied.up(), 1)
                pe.wait_ge(k.vec_step.sem, k.vec_step.at(2))
                for j in range(8):
                    mm = pe.matmul(k.psum[:, 2048 + 256 * j:2304 + 256 * j], k.blocks64, b.kdsum[:, j, :], start=True, stop=True)
                mm.then_inc(k.multiplied.up(), 1)
                pe.wait_ge(k.vec_step.sem, k.vec_step.at(3))
                for j in range(8):
                    out = k.psum[:, 256 * j:256 * j + 256]
                    pe.matmul(out, L.g2[:, 0, P * j:P * j + P], z[:, 26, :], start=True, stop=False)
                    mm = pe.matmul(out, L.g2[0:32, 1, P * j:P * j + P], z[0:32, 27, :], start=False, stop=True)
                mm.then_inc(k.multiplied.up(), 1)

            @block.vector
            def _(dve):
                chain = chained(k, dve)
                lower = k.psum[:, 0:2048].rearrange("p (j t) -> p j t", j=8)
                upper = k.psum[:, 2048:4096].rearrange("p (j t) -> p j t", j=8)
                chain(dve.tensor_tensor(b.kdsum, b.kdsum, z[:, 0:8, :], ALU.mult))
                chain(dve.tensor_tensor(b.kdsum, b.kdsum, over_tokens(L.r_k, 8, 256), ALU.mult))
                dve.wait_ge(k.multiplied.sem, k.multiplied.at(1))
                chain(dve.tensor_tensor(o, lower, over_tokens(L.lnx_g, 8, 256), ALU.mult))
                chain(dve.tensor_tensor(o, o, over_tokens(L.lnx_b, 8, 256), ALU.add))
                dve.wait_ge(k.multiplied.sem, k.multiplied.at(2))
                chain(dve.tensor_tensor(b.kk[:], upper, z[:, 16:24, :], ALU.mult))
                chain(dve.tensor_tensor(o, o, b.kk[:], ALU.add))
                dve.wait_ge(k.multiplied.sem, k.multiplied.at(3))
                chain(dve.tensor_tensor(o, o, lower, ALU.mult))


@contextmanager
def buffers_scope(k, **shapes):
    with ExitStack() as mem:
        yield buffers(k, mem, **shapes)


def conv_branch(k, L, zc, out, taps):
    reach = max(abs(s) for _, s in taps)
    with buffers_scope(k, u=[8, 256 + 2 * reach], conv=[8, 256]) as s:
        with k.stage() as block:

            @block.scalar
            def _(act):
                act.activation(zc[:, 8:16, :], zc[:, 8:16, :], ACT.Sigmoid).then_inc(k.act_step.up(), 1)

            @block.gpsimd
            def _(pool):
                pool.memset(s.u[:, :, 0:reach], 0.0).then_inc(k.pool_step.up(), 1)
                pool.memset(s.u[:, :, 256 + reach:256 + 2 * reach], 0.0).then_inc(k.pool_step.up(), 1)

            @block.vector
            def _(dve):
                dve.wait_ge(k.act_step.sem, k.act_step.at(1))
                dve.tensor_tensor(s.u[:, :, reach:reach + 256], zc[:, 0:8, :], zc[:, 8:16, :], ALU.mult).then_inc(k.vec_step.up(), 1)
                dve.wait_ge(k.vec_step.sem, k.vec_step.at(1))
                dve.wait_ge(k.pool_step.sem, k.pool_step.at(2))
                for n, (row, shift) in enumerate(taps):
                    for j in range(8):
                        src = s.u[:, j, reach + shift:reach + shift + 256]
                        w = L.conv_w[:, 8 * row + j:8 * row + j + 1]
                        if n:
                            dve.wait_ge(k.vec_step.sem, k.vec_step.count - 7)
                            ins = dve.scalar_tensor_tensor(s.conv[:, j, :], src, w, s.conv[:, j, :], ALU.mult, ALU.add)
                        else:
                            ins = dve.tensor_scalar(s.conv[:, j, :], src, w, None, ALU.mult)
                        ins.then_inc(k.vec_step.up(), 1)

        channel_norm(k, s.conv[:], out, 8, 1024, 1e-5, L.cnorm_g, L.cnorm_b, center=True)
        with k.stage() as block:

            @block.scalar
            def _(act):
                act.activation(s.conv[:], out, ACT.Sigmoid).then_inc(k.act_step.up(), 1)

            @block.vector
            def _(dve):
                dve.wait_ge(k.act_step.sem, k.act_step.at(1))
                dve.tensor_tensor(out, out, s.conv[:], ALU.mult).then_inc(k.vec_step.up(), 1)


def token_mixer(k, L, l, dram, x, mod, states, taps, emit, then):
    nc = k.nc
    with ExitStack() as mem:
        h = buffers(k, mem, h=[8, 256]).h
        channel_norm(k, x, h[:], 8, 1024, 1e-6, mod.scale1, mod.shift1)

        def rhs(t):
            return lambda j: t[:, j, :]

        if not emit:
            with buffers_scope(k, z=[28, 256]) as s:
                gemm(k, weight(dram.w_in[l, 8:28], 8), rhs(h), s.z[:, 8:28, :], then)
                rwkv(k, L, s.z, states, False)
            return
        w_oA, w_oB, w_out = (weight(t[l], 8) for t in (dram.w_oA, dram.w_oB, dram.w_out))
        gates = [weight(dram.w_in[l, 44 + 8 * g:52 + 8 * g], 8) for g in range(2)]
        w_rwkv = weight(dram.w_in[l, 0:28], 8)
        m = buffers(k, mem, m=[8, 256]).m
        ga = buffers(k, mem, g=[8, 256]).g
        with buffers_scope(k, gb=[8, 256], zc=[16, 256], y=[8, 256]) as s:
            gemm(k, weight(dram.w_in[l, 28:44], 8), rhs(h), s.zc[:], w_oB)
            conv_branch(k, L, s.zc[:], m[:], taps)
            gemm(k, w_oB, rhs(m), s.y[:], gates[0])
            gemm(k, gates[0], rhs(h), ga[:], gates[1])
            gemm(k, gates[1], rhs(h), s.gb[:], w_rwkv)
            with k.stage() as block:

                @block.scalar
                def _(act):
                    for g, t in enumerate((ga, s.gb)):
                        for j in range(8):
                            ins = act.activation(t[:, j, :], t[:, j, :], ACT.Sigmoid, bias=L.gate_b[:, 8 * g + j:8 * g + j + 1])
                    ins.then_inc(k.act_step.up(), 1)

                @block.vector
                def _(dve):
                    dve.wait_ge(k.act_step.sem, k.act_step.at(1))
                    dve.tensor_tensor(m[:], s.gb[:], s.y[:], ALU.mult).then_inc(k.vec_step.up(), 1)
        o = buffers(k, mem, o=[8, 256]).o
        with buffers_scope(k, z=[28, 256]) as s:
            gemm(k, w_rwkv, rhs(h), s.z[:], w_oA)
            rwkv(k, L, s.z, states, True, o[:], h[:])
        with buffers_scope(k, y=[8, 256]) as s:
            gemm(k, w_oA, rhs(o), s.y[:], w_out)
            with k.stage() as block:

                @block.vector
                def _(dve):
                    chain = chained(k, dve)
                    chain(dve.tensor_tensor(s.y[:], s.y[:], ga[:], ALU.mult))
                    chain(dve.tensor_tensor(m[:], m[:], s.y[:], ALU.add))

            gemm(k, w_out, rhs(m), s.y[:], then)
            with k.stage() as block:

                @block.vector
                def _(dve):
                    chain = chained(k, dve)
                    chain(dve.tensor_tensor(s.y[:], s.y[:], over_tokens(mod.gate1, 8, 256), ALU.mult))
                    chain(dve.tensor_tensor(x, x, s.y[:], ALU.add))


HEADS, KEYS, TOPK, SLOTS = 8, 128, 16, 128
RING = 8
LOWEST = -3.0e38


def top16(k, dve, lists, values, work, best, index):
    up = k.vec_step

    def settled():
        dve.wait_ge(up.sem, up.count)

    for n in lists:
        dve.max(best[:, n, 0:8], values(n)).then_inc(up.up(), 1)
    settled()
    for n in lists:
        dve.max_index(index[:, n, 0:8], best[:, n, 0:8], values(n)).then_inc(up.up(), 1)
    for n in lists:
        dve.match_replace(work(n), best[:, n, 0:8], values(n), LOWEST).then_inc(up.up(), 1)
    settled()
    for n in lists:
        dve.max(best[:, n, 8:16], work(n)).then_inc(up.up(), 1)
    settled()
    for n in lists:
        dve.max_index(index[:, n, 8:16], best[:, n, 8:16], work(n)).then_inc(up.up(), 1)
    settled()


def peer(k, l, dram, x, mod, then):
    nc = k.nc
    with ExitStack() as mem:
        b = buffers(k, mem, h=[8, 256], htok=[2, 1024], gw=[2, SLOTS], dots=[2, SLOTS])
        eidx = mem.enter_context(k.sbuf("expert", [2 * SLOTS + RING], U32))
        channel_norm(k, x, b.h[:], 8, 1024, 1e-6, mod.scale2, mod.shift2)
        with buffers_scope(k, q=[16, 256], keys=[16, P], s=[16, P], work=[16, P], best1=[16, 16], cand=[HEADS, 256],
                           cand2=[HEADS, 256], best=[HEADS, 16], i12=[16, 16], pf=[2, HEADS, 16], hot=[HEADS, 16, 16],
                           e12=[2, HEADS, 16], row=[HEADS]) as s, \
                k.sbuf("idx1", [16, 16], U32) as idx1, k.sbuf("pos", [HEADS, 16], U32) as pos, \
                k.sbuf("posab", [2, HEADS, 16], U32) as posab:
            load(k, (s.keys[:], dram.sub_keys[l]))
            gemm(k, weight(dram.w_q[l], 8), lambda j: b.h[:, j, :], s.q[:], then)
            for tile in range(2):
                toks = slice(tile * P, tile * P + P)
                with k.stage() as block:

                    @block.tensor
                    def _(pe):
                        for n in range(16):
                            mm = pe.matmul(k.psum[:, n * P:n * P + P], s.q[:, n, toks], s.keys[:, n, :], start=True, stop=True)
                        mm.then_inc(k.multiplied.up(), 1)
                        for j in range(8):
                            mm = pe.transpose(k.psum[:, 2048 + j * P:2048 + j * P + P], b.h[:, j, toks], k.ident)
                        mm.then_inc(k.multiplied.up(), 1)

                    @block.scalar
                    def _(act):
                        act.wait_ge(k.multiplied.sem, k.multiplied.at(1))
                        act.activation(s.s[:], k.psum[:, 0:2048].rearrange("p (n c) -> p n c", n=16), ACT.Copy).then_inc(k.act_step.up(), 1)
                        act.wait_ge(k.multiplied.sem, k.multiplied.at(2))
                        act.activation(b.htok[:, tile, :], k.psum[:, 2048:3072], ACT.Copy).then_inc(k.act_step.up(), 1)

                    @block.vector
                    def _(dve):
                        chain = chained(k, dve)
                        dve.wait_ge(k.act_step.sem, k.act_step.at(1))
                        top16(k, dve, range(16), lambda n: s.s[:, n, :], lambda n: s.work[:, n, :], s.best1, idx1)
                        two = s.best1[:].rearrange("p (h c) j -> p h c j", c=2)
                        chain(dve.tensor_tensor(s.cand[:].rearrange("p h (a b) -> p h a b", b=16),
                                                two[:, :, 0, :].unsqueeze(3).broadcast_to([P, HEADS, 16, 16]),
                                                two[:, :, 1, :].unsqueeze(2).broadcast_to([P, HEADS, 16, 16]), ALU.add))
                        top16(k, dve, range(HEADS), lambda n: s.cand[:, n, :], lambda n: s.cand2[:, n, :], s.best, pos)
                        chain(dve.tensor_scalar(posab[:, 0], pos[:], 4, None, ALU.logical_shift_right))
                        chain(dve.tensor_scalar(posab[:, 1], pos[:], 15, None, ALU.bitwise_and))
                        chain(dve.tensor_copy(s.pf[:], posab[:]))
                        chain(dve.tensor_copy(s.i12[:], idx1[:]))
                        i2 = s.i12[:].rearrange("p (h c) j -> p h c j", c=2)
                        iota = k.iota16.unsqueeze(1).unsqueeze(1).broadcast_to([P, HEADS, 16, 16])
                        for c in range(2):
                            chain(dve.tensor_tensor(s.hot[:], s.pf[:, c].unsqueeze(3).broadcast_to([P, HEADS, 16, 16]), iota, ALU.is_equal))
                            chain(dve.tensor_tensor(s.hot[:], s.hot[:], i2[:, :, c, :].unsqueeze(2).broadcast_to([P, HEADS, 16, 16]), ALU.mult))
                            chain(dve.tensor_reduce(s.e12[:, c], s.hot[:], AXX, ALU.add))
                        chain(dve.scalar_tensor_tensor(s.e12[:, 0], s.e12[:, 0], float(KEYS), s.e12[:, 1], ALU.mult, ALU.add))
                        chain(dve.tensor_scalar(eidx[:, tile * SLOTS:(tile + 1) * SLOTS], s.e12[:, 0].rearrange("p h j -> p (h j)"), float(l * KEYS * KEYS), None, ALU.add))
                        gw = b.gw[:, tile, :].rearrange("p (h j) -> p h j", j=16)
                        chain(dve.tensor_tensor(gw, s.best[:], s.best[:, :, 0:1].broadcast_to([P, HEADS, 16]), ALU.subtract))

                with k.stage() as block:

                    @block.scalar
                    def _(act):
                        act.activation(b.gw[:, tile, :], b.gw[:, tile, :], ACT.Exp).then_inc(k.act_step.up(), 1)

                    @block.vector
                    def _(dve):
                        chain = chained(k, dve)
                        dve.wait_ge(k.act_step.sem, k.act_step.at(1))
                        gw = b.gw[:, tile, :].rearrange("p (h j) -> p h j", j=16)
                        chain(dve.tensor_reduce(s.row[:], gw, AXX, ALU.add))
                        chain(dve.reciprocal(s.row[:], s.row[:]))
                        chain(dve.tensor_tensor(gw, gw, s.row[:].unsqueeze(2).broadcast_to([P, HEADS, 16]), ALU.mult))

        with ExitStack() as inner:
            r = buffers(k, inner, ring=[RING, 1024], acc=[2, 1024], dot8=[2, RING], act8=[2, RING])
            idx8 = [inner.enter_context(k.sbuf("expert_group", [RING], U32)) for _ in range(2)]
            groups = SLOTS // RING
            rounds = groups // 2
            passes = [(dram.peer_u, 0), (dram.peer_u, 1), (dram.peer_v, 0), (dram.peer_v, 1)]
            with k.stage() as block:
                def turn(n, i, part):
                    return i * 2 + (n * groups + part)

                @block.gpsimd
                def _(pool):
                    for n, (table, tile) in enumerate(passes):
                        def gather(i, part, first=False):
                            g = turn(n, i, part)
                            pool.wait_ge(k.staged.sem, g + k.staged.at(1))
                            pool.sem_inc(k.slot_free.sem, 1)
                            for j in range(RING):
                                if not first:
                                    pool.wait_ge(k.row_used.sem, g * RING + (k.row_used.at(1) + j - RING))
                                    pool.sem_inc(k.slot_free.sem, 1)
                                pool.indirect_dma_start(
                                    r.ring[:, j, :], None, table,
                                    bass.IndirectOffsetOnAxis(ap=idx8[part][:, j:j + 1], axis=0),
                                ).then_inc(k.gathered[j].sem, 16)

                        start = 0
                        if n == 0:
                            gather(0, 0, True)
                            gather(0, 1)
                            start = 1
                        with pool.Fori(start, rounds) as i:
                            gather(i, 0)
                            gather(i, 1)

                @block.vector
                def _(dve):
                    dve.memset(r.acc[:], 0.0).then_inc(k.vec_step.up(), 1)
                    dve.tensor_copy(eidx[:, 2 * SLOTS:2 * SLOTS + RING], eidx[:, 0:RING]).then_inc(k.vec_step.up(), 1)
                    dve.tensor_copy(idx8[0][:], eidx[:, 0:RING]).then_inc(k.staged.sem, 1)
                    dve.wait_ge(k.vec_step.sem, k.vec_step.count)
                    for n, (_, tile) in enumerate(passes):
                        if n >= 2:
                            dve.wait_ge(k.act_step.sem, k.act_step.at(tile + 1))
                            dve.tensor_tensor(b.dots[:, tile, :], b.dots[:, tile, :], b.gw[:, tile, :], ALU.mult).then_inc(k.weighted.up(), 1)
                            dve.wait_ge(k.weighted.sem, k.weighted.count)

                        def use(i, part):
                            g = turn(n, i, part)
                            at = i * (2 * RING) + part * RING
                            dve.tensor_copy(idx8[1 - part][:], eidx[:, bass.ds(at + (tile * SLOTS + RING), RING)]).then_inc(k.staged.sem, 1)
                            if n >= 2:
                                dve.tensor_copy(r.act8[:, part, :], b.dots[:, tile, bass.ds(at, RING)]).then_inc(k.weights_staged.sem, 1)
                                dve.wait_ge(k.weights_staged.sem, i * 2 + (k.weights_staged.at(1) + (n - 2) * groups + part))
                            for j in range(RING):
                                dve.wait_ge(k.gathered[j].sem, g * 16 + k.gathered[j].at(16))
                                if n < 2:
                                    dve.tensor_tensor_reduce(r.ring[:, j, :], r.ring[:, j, :], b.htok[:, tile, :], 1.0, 0.0, ALU.mult,
                                                             ALU.add, r.dot8[:, part, j:j + 1]).then_inc(k.row_used.sem, 1)
                                else:
                                    dve.wait_ge(k.row_used.sem, g * RING + (k.row_used.at(0) + j))
                                    dve.scalar_tensor_tensor(r.acc[:, tile, :], r.ring[:, j, :], r.act8[:, part, j:j + 1],
                                                             r.acc[:, tile, :], ALU.mult, ALU.add).then_inc(k.row_used.sem, 1)
                            if n < 2:
                                dve.wait_ge(k.row_used.sem, g * RING + k.row_used.at(RING))
                                dve.tensor_copy(b.dots[:, tile, bass.ds(at, RING)], r.dot8[:, part, :]).then_inc(k.dots_kept.sem, 1)

                        with dve.Fori(0, rounds) as i:
                            use(i, 0)
                            use(i, 1)

                @block.scalar
                def _(act):
                    for tile in range(2):
                        act.wait_ge(k.dots_kept.sem, k.dots_kept.at((tile + 1) * groups))
                        act.activation(b.dots[:, tile, :], b.dots[:, tile, :], ACT.Gelu).then_inc(k.act_step.up(), 1)

                k.staged.up(4 * groups + 1)
                k.row_used.up(4 * SLOTS)
                k.dots_kept.up(2 * groups)
                k.weights_staged.up(2 * groups)
                for j in range(RING):
                    k.gathered[j].up(16 * 4 * groups)

            with k.stage() as block:

                @block.tensor
                def _(pe):
                    for j in range(8):
                        for i in range(2):
                            mm = pe.transpose(k.psum[:, 256 * j + P * i:256 * j + P * i + P], r.acc[:, i, P * j:P * j + P], k.ident)
                    mm.then_inc(k.multiplied.up(), 1)

                @block.vector
                def _(dve):
                    dve.wait_ge(k.multiplied.sem, k.multiplied.at(1))
                    for j in range(8):
                        dve.scalar_tensor_tensor(x[:, j, :], k.psum[:, 256 * j:256 * j + 256], mod.gate2[:, j:j + 1], x[:, j, :],
                                                 ALU.mult, ALU.add).then_inc(k.vec_step.up(), 1)



DN_Q, DN_K, DN_V, DN_Z, CQ, CKV, KPE, GLA_Q, GLA_K, GLA_V, GLA_G, GLA_LR, FOX_Q, FOX_K, FOX_V, SMALL = (
    0, 2, 4, 6, 8, 10, 11, 12, 13, 14, 16, 18, 19, 21, 23, 25)
VECTORS2 = {"norm_mix_pre_2": 8, "norm_mix_post_2": 8, "norm_mlp_pre_2": 8, "norm_mlp_post_2": 8, "dn_conv_2": 24, "mla_q_norm_2": 2,
            "mla_kv_norm_2": 1, "gla_gate_bias_2": 1, "b_gate_2": 32, "dn_norm_2": 1, "gla_norm_2": 1}
ROWS2 = ("dn_dt_bias_2", "fox_f_bias_2", "dn_a_log_2")


def per_head(column, n):
    return column.unsqueeze(2).broadcast_to([P, 4, n])


def heads4(t):
    return t.rearrange("p (h c) -> p h c", h=4)


def for_heads(mask, n):
    return mask.unsqueeze(1).broadcast_to([P, n, mask.shape[1]])


def to_tokens(k, pairs):
    with k.stage() as block:

        @block.tensor
        def _(pe):
            for n, (src, _) in enumerate(pairs):
                for i in range(2):
                    mm = pe.transpose(k.psum[:, 256 * n + P * i:256 * n + P * i + P], src[:, P * i:P * i + P], k.ident)
            mm.then_inc(k.multiplied.up(), 1)

        @block.scalar
        def _(act):
            act.wait_ge(k.multiplied.sem, k.multiplied.at(1))
            for n, (_, dst) in enumerate(pairs):
                act.activation(dst, k.psum[:, 256 * n:256 * n + 256].rearrange("p (i c) -> p i c", i=2), ACT.Copy
                               ).then_inc(k.act_step.up(), 1)


def to_channels(k, y, out, gain=None, gate=None):
    with k.stage() as block:

        @block.tensor
        def _(pe):
            for j in range(2):
                for i in range(2):
                    mm = pe.transpose(k.psum[:, 256 * j + P * i:256 * j + P * i + P], y[:, i, P * j:P * j + P], k.ident)
            mm.then_inc(k.multiplied.up(), 1)

        @block.vector
        def _(dve):
            dve.wait_ge(k.multiplied.sem, k.multiplied.at(1))
            turned = k.psum[:, 0:512].rearrange("p (j t) -> p j t", j=2)
            if gate is None:
                dve.tensor_copy(out, turned).then_inc(k.vec_step.up(), 1)
            else:
                dve.scalar_tensor_tensor(out, turned, gain, gate, ALU.mult, ALU.mult).then_inc(k.vec_step.up(), 1)


def silu(k, t, tmp):
    with k.stage() as block:

        @block.scalar
        def _(act):
            act.activation(tmp, t, ACT.Sigmoid).then_inc(k.act_step.up(), 1)

        @block.vector
        def _(dve):
            dve.wait_ge(k.act_step.sem, k.act_step.at(1))
            dve.tensor_tensor(t, t, tmp, ALU.mult).then_inc(k.vec_step.up(), 1)


def softplus(k, y, tmp, out, scale):
    with k.stage() as block:

        @block.vector
        def _(dve):
            chain = chained(k, dve)
            chain(dve.scalar_tensor_tensor(tmp, y, -1.0, y, ALU.mult, ALU.min))
            dve.wait_ge(k.act_step.sem, k.act_step.at(2))
            chain(dve.scalar_tensor_tensor(out, y, 0.0, tmp, ALU.max, ALU.add))
            chain(dve.tensor_scalar(out, out, scale, None, ALU.mult))

        @block.scalar
        def _(act):
            act.wait_ge(k.vec_step.sem, k.vec_step.at(1))
            act.activation(tmp, tmp, ACT.Exp).then_inc(k.act_step.up(), 1)
            act.wait_ge(k.act_step.sem, k.act_step.at(1))
            act.activation(tmp, tmp, ACT.Ln, bias=1.0).then_inc(k.act_step.up(), 1)


def head_norm(k, y, squares, row):
    with k.stage() as block:
        marks = []

        @block.vector
        def _(dve):
            chain = chained(k, dve)
            chain(dve.tensor_tensor(squares, y, y, ALU.mult))
            chain(dve.tensor_reduce(row, squares, AXX, ALU.add))
            chain(dve.tensor_scalar(row, row, 1.0 / 64, 1e-6, ALU.mult, ALU.add))
            marks.append(k.vec_step.count)
            dve.wait_ge(k.act_step.sem, k.act_step.at(1))
            chain(dve.reciprocal(row, row))
            chain(dve.tensor_tensor(y, y, row.unsqueeze(2).broadcast_to([P, 8, 64]), ALU.mult))

        @block.scalar
        def _(act):
            act.wait_ge(k.vec_step.sem, marks[0])
            act.activation(row, row, ACT.Sqrt).then_inc(k.act_step.up(), 1)


def delta_branch(k, V, z, small, out):
    with buffers_scope(k, conv=[6, 256], tmp=[6, 256], ktok=[2, 256], vtok=[2, 256], km=[4, 256], qm=[4, 256], row=[8],
                       gcol=[2, 4], eg=[2, 4], bne=[2, 4], etail=[2, 4], eT=[2, 2, 4], D=[2, 4, P], L=[2, 4, P], Aq=[2, 4, P],
                       AqT=[2, 4, P], Ld=[2, 4, P], LdT=[2, 4, P], NT=[2, 4, P], E1=[2, 4, P], E2=[2, 4, P], E3=[2, 4, P],
                       X=[2, 4, P], TT=[2, 4, P], S=[2, P], R=[256], U=[2, 256], Y=[2, 256], inc=[2, P]) as b:
        beta, g = small.beta, small.g
        conv = b.conv
        with k.stage() as block:

            @block.vector
            def _(dve):
                chain = chained(k, dve)
                w = V.dn_conv_2.rearrange("p (r j) -> p r j", r=4)
                chain(dve.tensor_tensor(conv[:], z[:, 0:6, :], over_tokens(w[:, 3, :], 6, 256), ALU.mult))
                for r in range(3):
                    late = 3 - r
                    chain(dve.tensor_tensor(b.tmp[:, :, late:256], z[:, 0:6, 0:256 - late], over_tokens(w[:, r, :], 6, 256 - late), ALU.mult))
                    chain(dve.tensor_tensor(conv[:, :, late:256], conv[:, :, late:256], b.tmp[:, :, late:256], ALU.add))

        silu(k, conv[:], b.tmp[:])
        with k.stage() as block:

            @block.scalar
            def _(act):
                act.activation(b.tmp[:, 0:4, :], conv[:, 0:4, :], ACT.Square).then_inc(k.act_step.up(), 1)
                act.wait_ge(k.vec_step.sem, k.vec_step.at(1))
                act.activation(b.tmp[:, 0:4, :], b.tmp[:, 0:4, :], ACT.Sqrt).then_inc(k.act_step.up(), 1)

            @block.tensor
            def _(pe):
                pe.wait_ge(k.act_step.sem, k.act_step.at(1))
                for j in range(4):
                    mm = pe.matmul(k.psum[:, 256 * j:256 * j + 256], k.blocks64, b.tmp[:, j, :], start=True, stop=True)
                mm.then_inc(k.multiplied.up(), 1)

            @block.vector
            def _(dve):
                chain = chained(k, dve)
                dve.wait_ge(k.multiplied.sem, k.multiplied.at(1))
                t = b.tmp[:, 0:4, :]
                chain(dve.tensor_scalar(t, k.psum[:, 0:1024].rearrange("p (j t) -> p j t", j=4), 1e-6, None, ALU.add))
                dve.wait_ge(k.act_step.sem, k.act_step.at(2))
                chain(dve.reciprocal(t, t))
                chain(dve.tensor_tensor(conv[:, 0:4, :], conv[:, 0:4, :], t, ALU.mult))
                chain(dve.tensor_scalar(conv[:, 0:2, :], conv[:, 0:2, :], 64 ** -0.5, None, ALU.mult))
                for h in range(4):
                    chain(dve.tensor_scalar(b.qm[:, h, :], conv[:, h // 2, :], k.half_mask[h % 2], None, ALU.mult))
                    chain(dve.tensor_scalar(b.km[:, h, :], conv[:, 2 + h // 2, :], k.half_mask[h % 2], None, ALU.mult))
                chain(dve.memset(b.S[:], 0.0))

        to_tokens(k, [(conv[:, 2 + j, :], b.ktok[:, :, P * j:P * j + P]) for j in range(2)]
                  + [(conv[:, 4 + j, :], b.vtok[:, :, P * j:P * j + P]) for j in range(2)])
        for i in range(2):
            toks = slice(P * i, P * i + P)
            with k.stage() as block:

                @block.tensor
                def _(pe):
                    gi = g[:, i, :]
                    for n, m in enumerate((k.up_incl, k.blocks64, k.chunk0, k.chunk1)):
                        pe.matmul(k.bank(0)[:, 4 * n:4 * n + 4], m, gi, start=True, stop=True)
                    for h in range(4):
                        hs = slice(P * h, P * h + P)
                        pe.matmul(k.bank(1)[:, hs], g[:, i, h:h + 1].broadcast_to([P, P]), k.up_incl, start=True, stop=True)
                        pe.matmul(k.bank(2)[:, hs], b.km[:, h, toks], conv[:, 2 + h // 2, toks], start=True, stop=True)
                        mm = pe.matmul(k.bank(3)[:, hs], b.qm[:, h, toks], conv[:, 2 + h // 2, toks], start=True, stop=True)
                    mm.then_inc(k.multiplied.up(), 1)

                @block.vector
                def _(dve):
                    chain = chained(k, dve)
                    dve.wait_ge(k.multiplied.sem, k.multiplied.at(1))
                    sums = k.bank(0)
                    chain(dve.tensor_copy(b.gcol[:, i, :], sums[:, 0:4]))
                    chain(dve.tensor_tensor(b.etail[:, i, :], sums[:, 4:8], b.gcol[:, i, :], ALU.subtract))
                    chain(dve.tensor_copy(b.eT[:, i], sums[:, 8:16].rearrange("p (c h) -> p c h", c=2)))
                    for h in range(4):
                        chain(dve.tensor_scalar(b.D[:, i, h, :], k.bank(1)[:, P * h:P * h + P], -1.0, b.gcol[:, i, h:h + 1], ALU.mult, ALU.add))
                    chain(dve.tensor_tensor(b.D[:, i], b.D[:, i], for_heads(k.lo_incl, 4), ALU.mult))

            with k.stage() as block:

                @block.scalar
                def _(act):
                    act.activation(b.D[:, i], b.D[:, i], ACT.Exp).then_inc(k.act_step.up(), 1)
                    act.activation(b.eg[:, i, :], b.gcol[:, i, :], ACT.Exp).then_inc(k.act_step.up(), 1)
                    act.activation(b.etail[:, i, :], b.etail[:, i, :], ACT.Exp).then_inc(k.act_step.up(), 1)
                    act.activation(b.eT[:, i], b.eT[:, i], ACT.Exp).then_inc(k.act_step.up(), 1)

                @block.vector
                def _(dve):
                    chain = chained(k, dve)
                    dve.wait_ge(k.act_step.sem, k.act_step.at(4))
                    chain(dve.scalar_tensor_tensor(b.bne[:, i, :], b.eg[:, i, :], -1.0, beta[:, i, :], ALU.mult, ALU.mult))
                    chain(dve.tensor_tensor(b.D[:, i], b.D[:, i], for_heads(k.lo_incl, 4), ALU.mult))
                    chain(dve.scalar_tensor_tensor(b.L[:, i], heads4(k.bank(2)), -1.0, b.D[:, i], ALU.mult, ALU.mult))
                    chain(dve.tensor_tensor(b.L[:, i], b.L[:, i], for_heads(k.lo, 4), ALU.mult))
                    chain(dve.tensor_tensor(b.L[:, i], b.L[:, i], per_head(beta[:, i, :], P), ALU.mult))
                    chain(dve.tensor_tensor(b.Aq[:, i], heads4(k.bank(3)), b.D[:, i], ALU.mult))
                    chain(dve.tensor_tensor(b.Ld[:, i], b.L[:, i], for_heads(k.lo8, 4), ALU.mult))
                    chain(dve.tensor_tensor(heads4(b.vtok[:, i, :]), heads4(b.vtok[:, i, :]), per_head(beta[:, i, :], 64), ALU.mult))
                    chain(dve.tensor_tensor(heads4(b.ktok[:, i, :]), heads4(b.ktok[:, i, :]), per_head(b.etail[:, i, :], 64), ALU.mult))

            with k.stage() as block:

                @block.tensor
                def _(pe):
                    for h in range(4):
                        pe.transpose(k.bank(4)[:, P * h:P * h + P], b.L[:, i, h, :], k.ident)
                        mm = pe.transpose(k.bank(5)[:, P * h:P * h + P], b.Aq[:, i, h, :], k.ident)
                    mm.then_inc(k.multiplied.up(), 1)

                @block.vector
                def _(dve):
                    dve.wait_ge(k.multiplied.sem, k.multiplied.at(1))
                    dve.tensor_tensor(b.LdT[:, i], heads4(k.bank(4)), for_heads(k.up8, 4), ALU.mult).then_inc(k.vec_step.up(), 1)
                    dve.tensor_tensor(b.NT[:, i], heads4(k.bank(4)), for_heads(k.up_far, 4), ALU.mult).then_inc(k.vec_step.up(), 1)
                    dve.tensor_copy(b.AqT[:, i], heads4(k.bank(5))).then_inc(k.vec_step.up(), 1)

        invert_unit_lower(k, 2, b.Ld, b.LdT, b.NT, (b.E1, b.E2, b.E3, b.X), b.TT)
        for i in range(2):
            toks = slice(P * i, P * i + P)
            bK, bQ, bU, bS, bY = (k.bank(n, 256) for n in range(5))
            y = b.Y[:, i, :]
            with k.stage() as block:
                marks = {}

                @block.vector
                def _(dve):
                    chain = chained(k, dve)
                    for c in range(2):
                        dve.wait_ge(k.multiplied.sem, k.multiplied.at(3 * c + 1))
                        chain(dve.tensor_tensor(heads4(b.R[:]), heads4(bK), per_head(b.bne[:, i, :], 64), ALU.mult))
                        chain(dve.tensor_tensor(b.R[:], b.R[:], b.vtok[:, i, :], ALU.add))
                        marks["R", c] = k.vec_step.count
                        if c == 0:
                            chain(dve.tensor_scalar(y, bQ, k.half_mask[0], None, ALU.mult))
                        else:
                            chain(dve.scalar_tensor_tensor(y, bQ, k.half_mask[1], y, ALU.mult, ALU.add))
                        dve.wait_ge(k.multiplied.sem, k.multiplied.at(3 * c + 2))
                        chain(dve.tensor_scalar(b.U[:, c, :], bU, k.half_mask[c], None, ALU.mult))
                        marks["U", c] = k.vec_step.count
                        dve.wait_ge(k.multiplied.sem, k.multiplied.at(3 * c + 3))
                        chain(dve.tensor_tensor(b.inc[:], bS.rearrange("p (j v) -> p j v", j=2), for_heads(k.blocks64, 2), ALU.mult))
                        S4 = b.S[:].rearrange("p j (h v) -> p (j h) v", h=2)
                        chain(dve.tensor_tensor(S4, S4, per_head(b.eT[:, i, c, :], 64), ALU.mult))
                        chain(dve.tensor_tensor(b.S[:], b.S[:], b.inc[:], ALU.add))
                        marks["S", c] = k.vec_step.count
                    chain(dve.tensor_tensor(heads4(y), heads4(y), per_head(b.eg[:, i, :], 64), ALU.mult))
                    chain(dve.tensor_tensor(b.U[:, 0, :], b.U[:, 0, :], b.U[:, 1, :], ALU.add))
                    marks["Usum"] = k.vec_step.count
                    dve.wait_ge(k.multiplied.sem, k.multiplied.at(7))
                    chain(dve.tensor_tensor(y, y, bY, ALU.add))

                @block.tensor
                def _(pe):
                    for c in range(2):
                        if c:
                            pe.wait_ge(k.vec_step.sem, marks["S", 0])
                        for j in range(2):
                            js = slice(P * j, P * j + P)
                            pe.matmul(bK[:, js], conv[:, 2 + j, toks], b.S[:, j, :], start=True, stop=True)
                            mm = pe.matmul(bQ[:, js], conv[:, j, toks], b.S[:, j, :], start=True, stop=True)
                        mm.then_inc(k.multiplied.up(), 1)
                        pe.wait_ge(k.vec_step.sem, marks["R", c])
                        for h in range(4):
                            hs = slice(64 * h, 64 * h + 64)
                            mm = pe.matmul(bU[:, hs], b.TT[:, i, h, :], b.R[:, hs], start=True, stop=True)
                        mm.then_inc(k.multiplied.up(), 1)
                        pe.wait_ge(k.vec_step.sem, marks["U", c])
                        for j in range(2):
                            js = slice(P * j, P * j + P)
                            mm = pe.matmul(bS[:, js], b.ktok[:, i, js], b.U[:, c, js], start=True, stop=True)
                        mm.then_inc(k.multiplied.up(), 1)
                    pe.wait_ge(k.vec_step.sem, marks["Usum"])
                    for h in range(4):
                        hs = slice(64 * h, 64 * h + 64)
                        mm = pe.matmul(bY[:, hs], b.AqT[:, i, h, :], b.U[:, 0, hs], start=True, stop=True)
                    mm.then_inc(k.multiplied.up(), 1)

        head_norm(k, b.Y[:].rearrange("p i (h v) -> p (i h) v", v=64), b.tmp[:, 0:2, :].rearrange("p i (h v) -> p (i h) v", v=64), b.row[:])
        silu(k, z[:, DN_Z:DN_Z + 2, :], b.tmp[:, 0:2, :])
        to_channels(k, b.Y, out, V.dn_norm_2, z[:, DN_Z:DN_Z + 2, :])


def gla_branch(k, V, z, gate_up, out):
    with buffers_scope(k, w=[256], tmp=[256], cum=[256], tot=[4], pc=[4], dist=[256], qin=[256], kin=[256], ktail=[256], qm=[4, 256],
                       ktok=[2, P], vtok=[2, 256], Vc=[2, 2, 256], AT=[2, 4, P], S=[256], inc=[256], Y=[2, 256], squares=[8, 64],
                       row=[8], tmp2=[2, 256]) as b:
        with k.stage() as block:

            @block.tensor
            def _(pe):
                pe.matmul(k.bank(0, 256), gate_up, z[0:16, GLA_LR, :], start=True, stop=True).then_inc(k.multiplied.up(), 1)

            @block.vector
            def _(dve):
                dve.wait_ge(k.multiplied.sem, k.multiplied.at(1))
                dve.tensor_scalar(b.w[:], k.bank(0, 256), V.gla_gate_bias_2, -1.0, ALU.add, ALU.mult).then_inc(k.vec_step.up(), 1)

        softplus(k, b.w[:], b.tmp[:], b.w[:], -1.0 / 16.0)
        with k.stage() as block:

            @block.vector
            def _(dve):
                chain = chained(k, dve)
                chain(dve.tensor_tensor_scan(b.cum[:], k.segments[:, 0:256], b.w[:], 0.0, ALU.mult, ALU.add))
                chain(dve.tensor_copy(b.tot[:], b.cum[:, 63::64]))
                chain(dve.tensor_tensor(b.dist[:].rearrange("p (c t) -> p c t", c=4), b.tot[:].unsqueeze(2).broadcast_to([P, 4, 64]),
                                        b.cum[:].rearrange("p (c t) -> p c t", c=4), ALU.subtract))
                dve.wait_ge(k.act_step.sem, k.act_step.at(4))
                chain(dve.scalar_tensor_tensor(b.qin[:], b.qin[:], 32 ** -0.5, z[:, GLA_Q, :], ALU.mult, ALU.mult))
                chain(dve.tensor_tensor(b.kin[:], b.kin[:], z[:, GLA_K, :], ALU.mult))
                chain(dve.tensor_tensor(b.ktail[:], b.dist[:], z[:, GLA_K, :], ALU.mult))
                for h in range(4):
                    chain(dve.tensor_scalar(b.qm[:, h, :], b.qin[:], k.quarter_mask[h], None, ALU.mult))
                chain(dve.memset(b.S[:], 0.0))
                chain(dve.memset(b.AT[:], 0.0))

            @block.scalar
            def _(act):
                act.wait_ge(k.vec_step.sem, k.vec_step.at(3))
                act.activation(b.qin[:], b.cum[:], ACT.Exp).then_inc(k.act_step.up(), 1)
                act.activation(b.kin[:], b.cum[:], ACT.Exp, scale=-1.0).then_inc(k.act_step.up(), 1)
                act.activation(b.pc[:], b.tot[:], ACT.Exp).then_inc(k.act_step.up(), 1)
                act.activation(b.dist[:], b.dist[:], ACT.Exp).then_inc(k.act_step.up(), 1)

        to_tokens(k, [(b.ktail[:], b.ktok[:])] + [(z[:, GLA_V + j, :], b.vtok[:, :, P * j:P * j + P]) for j in range(2)])
        with k.stage() as block:
            marks = {}

            @block.vector
            def _(dve):
                chain = chained(k, dve)
                for i in range(2):
                    for c in range(2):
                        chain(dve.tensor_scalar(b.Vc[:, i, c, :], b.vtok[:, i, :], k.half_mask[c], None, ALU.mult))
                marks["V"] = k.vec_step.count
                allowed = for_heads(k.up_incl, 4).bitcast(U32)
                for i in range(2):
                    dve.wait_ge(k.multiplied.sem, k.multiplied.at(i + 1))
                    chain(dve.copy_predicated(b.AT[:, i], allowed, heads4(k.bank(i))))
                marks["A"] = k.vec_step.count
                for n in range(4):
                    i, c = n // 2, n % 2
                    y = b.Y[:, i, :]
                    dve.wait_ge(k.multiplied.sem, k.multiplied.at(3 + n))
                    if c == 0:
                        chain(dve.tensor_scalar(y, k.bank(2, 256), k.half_mask[0], None, ALU.mult))
                    else:
                        chain(dve.scalar_tensor_tensor(y, k.bank(2, 256), k.half_mask[1], y, ALU.mult, ALU.add))
                    chain(dve.tensor_tensor(heads4(b.inc[:]), heads4(k.bank(3, 256)), per_head(k.quarters, 64), ALU.mult))
                    chain(dve.scalar_tensor_tensor(b.S[:], b.S[:], b.pc[:, n:n + 1], b.inc[:], ALU.mult, ALU.add))
                    marks["S", n] = k.vec_step.count
                dve.wait_ge(k.multiplied.sem, k.multiplied.at(7))
                chain(dve.tensor_tensor(b.Y[:], b.Y[:], k.bank(4).rearrange("p (i v) -> p i v", i=2), ALU.add))

            @block.tensor
            def _(pe):
                for i in range(2):
                    toks = slice(P * i, P * i + P)
                    pe.matmul(heads4(k.bank(i)), b.kin[:, toks], b.qm[:, :, toks], start=True, stop=True).then_inc(k.multiplied.up(), 1)
                pe.wait_ge(k.vec_step.sem, marks["V"])
                for n in range(4):
                    i, c = n // 2, n % 2
                    if n:
                        pe.wait_ge(k.vec_step.sem, marks["S", n - 1])
                    pe.matmul(k.bank(2, 256), b.qin[:, P * i:P * i + P], b.S[:], start=True, stop=True)
                    pe.matmul(k.bank(3, 256), b.ktok[:, i, :], b.Vc[:, i, c, :], start=True, stop=True).then_inc(k.multiplied.up(), 1)
                for i in range(2):
                    for h in range(4):
                        at = 256 * i + 64 * h
                        mm = pe.matmul(k.bank(4)[:, at:at + 64], b.AT[:, i, h, :], b.vtok[:, i, 64 * h:64 * h + 64], start=True, stop=True)
                mm.then_inc(k.multiplied.up(), 1)

        head_norm(k, b.Y[:].rearrange("p i (h v) -> p (i h) v", v=64), b.squares[:], b.row[:])
        silu(k, z[:, GLA_G:GLA_G + 2, :], b.tmp2[:])
        to_channels(k, b.Y, out, V.gla_norm_2, z[:, GLA_G:GLA_G + 2, :])


def attention(k, products, scale, mask, v, forget, out):
    with buffers_scope(k, vtok=[2, 256], F=[4, 256], lg=[4, 256], top=[4], total=[4], PT=[2, 4, P], Y=[2, 256]) as b:
        to_tokens(k, [(v[:, j, :], b.vtok[:, :, P * j:P * j + P]) for j in range(2)])
        if forget is not None:
            with k.stage() as block:

                @block.tensor
                def _(pe):
                    for h in range(4):
                        for m in range(2):
                            at = 256 * h + P * m
                            for i in range(m + 1):
                                mm = pe.matmul(k.psum[:, at:at + P], forget[:, i, h:h + 1].broadcast_to([P, P]),
                                               k.upto if i == m else k.ones, start=(i == 0), stop=(i == m))
                    mm.then_inc(k.multiplied.up(), 1)

                @block.vector
                def _(dve):
                    dve.wait_ge(k.multiplied.sem, k.multiplied.at(1))
                    dve.tensor_copy(b.F[:], heads4(k.psum[:, 0:1024])).then_inc(k.vec_step.up(), 1)

        for i in range(2):
            n = P * (i + 1)
            toks, keys = slice(P * i, n), slice(0, n)
            with k.stage() as block:
                logits = k.psum[:, 0:4 * 256].rearrange("p (h s) -> p h s", h=4)[:, :, 0:n]
                lg = b.lg[:, :, 0:n]
                marks = {}

                @block.vector
                def _(dve):
                    chain = chained(k, dve)
                    dve.wait_ge(k.multiplied.sem, k.multiplied.at(1))
                    if forget is None:
                        chain(dve.tensor_scalar(lg, logits, scale, None, ALU.mult))
                    else:
                        chain(dve.scalar_tensor_tensor(lg, logits, scale, b.F[:, :, 0:n], ALU.mult, ALU.subtract))
                    chain(dve.tensor_tensor(b.lg[:, :, toks], b.lg[:, :, toks], for_heads(mask, 4), ALU.add))
                    chain(dve.tensor_reduce(b.top[:], lg, AXX, ALU.max))
                    chain(dve.tensor_tensor(lg, lg, per_head(b.top[:], n), ALU.subtract))
                    marks["less"] = k.vec_step.count
                    dve.wait_ge(k.act_step.sem, k.act_step.at(1))
                    chain(dve.tensor_reduce(b.total[:], lg, AXX, ALU.add))
                    chain(dve.reciprocal(b.total[:], b.total[:]))
                    dve.wait_ge(k.multiplied.sem, k.multiplied.at(3))
                    y = heads4(b.Y[:, i, :])
                    chain(dve.tensor_tensor(y, heads4(k.bank(4, 256)), per_head(b.total[:], 64), ALU.mult))

                @block.scalar
                def _(act):
                    act.wait_ge(k.vec_step.sem, marks["less"])
                    act.activation(lg, lg, ACT.Exp).then_inc(k.act_step.up(), 1)
                    act.wait_ge(k.multiplied.sem, k.multiplied.at(2))
                    act.activation(b.PT[:, 0:i + 1], k.psum[:, 1024:1024 + 512 * (i + 1)].rearrange("p (m h t) -> p m h t", h=4, t=P),
                                   ACT.Copy).then_inc(k.act_step.up(), 1)

                @block.tensor
                def _(pe):
                    for h in range(4):
                        pairs = products(h, toks, keys)
                        for a, (q, kk) in enumerate(pairs):
                            mm = pe.matmul(logits[:, h, :], q, kk, start=(a == 0), stop=(a == len(pairs) - 1))
                    mm.then_inc(k.multiplied.up(), 1)
                    pe.wait_ge(k.act_step.sem, k.act_step.at(1))
                    for m in range(i + 1):
                        for h in range(4):
                            at = 1024 + 512 * m + P * h
                            mm = pe.transpose(k.psum[:, at:at + P], b.lg[:, h, P * m:P * m + P], k.ident)
                    mm.then_inc(k.multiplied.up(), 1)
                    pe.wait_ge(k.act_step.sem, k.act_step.at(2))
                    for h in range(4):
                        for m in range(i + 1):
                            mm = pe.matmul(k.bank(4)[:, 64 * h:64 * h + 64], b.PT[:, m, h, :], b.vtok[:, m, 64 * h:64 * h + 64],
                                           start=(m == 0), stop=(m == i))
                    mm.then_inc(k.multiplied.up(), 1)

        to_channels(k, b.Y, out)


def fox_branch(k, z, forget, out):
    with buffers_scope(k, qm=[4, 256]) as b:
        with k.stage() as block:

            @block.vector
            def _(dve):
                for h in range(4):
                    dve.tensor_scalar(b.qm[:, h, :], z[:, FOX_Q + h // 2, :], k.half_mask[h % 2], None, ALU.mult).then_inc(k.vec_step.up(), 1)

        attention(k, lambda h, toks, keys: [(b.qm[:, h, toks], z[:, FOX_K + h // 2, keys])], 64 ** -0.5, k.causal,
                  z[:, FOX_V:FOX_V + 2, :], forget, out)


def mla_branch(k, V, z, dram, gates, out):
    with buffers_scope(k, cq=[2, 256], ckv=[1, 256], q=[4, 256], kv=[4, 256], rot=[256], qm=[4, 256], qpm=[4, 256]) as b:
        channel_norm(k, z[:, CQ:CQ + 2, :], b.cq[:], 2, 256, 1e-6, V.mla_q_norm_2)
        channel_norm(k, z[:, CKV:CKV + 1, :], b.ckv[:], 1, 128, 1e-6, V.mla_kv_norm_2)
        gemm(k, weight(dram.mla_q_up, 2), lambda j: b.cq[:, j, :], b.q[:], weight(dram.mla_kv_up, 1))
        gemm(k, weight(dram.mla_kv_up, 1), lambda j: b.ckv[:, j, :], b.kv[:], gates[0])
        with k.stage() as block:

            @block.tensor
            def _(pe):
                pe.matmul(k.bank(0, 256), k.turn, b.q[:, 2, :], start=True, stop=True)
                pe.matmul(k.bank(1, 256), k.turn, z[:, KPE, :], start=True, stop=True).then_inc(k.multiplied.up(), 1)

            @block.vector
            def _(dve):
                chain = chained(k, dve)
                dve.wait_ge(k.multiplied.sem, k.multiplied.at(1))
                for n, t in enumerate((b.q[:, 2, :], z[:, KPE, :])):
                    chain(dve.tensor_tensor(b.rot[:], k.bank(n, 256), k.sin, ALU.mult))
                    chain(dve.tensor_tensor(t, t, k.cos, ALU.mult))
                    chain(dve.tensor_tensor(t, t, b.rot[:], ALU.add))
                for h in range(4):
                    chain(dve.tensor_scalar(b.qm[:, h, :], b.q[:, h // 2, :], k.half_mask[h % 2], None, ALU.mult))
                    chain(dve.tensor_scalar(b.qpm[:, h, :], b.q[:, 2, :], k.quarter_mask[h], None, ALU.mult))

        attention(k, lambda h, toks, keys: [(b.qm[:, h, toks], b.kv[:, h // 2, keys]), (b.qpm[:, h, toks], z[:, KPE, keys])],
                  96 ** -0.5, k.chunk_causal, b.kv[:, 2:4, :], None, out)


def second_block(k, dram, x):
    with ExitStack() as mem:
        lay = Layout(VECTORS2)
        c = buffers(k, mem, vec=[lay.width], rows=[12], gate_up=[P], h=[8, 256], branches=[4, 2, 256])
        load(k, (c.vec[:], dram.vectors2), (c.rows[:], dram.rows2), (c.gate_up[0:16, :], dram.gate_up))
        V = names(**{name: c.vec[:, a:z] for name, (a, z) in lay.at.items()})
        channel_norm(k, x[:], c.h[:], 8, 1024, 1e-6, V.norm_mix_pre_2)

        def rhs(t):
            return lambda j: t[:, j, :]

        gates = [weight(dram.w_gate_2[i], 8) for i in range(4)]
        ups = [weight(dram.w_branch_up_2[i], 2) for i in range(4)]
        w_out, w_mlp_in = weight(dram.w_out_2, 8), weight(dram.w_mlp_in_2, 8)
        with buffers_scope(k, z=[28, 256], rates=[2, 12], beta=[2, 4], y=[2, 8], tmp=[2, 8], ea=[4]) as s:
            gemm(k, weight(dram.w_in_2, 8), rhs(c.h), s.z[:], weight(dram.mla_q_up, 2))
            with k.stage() as block:

                @block.tensor
                def _(pe):
                    for i in range(2):
                        mm = pe.transpose(k.psum[:, P * i:P * i + P], s.z[:, SMALL, P * i:P * i + P], k.ident)
                    mm.then_inc(k.multiplied.up(), 1)

                @block.scalar
                def _(act):
                    act.wait_ge(k.vec_step.sem, k.vec_step.at(1))
                    turned = k.psum[:, 0:256].rearrange("p (i c) -> p i c", i=2)
                    act.activation(s.beta[:], turned[:, :, 0:4], ACT.Sigmoid).then_inc(k.act_step.up(), 1)
                    act.activation(s.ea[:], c.rows[:, 8:12], ACT.Exp).then_inc(k.act_step.up(), 1)

                @block.vector
                def _(dve):
                    chain = chained(k, dve)
                    dve.wait_ge(k.multiplied.sem, k.multiplied.at(1))
                    turned = k.psum[:, 0:256].rearrange("p (i c) -> p i c", i=2)
                    bias = c.rows[:, 0:8].unsqueeze(1).broadcast_to([P, 2, 8])
                    chain(dve.tensor_tensor(s.y[:], turned[:, :, 4:12], bias, ALU.add))
                    chain(dve.tensor_scalar(s.y[:, :, 4:8], s.y[:, :, 4:8], -1.0, None, ALU.mult))

            softplus(k, s.y[:], s.tmp[:], s.y[:], -1.0)
            with k.stage() as block:

                @block.vector
                def _(dve):
                    g = s.y[:, :, 0:4]
                    dve.tensor_tensor(g, g, s.ea[:].unsqueeze(1).broadcast_to([P, 2, 4]), ALU.mult).then_inc(k.vec_step.up(), 1)

            small = names(beta=s.beta, g=s.y[:, :, 0:4])
            delta_branch(k, V, s.z, small, c.branches[:, 0])
            mla_branch(k, V, s.z, dram, gates, c.branches[:, 1])
            gla_branch(k, V, s.z, c.gate_up[0:16, :], c.branches[:, 2])
            fox_branch(k, s.z, s.y[:, :, 4:8], c.branches[:, 3])
        with buffers_scope(k, merged=[8, 256], gate=[8, 256], up=[8, 256]) as s:
            for i in range(4):
                gemm(k, gates[i], rhs(c.h), s.gate[:], ups[i])
                gemm(k, ups[i], lambda j: c.branches[:, i, j, :], s.up[:], gates[i + 1] if i < 3 else w_out)
                with k.stage() as block:

                    @block.scalar
                    def _(act):
                        for j in range(8):
                            ins = act.activation(s.gate[:, j, :], s.gate[:, j, :], ACT.Sigmoid, bias=V.b_gate_2[:, 8 * i + j:8 * i + j + 1])
                        ins.then_inc(k.act_step.up(), 1)

                    @block.vector
                    def _(dve):
                        chain = chained(k, dve)
                        dve.wait_ge(k.act_step.sem, k.act_step.at(1))
                        if i == 0:
                            chain(dve.tensor_tensor(s.merged[:], s.gate[:], s.up[:], ALU.mult))
                        else:
                            chain(dve.tensor_tensor(s.up[:], s.gate[:], s.up[:], ALU.mult))
                            chain(dve.tensor_tensor(s.merged[:], s.merged[:], s.up[:], ALU.add))

            gemm(k, w_out, rhs(s.merged), s.up[:], w_mlp_in)
            channel_norm(k, s.up[:], s.gate[:], 8, 1024, 1e-6, V.norm_mix_post_2)
            add_to(k, x[:], s.gate[:])
        channel_norm(k, x[:], c.h[:], 8, 1024, 1e-6, V.norm_mlp_pre_2)
        with buffers_scope(k, u=[32, 256], y=[8, 256], n=[8, 256]) as s:
            gemm(k, w_mlp_in, rhs(c.h), s.u[:])
            with k.stage() as block:

                @block.vector
                def _(dve):
                    dve.scalar_tensor_tensor(s.u[:], s.u[:], 0.0, s.u[:], ALU.max, ALU.mult).then_inc(k.vec_step.up(), 1)

            gemm(k, weight(dram.w_mlp_out_2, 32), rhs(s.u), s.y[:], own_ring=True)
            channel_norm(k, s.y[:], s.n[:], 8, 1024, 1e-6, V.norm_mlp_post_2)
            add_to(k, x[:], s.n[:])


def add_to(k, x, y):
    with k.stage() as block:

        @block.vector
        def _(dve):
            dve.tensor_tensor(x, x, y, ALU.add).then_inc(k.vec_step.up(), 1)


def layout_second(i):
    i = {n: a[0] for n, a in i.items() if n.endswith("_2")}
    a = {}
    at = np.cumsum([0, 768, 256, 4, 4, 256, 128, 32, 128, 128, 256, 256, 16, 256, 256, 256, 4])
    part = [i["w_in_2"][:, at[n]:at[n + 1]] for n in range(16)]
    qkv, dz, db, da, cq, ckv, kpe, gq, gk, gv, gg, lr, fq, fk, fv, ff = part
    w = np.concatenate([qkv, dz, cq, ckv, np.tile(kpe, (1, 4)), gq, gk, gv, gg, padded_to(lr, P), fq, fk, fv,
                        padded_to(np.concatenate([db, da, ff], axis=1), 3 * P)], axis=1)
    a["w_in_2"] = blocked(w, P)
    a["vectors2"] = np.concatenate([columns(np.tile(i[n], 2) if n in ("dn_norm_2", "gla_norm_2") else i[n]) for n in VECTORS2], axis=1)
    a["rows2"] = np.ascontiguousarray(np.broadcast_to(np.concatenate([i[n] for n in ROWS2])[None, :], (P, 12)))
    a["gate_up"] = i["gla_w_gate_up_2"]
    q = i["mla_w_q_up_2"].reshape(256, 4, 96)
    a["mla_q_up"] = blocked(padded_to(np.concatenate([q[:, :, :64].reshape(256, 256), q[:, :, 64:].reshape(256, 128)], axis=1), 4 * P), P)
    kv = i["mla_w_kv_up_2"].reshape(128, 4, 128)
    a["mla_kv_up"] = blocked(np.concatenate([kv[:, :, :64].reshape(128, 256), kv[:, :, 64:].reshape(128, 256)], axis=1), P)
    a["w_gate_2"] = np.stack([blocked(w, P) for w in i["w_gate_2"]])
    a["w_branch_up_2"] = np.stack([blocked(w, P) for w in i["w_branch_up_2"]])
    a["w_out_2"] = blocked(i["w_out_2"], P)
    a["w_mlp_in_2"] = blocked(i["w_mlp_in_2"], P)
    a["w_mlp_out_2"] = blocked(i["w_mlp_out_2"], P)
    return a


def constants():
    p, f = np.arange(P)[:, None], np.arange(P)[None, :]
    same, same8 = p // 64 == f // 64, p // 8 == f // 8
    t = np.arange(512)[None, :]
    freq = 1.0 / (10000.0 ** (np.arange(0, 32, 2, dtype=np.float32) / np.float32(32)))
    angle = (np.arange(256, dtype=np.float32)[:, None] * freq[None, :].astype(np.float32)).astype(np.float32)
    angle = np.concatenate([angle, angle], axis=1).T
    turn = np.zeros((P, P))
    for i in range(P):
        turn[i + 16 if i % 32 < 16 else i - 16, i] = -1.0 if i % 32 < 16 else 1.0
    table = {
        "ident": p == f, "ones": p * f >= 0, "blocks64": same,
        "up": same & (p < f), "lo": same & (p > f), "up_incl": same & (p <= f), "lo_incl": same & (p >= f),
        "up8": same8 & (p < f), "lo8": same8 & (p > f), "up_far": same & ~same8 & (p < f), "lo_far": same & ~same8 & (p > f),
        "upto": p <= f, "chunk0": (p < 64) & (f >= 0), "chunk1": (p >= 64) & (f >= 0),
        "causal": np.where(f <= p, 0.0, -1e30), "chunk_causal": np.where(f // 64 <= p // 64, 0.0, -1e30),
        "turn": turn, "halves": np.concatenate([p < 64, p >= 64], axis=1),
        "quarters": np.concatenate([p // 32 == i for i in range(4)], axis=1),
        "segments": np.broadcast_to(t % 64 != 0, (P, 512)), "iota16": np.broadcast_to(np.arange(16)[None, :], (P, 16)),
        "cos": np.tile(np.cos(angle), (4, 1)), "sin": np.tile(np.sin(angle), (4, 1)),
    }
    return {n: np.asarray(a, np.float32) for n, a in table.items()}


class Layout:

    def __init__(self, widths):
        self.at, n = {}, 0
        for name, w in widths.items():
            self.at[name] = (n, n + w)
            n += w
        self.width = n


VECTORS = {"norm1_g": 8, "norm2_g": 8, "shift_mu": 56, "w0": 16, "a0": 16, "k_k": 8, "k_a": 8, "r_k": 8, "lnx_g": 8, "lnx_b": 8,
           "conv_w": 248, "cnorm_g": 8, "cnorm_b": 8, "gate_b": 16, "ada_b": 48}


def load_layer(k, mem, l, dram):
    lay = Layout(VECTORS)
    b = buffers(k, mem, vec=[lay.width], w2=[1024], a2=[1024], g2=[2, 1024])
    load(k, (b.vec[:], dram.vectors[l]), (b.w2[:], dram.w2[l]), (b.a2[:], dram.a2[l]), (b.g2[:], dram.g2[l]))
    L = names(**{name: b.vec[:, a:z] for name, (a, z) in lay.at.items()})
    L.mu = L.shift_mu.rearrange("p (d j) -> p d j", d=2)
    L.w2, L.a2, L.g2 = b.w2, b.a2, b.g2
    return L


def first_block(k, dram, x, xc):
    nc = k.nc
    with ExitStack() as mem:
        mods = buffers(k, mem, mods=[2, 48, 2]).mods
        with buffers_scope(k, c=[8, 2], sig=[8, 2]) as s:
            load(k, (s.c[:], dram.c))
            with k.stage() as block:

                @block.scalar
                def _(act):
                    act.activation(s.sig[:], s.c[:], ACT.Sigmoid).then_inc(k.act_step.up(), 1)

                @block.vector
                def _(dve):
                    dve.wait_ge(k.act_step.sem, k.act_step.at(1))
                    dve.tensor_tensor(s.c[:], s.c[:], s.sig[:], ALU.mult).then_inc(k.vec_step.up(), 1)

            modulation_rows(k, dram.ada_w, s.c, mods[:].rearrange("p l j c -> p (l j) c"))
        states = [buffers(k, mem, state=[8, P]).state for d in range(2)]
        for l in range(2):
            with ExitStack() as layer_mem:
                L = load_layer(k, layer_mem, l, dram)
                m = buffers(k, layer_mem, mod=[2, 48])
                with k.stage() as block:

                    @block.vector
                    def _(dve):
                        chain = chained(k, dve)
                        for d in range(2):
                            chain(dve.memset(states[d][:], 0.0))
                        for c in range(2):
                            chain(dve.tensor_tensor(m.mod[:, c, :], mods[:, l, :, c], L.ada_b, ALU.add))
                            for at, gain in ((8, L.norm1_g), (32, L.norm2_g)):
                                part = m.mod[:, c, at:at + 8]
                                chain(dve.scalar_tensor_tensor(part, part, 1.0, gain, ALU.add, ALU.mult))


                def modulation(c):
                    shift1, scale1, gate1, shift2, scale2, gate2 = (m.mod[:, c, 8 * i:8 * i + 8] for i in range(6))
                    return names(shift1=shift1, scale1=scale1, gate1=gate1, shift2=shift2, scale2=scale2, gate2=gate2)

                last = l == 1
                token_mixer(k, L, l, dram, xc[:], modulation(1), states, [(15, 0)] + [(r, r - 15) for r in range(31) if r != 15],
                            not last, weight(dram.w_in[l, 28:44], 8))
                k.dump(f"xc_mix{l}", xc[:])
                token_mixer(k, L, l, dram, x[:], modulation(0), states, [(15, 0)] + [(r, 64 * (r - 15)) for r in range(12, 19) if r != 15],
                            True, weight(dram.w_q[l], 8))
                k.dump(f"x_mix{l}", x[:])
                mx, mc = modulation(0), modulation(1)
                after = weight(dram.w_in_2, 8) if last else weight(dram.w_q[l], 8)
                peer(k, l, dram, x[:], mx, after)
                k.dump(f"x_peer{l}", x[:])
                if not last:
                    peer(k, l, dram, xc[:], mc, weight(dram.w_in[1, 8:28], 8))


def program(nc, dram, dump=None):
    with ExitStack() as ctx:
        k = Core(nc, ctx)
        k.dump = dump(k) if dump else lambda name, ap: None
        lay = Layout({n: a.shape[1] for n, a in constants().items()})
        table = ctx.enter_context(nc.sbuf_tensor("constants", [P, lay.width], F32))
        (k.ident, k.ones, k.blocks64, k.up, k.lo, k.up_incl, k.lo_incl, k.up8, k.lo8, k.up_far, k.lo_far, k.upto, k.chunk0, k.chunk1,
         k.causal, k.chunk_causal, k.turn, k.halves, k.quarters, k.segments, k.iota16, k.cos, k.sin) = (
            table[:, a:z] for a, z in lay.at.values())
        k.half_mask = [k.halves[:, i:i + 1] for i in range(2)]
        k.quarter_mask = [k.quarters[:, i:i + 1] for i in range(4)]
        k.ring = ctx.enter_context(k.sbuf("weight_ring", [SLOTS_W, 8 * P]))
        x = ctx.enter_context(nc.sbuf_tensor("x_tokens", [P, 8, 256], F32))
        with nc.sbuf_tensor("context_tokens", [P, 8, 256], F32) as xc:
            load(k, (table[:], dram.constants), (x[:], dram.x), (xc[:], dram.ctx))
            first_block(k, dram, x, xc)
        channel_norm(k, x[:], x[:], 8, 1024, 1e-6, k_final(k, ctx, dram))
        k.dump("x_first", x[:])
        second_block(k, dram, x)
        with buffers_scope(k, rows=[2, 1024]) as s, k.stage() as block:

            @block.tensor
            def _(pe):
                for i in range(2):
                    for j in range(8):
                        mm = pe.transpose(k.psum[:, 1024 * i + P * j:1024 * i + P * j + P], x[:, j, P * i:P * i + P], k.ident)
                mm.then_inc(k.multiplied.up(), 1)

            @block.scalar
            def _(act):
                act.wait_ge(k.multiplied.sem, k.multiplied.at(1))
                act.activation(s.rows[:], k.psum[:, 0:2048].rearrange("p (i c) -> p i c", i=2), ACT.Copy).then_inc(k.act_step.up(), 1)

            @block.sync
            def _(sp):
                sp.wait_ge(k.act_step.sem, k.act_step.at(1))
                sp.dma_start(dram.out.rearrange("b (i p) c -> p (b i) c", p=P), s.rows[:]).then_inc(k.stored.up(16), 16)
                sp.wait_ge(k.stored.sem, k.stored.count)


def k_final(k, ctx, dram):
    g = ctx.enter_context(k.nc.sbuf_tensor("final_g", [P, 8], F32))
    load(k, (g[:], dram.final_g))
    return g[:]




def columns(v):
    v = np.asarray(v)
    n = -(-v.shape[-1] // P) * P
    out = np.zeros((*v.shape[:-1], n), v.dtype)
    out[..., :v.shape[-1]] = v
    return np.ascontiguousarray(out.reshape(-1, P).T)


def blocked(w, cols):
    w = np.asarray(w)
    k, n = w.shape
    kt = -(-k // P)
    padded = np.zeros((kt * P, -(-n // cols) * cols), w.dtype)
    padded[:k, :n] = w
    return np.ascontiguousarray(padded.reshape(kt, P, -1, cols).transpose(2, 1, 0, 3).reshape(-1, P, kt * cols))


def padded_to(w, n):
    out = np.zeros((w.shape[0], n), w.dtype)
    out[:, :w.shape[1]] = w
    return out


def layout(i):
    i = {n: np.asarray(a) for n, a in i.items()}
    a = {}
    a["x"] = np.ascontiguousarray(i["x"][0].T.reshape(8, P, 256).transpose(1, 0, 2))
    a["ctx"] = np.ascontiguousarray(i["ctx"][0].T.reshape(8, P, 256).transpose(1, 0, 2))
    a["c"] = np.ascontiguousarray(np.stack([columns(i["c"][0]), columns(i["c_ctx"])], axis=2))
    a["constants"] = np.concatenate(list(constants().values()), axis=1)
    a["final_g"] = columns(i["final_g"])
    a["vectors"] = np.stack([np.concatenate([columns(i[n][l].reshape(-1) if n == "r_k" else i[n][l]) for n in VECTORS], axis=1) for l in range(2)])
    a["ada_w"] = np.concatenate([blocked(i["ada_w"][l], 512) for l in range(2)])
    a["w_in"] = np.stack([np.concatenate([blocked(i["w_in"][l][:, :3488], P), blocked(i["w_in"][l][:, 3488:], P)]) for l in range(2)])
    a["w2"] = np.ascontiguousarray(i["w2"].reshape(2, P, 1024))
    a["a2"] = np.ascontiguousarray(i["a2"].reshape(2, P, 1024))
    g2 = np.zeros((2, 256, 1024), np.float32)
    g2[:, :160] = i["g2"]
    a["g2"] = np.ascontiguousarray(g2.reshape(2, 2, P, 1024).transpose(0, 2, 1, 3))
    for n in ("w_oA", "w_oB", "w_out", "w_q"):
        a[n] = np.stack([blocked(i[n][l], P) for l in range(2)])
    a["sub_keys"] = np.ascontiguousarray(i["sub_keys"].transpose(0, 4, 1, 2, 3).reshape(2, P, 16, P))
    a["peer_u"] = i["peer_u"].reshape(-1, 1024)
    a["peer_v"] = i["peer_v"].reshape(-1, 1024)
    a.update(layout_second(i))
    return a


def kernel(**inputs):
    import concourse.bacc as bacc
    from concourse.bass_utils import run_bass_kernel_spmd

    nc = bacc.Bacc("TRN2", target_bir_lowering=False, num_devices=1)
    arrays = {f"in_{n}": a for n, a in layout(inputs).items()}
    dram = names(**{n[3:]: nc.dram_tensor(n, a.shape, mybir.dt.from_np(a.dtype), kind="ExternalInput").ap()
                              for n, a in arrays.items()})
    dram.out = nc.dram_tensor("out_tokens", (1, 256, 1024), F32, kind="ExternalOutput").ap()
    program(nc, dram)
    return run_bass_kernel_spmd(nc, [arrays], core_ids=[0]).results[0]["out_tokens"]
```

```python
import math
from contextlib import ExitStack, contextmanager

import numpy as np

import concourse.bass as bass
from concourse import mybir

F32 = mybir.dt.float32
U32 = mybir.dt.uint32
ACT = mybir.ActivationFunctionType
ALU = mybir.AluOpType
AXX = mybir.AxisListType.X
P = 128


def names(**values):
    return type("Names", (), values)()


class Signal:

    def __init__(self, sem):
        self.sem, self.count, self.mark = sem, 0, 0

    def up(self, by=1):
        self.count += by
        return self.sem

    def at(self, n):
        return self.mark + n


class Core:

    def __init__(self, nc, ctx):
        self.nc, self.ctx = nc, ctx
        self.signals, self.made = [], 0
        self.fetched = False
        self.job = None
        self.psum = ctx.enter_context(nc.psum_tensor("psum", [P, 4096], F32))
        self.weights = [self.counter(f"weights_loaded{i}") for i in range(SLOTS_W)]
        self.multiplied = self.counter("multiplied")
        self.low_rank = self.counter("low_rank_multiplied")
        self.evacuated = self.counter("evacuated")
        self.vec_step = self.counter("vec_step")
        self.act_step = self.counter("act_step")
        self.pool_step = self.counter("pool_step")
        self.staged = self.counter("numbers_staged")
        self.weights_staged = self.counter("weights_staged")
        self.slot_free = self.counter("slot_free")
        self.row_used = self.counter("row_used")
        self.dots_kept = self.counter("dots_kept")
        self.weighted = self.counter("weighted")
        self.gathered = [self.counter(f"row_gathered{j}") for j in range(8)]
        self.loaded = self.counter("loaded")
        self.stored = self.counter("stored")

    def sbuf(self, name, shape, dtype=F32):
        self.made += 1
        return self.nc.sbuf_tensor(f"{name}_{self.made}", [P, *shape], dtype)

    def counter(self, name):
        s = Signal(self.ctx.enter_context(self.nc.semaphore(name)))
        self.signals.append(s)
        return s

    @contextmanager
    def stage(self):
        self.phase()
        with self.nc.Block(no_gpsimd_drain=True) as block:
            yield block

    def phase(self):
        for s in self.signals:
            s.mark = s.count

    def bank(self, i, n=512):
        return self.psum[:, 512 * i:512 * i + n]


SLOTS_W = 4


def fetch(k, sp, w, n, ring):
    slot = n % SLOTS_W
    sp.dma_start(ring[:, slot, 0:w.kt * P], w.ap[n]).then_inc(k.weights[slot].sem, 16)


def weight(ap, kt):
    return names(ap=ap, blocks=ap.shape[0], kt=kt)


def gemm(k, w, rhs, dst, then=None, own_ring=False, tokens=256, shift=None, beside=None, sigmoid=None, after=()):
    rounds, extra = divmod(w.blocks, SLOTS_W)
    assert extra == 0
    with ExitStack() as mem:
        ring = mem.enter_context(k.sbuf("weight_ring", [SLOTS_W, w.kt * P])) if own_ring else k.ring
        fetched = not own_ring and k.fetched
        wl, mu, ev = k.weights, k.multiplied, k.evacuated
        if shift is not None:
            steps = mem.enter_context(k.sbuf("token_steps", [2, tokens + 1]))
        expert_weights(k)
        with k.stage() as block:
            landed = [s.at(0) if fetched else s.at(16) for s in wl]

            @block.sync
            def _(sp):
                if not fetched:
                    for n in range(SLOTS_W):
                        fetch(k, sp, w, n, ring)
                        wl[n].up(16)
                if rounds > 1:
                    with sp.Fori(1, rounds) as i:
                        for slot in range(SLOTS_W):
                            sp.wait_ge(mu.sem, i * SLOTS_W + (mu.at(slot + 1) - SLOTS_W))
                            sp.dma_start(ring[:, slot, 0:w.kt * P], w.ap[i * SLOTS_W + slot]).then_inc(wl[slot].sem, 16)
                for slot in range(SLOTS_W):
                    wl[slot].up(16 * (rounds - 1))
                if then is not None:
                    for slot in range(SLOTS_W):
                        sp.wait_ge(mu.sem, mu.at((rounds - 1) * SLOTS_W + slot + 1))
                        fetch(k, sp, then, slot, ring)
                        wl[slot].up(16)

            @block.tensor
            def _(pe):
                def multiply(i, slot, first):
                    pe.wait_ge(wl[slot].sem, i * 16 + landed[slot])
                    if not first:
                        pe.wait_ge(ev.sem, i * SLOTS_W + (ev.at(slot + 1) - SLOTS_W))
                    for j in range(w.kt):
                        mm = pe.matmul(k.bank(slot, tokens), ring[:, slot, j * P:j * P + P], rhs(j), start=(j == 0), stop=(j == w.kt - 1))
                    mm.then_inc(mu.sem, 1)

                for slot in range(SLOTS_W):
                    multiply(0, slot, True)
                if rounds > 1:
                    with pe.Fori(1, rounds) as i:
                        for slot in range(SLOTS_W):
                            multiply(i, slot, False)

            @block.scalar
            def _(act):
                with act.Fori(0, rounds) as i:
                    for slot in range(SLOTS_W):
                        act.wait_ge(mu.sem, i * SLOTS_W + mu.at(slot + 1))
                        out, product = dst[:, bass.ds(i * SLOTS_W + slot, 1), :], k.bank(slot, tokens).unsqueeze(1)
                        if sigmoid is None:
                            ins = act.activation(out, product, ACT.Copy)
                        else:
                            ins = act.activation(out, product, ACT.Sigmoid, bias=sigmoid[:, bass.ds(i * SLOTS_W + slot, 1)])
                        ins.then_inc(ev.sem, 1)

            if beside is not None:

                @block.vector
                def _(dve):
                    beside(dve)
                    use_rows(k, dve, w.blocks)

            elif shift is None:

                @block.vector
                def _(dve):
                    use_rows(k, dve, 7 * w.blocks // 4)
                    if not after:
                        return
                    with dve.Fori(0, rounds) as i:
                        for slot in range(SLOTS_W):
                            def block_of(t):
                                return t[:, bass.ds(i * SLOTS_W + slot, 1), :].rearrange("p n t -> p (n t)")

                            block_of.column = bass.ds(i * SLOTS_W + slot, 1)
                            dve.wait_ge(ev.sem, i * SLOTS_W + ev.at(slot + 1))
                            for n, step in enumerate(after):
                                if n:
                                    dve.wait_ge(k.vec_step.sem, i * (len(after) * SLOTS_W) + k.vec_step.at(len(after) * slot + n))
                                step(dve, block_of).then_inc(k.vec_step.sem, 1)

                k.vec_step.up(len(after) * w.blocks)

            if shift is not None:

                @block.vector
                def _(dve):
                    up = k.vec_step

                    def shift_block(i, slot):
                        block_n, e = i * SLOTS_W + slot, steps[:, slot % 2, :]
                        z = dst[:, bass.ds(block_n, 1), :].rearrange("p n t -> p (n t)")
                        dve.wait_ge(ev.sem, i * SLOTS_W + ev.at(slot + 1))
                        dve.tensor_tensor(e[:, 1:tokens], dst[:, bass.ds(block_n, 1), 1:tokens].rearrange("p n t -> p (n t)"),
                                          dst[:, bass.ds(block_n, 1), 0:tokens - 1].rearrange("p n t -> p (n t)"), ALU.subtract).then_inc(up.sem, 1)
                        dve.tensor_copy(e[:, 0:1], dst[:, bass.ds(block_n, 1), 0:1].rearrange("p n t -> p (n t)")).then_inc(up.sem, 1)
                        dve.tensor_scalar(e[:, tokens:tokens + 1], dst[:, bass.ds(block_n, 1), tokens - 1:tokens].rearrange("p n t -> p (n t)"),
                                          -1.0, None, ALU.mult).then_inc(up.sem, 1)
                        for n in range(2):
                            dve.wait_ge(up.sem, i * (5 * SLOTS_W) + up.at(5 * slot + 3 + n))
                            dve.scalar_tensor_tensor(z, e[:, n:n + tokens], shift[:, n, bass.ds(block_n, 1)], z, ALU.mult, ALU.subtract
                                                     ).then_inc(up.sem, 1)

                    use_rows(k, dve, 3 * w.blocks // 4)
                    with dve.Fori(0, rounds) as i:
                        for slot in range(SLOTS_W):
                            shift_block(i, slot)

                k.vec_step.up(5 * w.blocks)

            @block.gpsimd
            def _(pool):
                fetch_rows(k, pool)

            mu.up(w.blocks)
            ev.up(w.blocks)
            if not own_ring:
                k.fetched = then is not None


def modulation_rows(k, w, c, out):
    blocks, depth = w.shape[0], 4
    with k.sbuf("ada_ring", [depth, 4096]) as ring, k.sbuf("ada_rows", [blocks * 512]) as rows:
        mu, ev, wl = k.multiplied, k.evacuated, k.weights
        rounds = blocks // depth
        with k.stage() as block:

            @block.sync
            def _(sp):
                for slot in range(depth):
                    sp.dma_start(ring[:, slot, :], w[slot]).then_inc(wl[slot].sem, 16)
                with sp.Fori(1, rounds) as i:
                    for slot in range(depth):
                        sp.wait_ge(mu.sem, i * depth + (mu.at(slot + 1) - depth))
                        sp.dma_start(ring[:, slot, :], w[i * depth + slot]).then_inc(wl[slot].sem, 16)

            @block.tensor
            def _(pe):
                def multiply(i, slot, first):
                    pe.wait_ge(wl[slot].sem, i * 16 + wl[slot].at(16))
                    if not first:
                        pe.wait_ge(ev.sem, i * depth + (ev.at(slot + 1) - depth))
                    for j in range(8):
                        mm = pe.matmul(k.bank(slot)[0:2, :], c[:, j, :], ring[:, slot, 512 * j:512 * j + 512], start=(j == 0), stop=(j == 7))
                    mm.then_inc(mu.sem, 1)

                for slot in range(depth):
                    multiply(0, slot, True)
                with pe.Fori(1, rounds) as i:
                    for slot in range(depth):
                        multiply(i, slot, False)

            @block.scalar
            def _(act):
                with act.Fori(0, rounds) as i:
                    for slot in range(depth):
                        act.wait_ge(mu.sem, i * depth + mu.at(slot + 1))
                        act.activation(rows[0:2, bass.ds((i * depth + slot) * 512, 512)], k.bank(slot)[0:2, :], ACT.Copy).then_inc(ev.sem, 1)

            for slot in range(depth):
                wl[slot].up(16 * rounds)
            mu.up(blocks)
            ev.up(blocks)

        with k.stage() as block:

            @block.tensor
            def _(pe):
                for n in range(blocks * 4):
                    mm = pe.transpose(k.bank(0)[:, 2 * n:2 * n + 2], rows[0:2, P * n:P * n + P], k.ident[0:2, 0:2])
                mm.then_inc(mu.up(), 1)

            @block.vector
            def _(dve):
                dve.wait_ge(mu.sem, mu.at(1))
                dve.tensor_copy(out, k.bank(0, blocks * 8).rearrange("p (n c) -> p n c", c=2)).then_inc(k.vec_step.up(), 1)


def chained(k, dve):
    step = k.vec_step

    def chain(instruction):
        instruction.then_inc(step.up(), 1)
        dve.wait_ge(step.sem, step.count)

    return chain


def over_tokens(column, tiles, tokens):
    return column.unsqueeze(2).broadcast_to([P, tiles, tokens])


def over_tiles(row, tiles, tokens):
    return row.unsqueeze(1).broadcast_to([P, tiles, tokens])


def load(k, *pairs):
    with k.stage() as block:

        @block.sync
        def _(sp):
            for dst, src in pairs:
                sp.dma_start(dst, src).then_inc(k.loaded.up(16), 16)
            sp.wait_ge(k.loaded.sem, k.loaded.count)


def channel_norm(k, src, dst, tiles, width, eps, mul=None, add=None, center=False, tokens=256):
    nc = k.nc
    with (
        k.sbuf("squares", [tiles, tokens]) as squares,
        k.sbuf("row", [tokens]) as row,
        k.stage() as block,
    ):
        total, mean = k.bank(0, tokens), k.bank(1, tokens)
        marks = {}

        @block.vector
        def _(dve):
            chain = chained(k, dve)
            base = src
            use_rows(k, dve, 2 if center else 4)
            if center:
                dve.wait_ge(k.multiplied.sem, k.multiplied.at(1))
                chain(dve.tensor_scalar(row[:], mean, 1.0 / width, None, ALU.mult))
                chain(dve.tensor_tensor(dst, src, over_tiles(row[:], tiles, tokens), ALU.subtract))
                base = dst
            marks["centered"] = k.vec_step.count
            n = 2 if center else 1
            dve.wait_ge(k.multiplied.sem, k.multiplied.at(n))
            chain(dve.tensor_scalar(row[:], total, 1.0 / width, eps, ALU.mult, ALU.add))
            marks["variance"] = k.vec_step.count
            dve.wait_ge(k.act_step.sem, k.act_step.at(2))
            chain(dve.reciprocal(row[:], row[:]))
            for j in range(tiles):
                dve.tensor_tensor(dst[:, j, :], base[:, j, :], row[:], ALU.mult).then_inc(k.vec_step.up(), 1)
            marks["normed"] = k.vec_step.count

        @block.gpsimd
        def _(pool):
            fetch_rows(k, pool)

        @block.scalar
        def _(act):
            if center:
                act.wait_ge(k.vec_step.sem, marks["centered"])
            act.activation(squares[:], dst if center else src, ACT.Square).then_inc(k.act_step.up(), 1)
            act.wait_ge(k.vec_step.sem, marks["variance"])
            act.activation(row[:], row[:], ACT.Sqrt).then_inc(k.act_step.up(), 1)
            for j in range(tiles if mul is not None else 0):
                act.wait_ge(k.vec_step.sem, marks["normed"] - tiles + j + 1)
                act.activation(dst[:, j, :], dst[:, j, :], ACT.Identity, scale=mul[:, j:j + 1], bias=0.0 if add is None else add[:, j:j + 1]
                               ).then_inc(k.act_step.up(), 1)

        @block.tensor
        def _(pe):
            if center:
                for j in range(tiles):
                    mm = pe.matmul(mean, k.ones, src[:, j, :], start=(j == 0), stop=(j == tiles - 1))
                mm.then_inc(k.multiplied.up(), 1)
            pe.wait_ge(k.act_step.sem, k.act_step.at(1))
            for j in range(tiles):
                mm = pe.matmul(total, k.ones, squares[:, j, :], start=(j == 0), stop=(j == tiles - 1))
            mm.then_inc(k.multiplied.up(), 1)


def invert_unit_lower(k, block, groups, Ld, LdT, NT, temps, TT, ahead=None):
    E1, E2, E3, X = temps
    ident = k.ident


    def grp(t, g):
        return t[:, g]

    steps = [
        (LdT, Ld, None, E1),
        (Ld, LdT, None, E2),
        (E1, E2, None, E3),
        (E2, X, X, X),
        (E3, X, X, X),
        (X, None, None, TT),
        (NT, X, None, E1),
        (X, NT, None, E2),
        (E2, E1, None, E3),
        (E1, E2, None, Ld),
        (Ld, E3, None, LdT),
        (E1, TT, TT, TT),
        (E3, TT, TT, TT),
        (LdT, TT, TT, TT),
    ]

    def product(q, g):
        return k.bank((groups * q + g) % 4).rearrange("p (h c) -> p h c", h=4)

    copied, started = {}, {}
    on_scalar = range(0 if k.job is not None else 1, groups)

    @block.vector
    def _(dve):
        dve.wait_ge(k.vec_step.sem, k.vec_step.mark)
        for g in range(groups):
            dve.tensor_tensor(grp(X, g), grp(Ld, g), k.ident.unsqueeze(1).broadcast_to([P, 4, P]),
                              ALU.add).then_inc(k.vec_step.up(), 1)
            started[g] = k.vec_step.count
            copied[-1, g] = k.vec_step.sem, k.vec_step.mark
        for q, (_, _, added, out) in enumerate(steps):
            for g in range(groups):
                if g in on_scalar and added is None:
                    continue
                dve.wait_ge(k.multiplied.sem, k.multiplied.at(groups * q + g + 1))
                if added is None:
                    ins = dve.tensor_copy(grp(out, g), product(q, g))
                else:
                    ins = dve.tensor_tensor(grp(out, g), product(q, g), grp(added, g), ALU.add)
                ins.then_inc(k.vec_step.up(), 1)
                copied[q, g] = k.vec_step.sem, k.vec_step.count
            use_rows(k, dve, 1)

    @block.gpsimd
    def _(pool):
        fetch_rows(k, pool)

    @block.scalar
    def _(act):
        act.wait_ge(k.act_step.sem, k.act_step.mark)
        for q, (_, _, added, out) in enumerate(steps):
            for g in on_scalar:
                if added is None:
                    act.wait_ge(k.multiplied.sem, k.multiplied.at(groups * q + g + 1))
                    act.activation(grp(out, g), product(q, g), ACT.Copy).then_inc(k.act_step.up(), 1)
                    copied[q, g] = k.act_step.sem, k.act_step.count
            if q == 9 and ahead is not None:
                ahead.sigmoids(act)

    @block.tensor
    def _(pe):
        for q, (left, right, _, _) in enumerate(steps):
            for g in range(groups):
                sem, value = copied[q - 1, g]
                pe.wait_ge(sem, value)
                if right is X and q == 3:
                    pe.wait_ge(k.vec_step.sem, started[g])
                for h in range(4):
                    out = product(q, g)[:, h, :]
                    if right is None:
                        mm = pe.transpose(out, grp(left, g)[:, h, :], ident)
                    else:
                        mm = pe.matmul(out, grp(left, g)[:, h, :], grp(right, g)[:, h, :], start=True, stop=True)
                mm.then_inc(k.multiplied.up(), 1)
            if q == 9 and ahead is not None:
                ahead.low_rank(pe)


class Operands:

    def __init__(self, k, b, L, quarter, sweep, emit):
        self.k, self.b, self.L, self.quarter, self.sweep, self.emit = k, b, L, quarter, sweep, emit
        self.ways = [i ^ sweep for i in range(2)]
        self.tot, self.pc = b.tot[:, sweep], b.pc[:, sweep]
        self.done, self.first = {}, False

    def tiles(self, t, first=0):
        return t[:, first + 2 * self.quarter:first + 2 * self.quarter + 2, :]

    def parts(self):
        for i in range(2):
            for j in range(2):
                yield i, self.ways[i], slice(i * P, (i + 1) * P), slice(j * P, (j + 1) * P), j, 2 * self.quarter + j

    def low_rank(self, pe):
        k, b, L = self.k, self.b, self.L
        pe.wait_ge(k.act_step.sem, k.act_step.mark)
        for i, way, tokens, out, j, col in self.parts():
            rows, channels = slice(64 * way, 64 * way + 64), slice(col * P, (col + 1) * P)
            pe.matmul(k.bank(4 + 2 * i)[:, out], L.w2[rows, channels], b.z[rows, 24, tokens], start=True, stop=True)
            mm = pe.matmul(k.bank(5 + 2 * i)[:, out], L.a2[rows, channels], b.z[rows, 25, tokens], start=True, stop=True)
        mm.then_inc(k.low_rank.up(), 1)

    def sigmoids(self, act):
        k, b, L = self.k, self.b, self.L
        act.wait_ge(k.low_rank.sem, k.low_rank.count + (0 if self.first else 1))
        for i, way, tokens, out, j, col in self.parts():
            bias = slice(8 * way + col, 8 * way + col + 1)
            act.activation(b.sg[:, j, tokens], k.bank(4 + 2 * i)[:, out], ACT.Sigmoid, bias=L.w0[:, bias])
            last = act.activation(b.a[:, j, tokens], k.bank(5 + 2 * i)[:, out], ACT.Sigmoid, bias=L.a0[:, bias])
        last.then_inc(k.act_step.up(), 1)
        self.done["sigmoids"] = k.act_step.count

    def sums(self, dve):
        k, b = self.k, self.b
        chain = chained(k, dve)
        dve.wait_ge(k.act_step.sem, self.done["sigmoids"])
        chain(dve.tensor_tensor_scan(b.cum.rearrange("p j t -> p (j t)"), k.segments, b.sg.rearrange("p j t -> p (j t)"),
                                     0.0, ALU.mult, ALU.add))
        chain(dve.tensor_copy(self.tot, b.cum[:, :, 63::64]))
        for i in range(2):
            tokens = slice(i * P, (i + 1) * P)
            if self.ways[i] == 0:
                chain(dve.tensor_tensor(b.excl[:, :, tokens], b.cum[:, :, tokens], b.sg[:, :, tokens], ALU.subtract))
            else:
                by_chunk = [t[:, :, tokens].rearrange("p j (c t) -> p j c t", c=2) for t in (b.excl, b.cum)]
                chain(dve.tensor_tensor(by_chunk[0], self.tot[:, :, 2 * i:2 * i + 2].unsqueeze(3).broadcast_to([P, 2, 2, 64]), by_chunk[1],
                                        ALU.subtract))
                chain(dve.tensor_tensor(b.cum[:, :, tokens], b.excl[:, :, tokens], b.sg[:, :, tokens], ALU.add))
        self.done["sums"] = k.vec_step.count

    def exponentials(self, act):
        k, b = self.k, self.b
        C = math.exp(-0.5)
        act.wait_ge(k.vec_step.sem, self.done["sums"])
        act.activation(b.eX, b.excl, ACT.Exp, scale=-C).then_inc(k.act_step.up(), 1)
        self.done["eX"] = k.act_step.count
        act.activation(b.eN, b.cum, ACT.Exp, scale=C).then_inc(k.act_step.up(), 1)
        self.done["eN"] = k.act_step.count
        if self.emit:
            act.activation(b.eP, b.cum, ACT.Exp, scale=-C)
        act.activation(self.pc, self.tot, ACT.Exp, scale=-C).then_inc(k.act_step.up(), 1)
        self.done["eP"] = k.act_step.count

    def rates(self, dve):
        k, b = self.k, self.b
        chain = chained(k, dve)
        ka = self.L.k_a[:, 2 * self.quarter:2 * self.quarter + 2].unsqueeze(2).broadcast_to([P, 2, 256])
        chain(dve.scalar_tensor_tensor(b.kd, b.a, 1.0, ka, ALU.subtract, ALU.mult))
        chain(dve.scalar_tensor_tensor(b.kd, b.kd, 1.0, self.tiles(b.z, 8), ALU.add, ALU.mult))
        chain(dve.scalar_tensor_tensor(b.a, b.a, -1.0, self.tiles(b.kk), ALU.mult, ALU.mult))
        if self.emit:
            ks = self.tiles(b.kdsum)
            if self.sweep == 0:
                chain(dve.tensor_copy(ks, b.kd))
            else:
                chain(dve.tensor_tensor(ks, ks, b.kd, ALU.add))

    def scaled(self, dve):
        k, b = self.k, self.b
        chain = chained(k, dve)
        dve.wait_ge(k.act_step.sem, self.done["eN"])
        chain(dve.tensor_tensor(b.kh[:], b.kd, b.eN, ALU.mult))
        self.done["kh"] = k.vec_step.count
        chain(dve.tensor_tensor(b.nb[:], b.a, b.eN, ALU.mult))
        self.done["nb"] = k.vec_step.count


def rwkv_unit(k, b, operands, following):
    ways, quarter, sweep, emit, done = operands.ways, operands.quarter, operands.sweep, operands.emit, operands.done
    kts = slice(2 * quarter, 2 * quarter + 2)
    masks = [(k.up, k.up_incl, k.up8, k.up_far, k.lo8), (k.lo, k.lo_incl, k.lo8, k.lo_far, k.up8)]

    def masked(m, n):
        return m.unsqueeze(1).broadcast_to([P, n, P])

    def tokens(i):
        return slice(i * P, (i + 1) * P)

    vz, kk = operands.tiles(b.z, 16), operands.tiles(b.kk)
    marks = {}
    expert_weights(k)
    with k.stage() as block:
        if operands.first:
            block.tensor(operands.low_rank)
            block.scalar(operands.sigmoids)
            block.vector(operands.sums)
            block.scalar(operands.exponentials)
            block.vector(operands.rates)
            block.vector(operands.scaled)
            k.phase()

        @block.vector
        def _(dve):
            chain = chained(k, dve)
            dve.wait_ge(k.act_step.sem, done["eX"])
            chain(dve.tensor_tensor(b.kt[:], kk, b.eX, ALU.mult))
            marks["kt"] = k.vec_step.count
            if emit:
                dve.wait_ge(k.act_step.sem, done["eP"])
                chain(dve.tensor_tensor(b.rt[:], operands.tiles(b.z), b.eP, ALU.mult))
                marks["rt"] = k.vec_step.count
            use_rows(k, dve, 2)

        @block.gpsimd
        def _(pool):
            fetch_rows(k, pool)

        @block.scalar
        def _(act):
            act.wait_ge(k.multiplied.sem, k.multiplied.at(1))
            act.activation(b.V[:], k.bank(2).rearrange("p (i c) -> p i c", i=2), ACT.Copy).then_inc(k.act_step.up(), 1)
            for n, (name, t) in enumerate((("kt", b.kt), ("rt", b.rt)) if emit else (("kt", b.kt),)):
                act.wait_ge(k.vec_step.sem, marks[name])
                for hh in range(2):
                    act.activation(b.rhs4[:, :, :, 2 * n + hh, :], t[:].rearrange("p j (i t) -> p j i t", i=2), ACT.Copy,
                                   scale=k.half_mask[hh]).then_inc(k.act_step.up(), 1)
            marks["rhs"] = k.act_step.count
            act.wait_ge(k.multiplied.sem, k.multiplied.at(2))
            act.activation(b.khT[:], k.bank(6).rearrange("p (i c) -> p i c", i=2), ACT.Copy).then_inc(k.act_step.up(), 1)
            act.wait_ge(k.multiplied.sem, k.multiplied.at(3))
            act.activation(b.nbT[:], k.bank(7).rearrange("p (i c) -> p i c", i=2), ACT.Copy).then_inc(k.act_step.up(), 1)

        @block.tensor
        def _(pe):
            for i in range(2):
                for j in range(2):
                    at = (2 * i + j) * P
                    mm = pe.transpose(k.bank(2)[:, at:at + P], vz[:, j, tokens(i)], k.ident)
            mm.then_inc(k.multiplied.up(), 1)
            for bank, name, t in ((6, "kh", b.kh), (7, "nb", b.nb)):
                pe.wait_ge(k.vec_step.sem, done[name])
                for i in range(2):
                    for j in range(2):
                        at = (2 * i + j) * P
                        mm = pe.transpose(k.bank(bank)[:, at:at + P], t[:, j, tokens(i)], k.ident)
                mm.then_inc(k.multiplied.up(), 1)

        k.phase()
        width = 512 if emit else 256

        @block.tensor
        def _(pe):
            pe.wait_ge(k.vec_step.sem, k.vec_step.mark)
            pe.wait_ge(k.act_step.sem, marks["rhs"])
            for n in range(4):
                three = [k.bank(3 * (n % 2) + m) for m in range(3)]
                if n >= 2:
                    pe.wait_ge(k.vec_step.sem, k.vec_step.at(n - 1))
                i, j = n // 2, n % 2
                kh, nb = b.kh[:, j, tokens(i)], b.nb[:, j, tokens(i)]
                rhs = b.rhs4[:, j, i].rearrange("p a t -> p (a t)")[:, 0:width]
                pe.matmul(three[0][:, 0:width], kh, rhs, start=True, stop=True)
                pe.matmul(three[1][:, 0:width], nb, rhs, start=True, stop=True)
                for hh in range(2):
                    mm = pe.matmul(three[2][:, hh * P:(hh + 1) * P], b.rhs4[:, j, i, hh, :], nb, start=True, stop=True)
                mm.then_inc(k.multiplied.up(), 1)

        @block.vector
        def _(dve):
            use_rows(k, dve, 1)
            dve.wait_ge(k.vec_step.sem, k.vec_step.mark)
            dve.wait_ge(k.act_step.sem, marks["rhs"])
            for n in range(4):
                dve.wait_ge(k.multiplied.sem, k.multiplied.at(n + 1))
                i, hs = n // 2, slice(2 * (n % 2), 2 * (n % 2) + 2)
                strict, incl, near, far, back = masks[ways[i]]
                if n == 2:
                    use_rows(k, dve, 1)
                three = [k.bank(3 * (n % 2) + m).rearrange("p (h t) -> p h t", h=4) for m in range(3)]
                dve.tensor_tensor(b.MT[:, i, hs, :], three[0][:, 0:2, :], masked(strict, 2), ALU.mult)
                dve.tensor_tensor(b.LdT[:, i, hs, :], three[1][:, 0:2, :], masked(near, 2), ALU.mult)
                dve.tensor_tensor(b.NT[:, i, hs, :], three[1][:, 0:2, :], masked(far, 2), ALU.mult)
                if emit:
                    dve.tensor_tensor(b.ArT[:, i, hs, :], three[0][:, 2:4, :], masked(incl, 2), ALU.mult)
                    dve.tensor_tensor(b.AbT[:, i, hs, :], three[1][:, 2:4, :], masked(incl, 2), ALU.mult)
                dve.tensor_tensor(b.Ld[:, i, hs, :], three[2][:, 0:2, :], masked(back, 2), ALU.mult).then_inc(k.vec_step.up(), 1)

        @block.gpsimd
        def _(pool):
            fetch_rows(k, pool)

        k.phase()
        invert_unit_lower(k, block, 2, b.Ld, b.LdT, b.NT, (b.E1, b.E2, b.E3, b.X), b.TT,
                          following)
        k.phase()

        states = [b.states[ways[i]][:, kts, :] for i in range(2)]
        chunk = [[0, 1] if ways[i] == 0 else [1, 0] for i in range(2)]
        bR, bU, bS, bY = ([k.bank(4 * i + n, 256) for i in range(2)] for n in range(4))
        R, U = b.R, b.U

        def rows(n, i):
            return slice(64 * chunk[i][n], 64 * chunk[i][n] + 64)

        def summed(n, i):
            return k.multiplied.at(6 * n + i + 1)

        def solved(n, i):
            return k.multiplied.at(6 * n + 2 + i + 1)

        def stated(n, i):
            return k.multiplied.at(6 * n + 4 + i + 1)


        @block.vector
        def _(dve):
            dve.wait_ge(k.vec_step.sem, k.vec_step.mark)
            use_rows(k, dve, 1)
            if following is not None:
                following.sums(dve)

        @block.scalar
        def _(act):
            act.wait_ge(k.act_step.sem, k.act_step.mark)
            for n in range(2):
                for i in range(2):
                    act.wait_ge(k.multiplied.sem, summed(n, i))
                    act.activation(R[:, i, :], bR[i], ACT.Copy).then_inc(k.act_step.up(), 1)
                    marks["R", n, i] = k.act_step.count
                for i in range(2):
                    act.wait_ge(k.multiplied.sem, solved(n, i))
                    act.activation(U[rows(n, i), i, :], bU[i][rows(n, i), :], ACT.Copy).then_inc(k.act_step.up(), 1)
                    marks["U", n, i] = k.act_step.count
                if n == 0 and following is not None:
                    following.exponentials(act)

        @block.vector
        def _(dve):
            for n in range(2):
                use_rows(k, dve, 2)
                for i in range(2):
                    if emit:
                        dve.wait_ge(k.multiplied.sem, summed(n, i))
                        y = b.Y[rows(n, i), i, 256 * quarter:256 * quarter + 256]
                        if sweep == 0:
                            ins = dve.tensor_copy(y, bY[i][rows(n, i), :])
                        else:
                            ins = dve.tensor_tensor(y, y, bY[i][rows(n, i), :], ALU.add)
                        ins.then_inc(k.vec_step.up(), 1)
                        marks["y", n, i] = k.vec_step.count
                if following is not None:
                    (following.scaled if n else following.rates)(dve)
                use_rows(k, dve, 2)
                for i in range(2):
                    dve.wait_ge(k.multiplied.sem, stated(n, i))
                    for j in range(2):
                        c = chunk[i][n]
                        dve.scalar_tensor_tensor(states[i][:, j, :], bS[i][:, j * P:(j + 1) * P], operands.pc[:, j, 2 * i + c:2 * i + c + 1], k.blocks64,
                                                 ALU.mult, ALU.mult).then_inc(k.vec_step.up(), 1)
                    marks["S", n, i] = k.vec_step.count
            if emit:
                use_rows(k, dve, 1)
                for i in range(2):
                    dve.wait_ge(k.multiplied.sem, k.multiplied.at(12 + i + 1))
                    dve.wait_ge(k.vec_step.sem, marks["y", 1, i])
                    y = b.Y[:, i, 256 * quarter:256 * quarter + 256]
                    dve.tensor_tensor(y, y, bY[i], ALU.add).then_inc(k.vec_step.up(), 1)

        @block.gpsimd
        def _(pool):
            fetch_rows(k, pool)

        @block.tensor
        def _(pe):
            pe.wait_ge(k.vec_step.sem, k.vec_step.mark)
            pe.wait_ge(k.act_step.sem, k.act_step.mark)
            for n in range(2):
                for i in range(2):
                    if n:
                        pe.wait_ge(k.vec_step.sem, marks["S", 0, i])
                    for j in range(2):
                        js = slice(j * P, (j + 1) * P)
                        if emit:
                            pe.matmul(bY[i][:, js], b.rt[:, j, tokens(i)], states[i][:, j, :], start=True, stop=True)
                        pe.matmul(bR[i][:, js], b.kt[:, j, tokens(i)], states[i][:, j, :], start=True, stop=False, skip_group_check=True)
                        for hh in range(2):
                            h = 2 * j + hh
                            mm = pe.matmul(bR[i][:, 64 * h:64 * h + 64], b.MT[:, i, h, :], b.V[:, i, 64 * h:64 * h + 64], start=False,
                                           stop=True, skip_group_check=True)
                    mm.then_inc(k.multiplied.up(), 1)
                for i in range(2):
                    pe.matmul(bS[i], k.ident, states[i].rearrange("p j c -> p (j c)"), start=True, stop=False, skip_group_check=True)
                    for j in range(2):
                        js = slice(j * P, (j + 1) * P)
                        pe.matmul(bS[i][:, js], b.khT[rows(n, i), i, js], b.V[rows(n, i), i, js], start=False, stop=False, skip_group_check=True)
                for i in range(2):
                    pe.wait_ge(k.act_step.sem, marks["R", n, i])
                    for h in range(4):
                        hs = slice(64 * h, 64 * h + 64)
                        mm = pe.matmul(bU[i][:, hs], b.TT[:, i, h, :], R[:, i, hs], start=True, stop=True)
                    mm.then_inc(k.multiplied.up(), 1)
                for i in range(2):
                    pe.wait_ge(k.act_step.sem, marks["U", n, i])
                    for j in range(2):
                        js = slice(j * P, (j + 1) * P)
                        mm = pe.matmul(bS[i][:, js], b.nbT[rows(n, i), i, js], U[rows(n, i), i, js], start=False, stop=True, skip_group_check=True)
                    mm.then_inc(k.multiplied.up(), 1)
            if emit:
                for i in range(2):
                    pe.wait_ge(k.vec_step.sem, marks["y", 1, i])
                    for h in range(4):
                        hs = slice(64 * h, 64 * h + 64)
                        pe.matmul(bY[i][:, hs], b.ArT[:, i, h, :], b.V[:, i, hs], start=True, stop=False)
                        mm = pe.matmul(bY[i][:, hs], b.AbT[:, i, h, :], U[:, i, hs], start=False, stop=True)
                    mm.then_inc(k.multiplied.up(), 1)


def buffers(k, mem, **shapes):
    return names(**{name: mem.enter_context(k.sbuf(name, shape)) for name, shape in shapes.items()})


def rwkv(k, L, z, states, emit, o=None, spare=None):
    nc = k.nc
    with ExitStack() as mem:
        b = buffers(k, mem, kk=[8, 256])
        kz = z[:, 8:16, :]
        with buffers_scope(k, squares=[8, 256], norm=[8, 256]) as s, k.stage() as block:

            @block.vector
            def _(dve):
                chain = chained(k, dve)
                chain(dve.tensor_tensor(b.kk[:], kz, over_tokens(L.k_k, 8, 256), ALU.mult))
                use_rows(k, dve, 3)
                dve.wait_ge(k.act_step.sem, k.act_step.at(3 if emit else 2))
                chain(dve.tensor_scalar(s.norm[:], s.norm[:], 1e-12, None, ALU.max))
                chain(dve.reciprocal(s.norm[:], s.norm[:]))
                chain(dve.tensor_tensor(b.kk[:], b.kk[:], s.norm[:], ALU.mult))

            @block.gpsimd
            def _(pool):
                fetch_rows(k, pool)

            @block.scalar
            def _(act):
                act.wait_ge(k.vec_step.sem, k.vec_step.at(1))
                act.activation(s.squares[:], b.kk[:], ACT.Square).then_inc(k.act_step.up(), 1)
                act.activation(z[:, 24, :], z[:, 24, :], ACT.Tanh)
                if emit:
                    act.activation(z[:, 26:28, :], z[:, 26:28, :], ACT.Sigmoid).then_inc(k.act_step.up(), 1)
                act.wait_ge(k.multiplied.sem, k.multiplied.at(1))
                act.activation(s.norm[:], k.psum[:, 0:2048].rearrange("p (j t) -> p j t", j=8), ACT.Sqrt).then_inc(k.act_step.up(), 1)

            @block.tensor
            def _(pe):
                pe.wait_ge(k.act_step.sem, k.act_step.at(1))
                for j in range(8):
                    mm = pe.matmul(k.psum[:, 256 * j:256 * j + 256], k.blocks64, s.squares[:, j, :], start=True, stop=True)
                mm.then_inc(k.multiplied.up(), 1)

        if emit:
            b.Y, b.kdsum = o.rearrange("p j t -> p (j t)").rearrange("p (i c) -> p i c", i=2), spare
        with ExitStack() as inner:
            u = buffers(k, inner, tot=[2, 2, 4], pc=[2, 2, 4], scaled=[2, 2, 256], kt=[2, 256], rt=[2, 256], V=[2, 256],
                        khT=[2, 256], nbT=[2, 256], MT=[2, 4, P], LdT=[2, 4, P], NT=[2, 4, P], ArT=[2, 4, P], AbT=[2, 4, P],
                        Ld=[2, 4, P], rhs4=[2, 2, 4, P], X=[2, 4, P], TT=[2, 4, P])
            u.E1, u.E2 = u.rhs4[:, 0], u.rhs4[:, 1]
            u.R, u.U = (u.E1[:, n].rearrange("p a t -> p (a t)").rearrange("p (i c) -> p i c", i=2) for n in range(2))
            u.kh, u.nb = u.scaled[:, 0], u.scaled[:, 1]
            u.E3 = u.scaled[:].rearrange("p n j t -> p (n j t)").rearrange("p (i h t) -> p i h t", i=2, h=4)
            u.z, u.states, u.kk = z, states, b.kk
            if emit:
                u.Y, u.kdsum = b.Y, b.kdsum
            u.sg, u.a, u.cum, u.excl, u.eP, u.eN, u.eX, u.kd = (
                t[:, n].rearrange("p (j i) t -> p j (i t)", j=2) for t in (u.NT, u.LdT, u.X, u.Ld) for n in range(2))
            units = [Operands(k, u, L, quarter, sweep, emit) for quarter in range(4) for sweep in range(2)]
            for n, operands in enumerate(units):
                operands.first = n == 0
                rwkv_unit(k, u, operands, units[n + 1] if n + 1 < len(units) else None)
        if not emit:
            return
        heads, marks = 32, []
        g2 = buffers(k, mem, g2=[2, 1024]).g2
        with buffers_scope(k, squares=[heads, 64], row=[heads]) as s, k.stage() as block:

            @block.sync
            def _(sp):
                sp.dma_start(g2[:], L.g2).then_inc(k.loaded.up(16), 16)

            @block.vector
            def _(dve):
                chain = chained(k, dve)
                y = b.Y.rearrange("p i (h v) -> p (i h) v", v=64)
                row = s.row[:].unsqueeze(2).broadcast_to([P, heads, 64])
                chain(dve.tensor_reduce(s.row[:], y, AXX, ALU.add))
                chain(dve.tensor_scalar(s.row[:], s.row[:], 1.0 / 64, None, ALU.mult))
                chain(dve.tensor_tensor(y, y, row, ALU.subtract))
                chain(dve.tensor_tensor(s.squares[:], y, y, ALU.mult))
                chain(dve.tensor_reduce(s.row[:], s.squares[:], AXX, ALU.add))
                chain(dve.tensor_scalar(s.row[:], s.row[:], 1.0 / 64, 64e-5, ALU.mult, ALU.add))
                variance = k.vec_step.count
                dve.wait_ge(k.act_step.sem, k.act_step.at(1))
                chain(dve.reciprocal(s.row[:], s.row[:]))
                chain(dve.tensor_tensor(y, y, row, ALU.mult))
                marks.append(variance)

            @block.scalar
            def _(act):
                act.wait_ge(k.vec_step.sem, marks[0])
                act.activation(s.row[:], s.row[:], ACT.Sqrt).then_inc(k.act_step.up(), 1)

        with k.stage() as block:

            @block.tensor
            def _(pe):
                for j in range(8):
                    for i in range(2):
                        mm = pe.transpose(k.psum[:, 256 * j + P * i:256 * j + P * i + P], b.Y[:, i, P * j:P * j + P], k.ident)
                mm.then_inc(k.multiplied.up(), 1)
                pe.wait_ge(k.vec_step.sem, k.vec_step.at(2))
                for j in range(8):
                    mm = pe.matmul(k.psum[:, 2048 + 256 * j:2304 + 256 * j], k.blocks64, b.kdsum[:, j, :], start=True, stop=True)
                mm.then_inc(k.multiplied.up(), 1)
                pe.wait_ge(k.loaded.sem, k.loaded.count)
                pe.wait_ge(k.vec_step.sem, k.vec_step.at(3))
                for j in range(8):
                    out = k.psum[:, 256 * j:256 * j + 256]
                    pe.matmul(out, g2[:, 0, P * j:P * j + P], z[:, 26, :], start=True, stop=False)
                    mm = pe.matmul(out, g2[0:32, 1, P * j:P * j + P], z[0:32, 27, :], start=False, stop=True)
                mm.then_inc(k.multiplied.up(), 1)

            @block.vector
            def _(dve):
                chain = chained(k, dve)
                lower = k.psum[:, 0:2048].rearrange("p (j t) -> p j t", j=8)
                upper = k.psum[:, 2048:4096].rearrange("p (j t) -> p j t", j=8)
                chain(dve.tensor_tensor(b.kdsum, b.kdsum, z[:, 0:8, :], ALU.mult))
                chain(dve.tensor_tensor(b.kdsum, b.kdsum, over_tokens(L.r_k, 8, 256), ALU.mult))
                dve.wait_ge(k.multiplied.sem, k.multiplied.at(1))
                chain(dve.tensor_tensor(o, lower, over_tokens(L.lnx_g, 8, 256), ALU.mult))
                chain(dve.tensor_tensor(o, o, over_tokens(L.lnx_b, 8, 256), ALU.add))
                dve.wait_ge(k.multiplied.sem, k.multiplied.at(2))
                chain(dve.tensor_tensor(b.kk[:], upper, z[:, 16:24, :], ALU.mult))
                chain(dve.tensor_tensor(o, o, b.kk[:], ALU.add))
                dve.wait_ge(k.multiplied.sem, k.multiplied.at(3))
                chain(dve.tensor_tensor(o, o, lower, ALU.mult))


@contextmanager
def buffers_scope(k, **shapes):
    with ExitStack() as mem:
        yield buffers(k, mem, **shapes)


def conv_input(k, zc, u, reach):
    with k.stage() as block:

        @block.scalar
        def _(act):
            act.activation(zc[:, 8:16, :], zc[:, 8:16, :], ACT.Sigmoid).then_inc(k.act_step.up(), 1)

        @block.gpsimd
        def _(pool):
            pool.memset(u[:, :, 0:reach], 0.0).then_inc(k.pool_step.up(), 1)
            pool.memset(u[:, :, 256 + reach:256 + 2 * reach], 0.0).then_inc(k.pool_step.up(), 1)

        @block.vector
        def _(dve):
            dve.wait_ge(k.act_step.sem, k.act_step.at(1))
            dve.tensor_tensor(u[:, :, reach:reach + 256], zc[:, 0:8, :], zc[:, 8:16, :], ALU.mult).then_inc(k.vec_step.up(), 1)
            dve.wait_ge(k.pool_step.sem, k.pool_step.at(2))


def conv_taps(k, L, u, conv, reach, taps, first):

    def on_vector(dve):
        for n, (row, shift) in enumerate(taps):
            for j in range(8):
                src = u[:, j, reach + shift:reach + shift + 256]
                w = L.conv_w[:, 8 * row + j:8 * row + j + 1]
                if n or not first:
                    if n:
                        dve.wait_ge(k.vec_step.sem, k.vec_step.count - 7)
                    ins = dve.scalar_tensor_tensor(conv[:, j, :], src, w, conv[:, j, :], ALU.mult, ALU.add)
                else:
                    ins = dve.tensor_scalar(conv[:, j, :], src, w, None, ALU.mult)
                ins.then_inc(k.vec_step.up(), 1)

    return on_vector


def conv_output(k, L, conv, out):
    channel_norm(k, conv, out, 8, 1024, 1e-5, L.cnorm_g, L.cnorm_b, center=True)
    with k.stage() as block:

        @block.scalar
        def _(act):
            act.activation(conv, out, ACT.Sigmoid).then_inc(k.act_step.up(), 1)

        @block.vector
        def _(dve):
            dve.wait_ge(k.act_step.sem, k.act_step.at(1))
            dve.tensor_tensor(out, out, conv, ALU.mult).then_inc(k.vec_step.up(), 1)


def token_mixer(k, L, l, dram, x, mod, states, taps, emit, then):
    nc = k.nc
    with ExitStack() as mem:
        h = buffers(k, mem, h=[8, 256]).h
        expert_weights(k)
        channel_norm(k, x, h[:], 8, 1024, 1e-6, mod.scale1, mod.shift1)

        def rhs(t):
            return lambda j: t[:, j, :]

        if not emit:
            with buffers_scope(k, z=[28, 256]) as s:
                gemm(k, weight(dram.w_in[l, 8:28], 8), rhs(h), s.z[:, 8:28, :], then, shift=L.mu[:, :, 8:28])
                rwkv(k, L, s.z, states, False)
            return
        w_oA, w_oB, w_out = (weight(t[l], 8) for t in (dram.w_oA, dram.w_oB, dram.w_out))
        gates = [weight(dram.w_in[l, 44 + 8 * g:52 + 8 * g], 8) for g in range(2)]
        w_rwkv = weight(dram.w_in[l, 0:28], 8)
        m = buffers(k, mem, m=[8, 256]).m
        ga = buffers(k, mem, g=[8, 256]).g
        reach = max(abs(shift) for _, shift in taps)
        with buffers_scope(k, gb=[8, 256], zc=[16, 256], y=[8, 256], u=[8, 256 + 2 * reach]) as s:
            gemm(k, weight(dram.w_in[l, 28:44], 8), rhs(h), s.zc[:], gates[0])
            conv_input(k, s.zc[:], s.u, reach)
            conv, half = s.zc[:, 0:8, :], len(taps) // 2
            gemm(k, gates[0], rhs(h), ga[:], gates[1], sigmoid=L.gate_b[:, 0:8], beside=conv_taps(k, L, s.u, conv, reach, taps[:half], True))
            gemm(k, gates[1], rhs(h), s.gb[:], w_oB, sigmoid=L.gate_b[:, 8:16], beside=conv_taps(k, L, s.u, conv, reach, taps[half:], False))
            conv_output(k, L, conv, m[:])
            gemm(k, w_oB, rhs(m), s.y[:], w_rwkv)
            with k.stage() as block:

                @block.vector
                def _(dve):
                    dve.tensor_tensor(m[:], s.gb[:], s.y[:], ALU.mult).then_inc(k.vec_step.up(), 1)
        o = buffers(k, mem, o=[8, 256]).o
        with buffers_scope(k, z=[28, 256]) as s:
            gemm(k, w_rwkv, rhs(h), s.z[:], w_oA, shift=L.mu)
            rwkv(k, L, s.z, states, True, o[:], h[:])
        with buffers_scope(k, y=[8, 256]) as s:
            def gated(dve, block):
                return dve.tensor_tensor(block(s.y), block(s.y), block(ga), ALU.mult)

            def summed(dve, block):
                return dve.tensor_tensor(block(m), block(m), block(s.y), ALU.add)

            def onto_x(dve, block):
                return dve.scalar_tensor_tensor(block(x), block(s.y), mod.gate1[:, block.column], block(x), ALU.mult, ALU.add)

            gemm(k, w_oA, rhs(o), s.y[:], w_out, after=(gated, summed))
            gemm(k, w_out, rhs(m), s.y[:], then, after=(onto_x,))


HEADS, KEYS, TOPK, SLOTS = 8, 128, 16, 128
RING = 8
LOWEST = -3.0e38


def top16(k, dve, lists, values, work, best, index):
    up = k.vec_step

    def settled():
        dve.wait_ge(up.sem, up.count)

    for n in lists:
        dve.max(best[:, n, 0:8], values(n)).then_inc(up.up(), 1)
    settled()
    for n in lists:
        dve.max_index(index[:, n, 0:8], best[:, n, 0:8], values(n)).then_inc(up.up(), 1)
    for n in lists:
        dve.match_replace(work(n), best[:, n, 0:8], values(n), LOWEST).then_inc(up.up(), 1)
    settled()
    for n in lists:
        dve.max(best[:, n, 8:16], work(n)).then_inc(up.up(), 1)
    settled()
    for n in lists:
        dve.max_index(index[:, n, 8:16], best[:, n, 8:16], work(n)).then_inc(up.up(), 1)
    settled()


PASSES = [("u", 0), ("u", 1), ("v", 0), ("v", 1)]
HOSTED = 4


def expert_job(k, mem, dram):
    job = buffers(k, mem, tok=[2, 1024], gw=[2, SLOTS], dots=[2, SLOTS], gate=[8], ring=[HOSTED, 1024])
    job.eidx = mem.enter_context(k.sbuf("expert", [2 * SLOTS + RING], U32))
    job.tables = {"u": dram.peer_u, "v": dram.peer_v}
    return job


def host_rows(k, job, count):
    job.row, job.fetched, job.end, job.weighted, job.used = 0, 0, count, False, {}
    job.landed = [k.gathered[j].count for j in range(HOSTED)]
    k.job = job


def use_rows(k, dve, n):
    job = k.job
    if job is None:
        return
    for r in range(job.row, min(job.row + n, job.end if job.weighted else min(job.end, 2 * SLOTS))):
        (kind, tile), slot = PASSES[r // SLOTS], r % SLOTS
        dve.wait_ge(k.gathered[r % HOSTED].sem, job.landed[r % HOSTED] + 16 * (r // HOSTED + 1))
        row, dot = job.ring[:, r % HOSTED, :], job.dots[:, tile, slot:slot + 1]
        if kind == "u":
            ins = dve.tensor_tensor_reduce(row, row, job.tok[:, tile, :], 1.0, 0.0, ALU.mult, ALU.add, dot)
        else:
            dve.wait_ge(k.row_used.sem, k.row_used.count)
            ins = dve.scalar_tensor_tensor(job.tok[:, tile, :], row, dot, job.tok[:, tile, :], ALU.mult, ALU.add)
        ins.then_inc(k.row_used.up(), 1)
        job.used[r], job.row = k.row_used.count, r + 1


def fetch_rows(k, pool):
    job = k.job
    if job is None:
        return
    for r in range(job.fetched, min(job.row + HOSTED, job.end)):
        if r >= HOSTED:
            pool.wait_ge(k.row_used.sem, job.used[r - HOSTED])
        (kind, tile), slot = PASSES[r // SLOTS], r % SLOTS
        number = tile * SLOTS + slot
        pool.indirect_dma_start(
            job.ring[:, r % HOSTED, :], None, job.tables[kind],
            bass.IndirectOffsetOnAxis(ap=job.eidx[:, number:number + 1], axis=0),
        ).then_inc(k.gathered[r % HOSTED].up(16), 16)
        job.fetched = r + 1


def expert_weights(k):
    job = k.job
    if job is None or job.weighted or job.row < 2 * SLOTS:
        return
    job.weighted = True
    with k.stage() as block:

        @block.scalar
        def _(act):
            act.wait_ge(k.row_used.sem, k.row_used.count)
            act.activation(job.dots[:], job.dots[:], ACT.Gelu).then_inc(k.act_step.up(), 1)

        @block.vector
        def _(dve):
            dve.wait_ge(k.row_used.sem, k.row_used.count)
            dve.memset(job.tok[:], 0.0).then_inc(k.vec_step.up(), 1)
            dve.wait_ge(k.act_step.sem, k.act_step.at(1))
            dve.tensor_tensor(job.dots[:], job.dots[:], job.gw[:], ALU.mult).then_inc(k.vec_step.up(), 1)


def choose_experts(k, l, dram, x, mod, job, hosted, then):
    nc = k.nc
    eidx = job.eidx
    with ExitStack() as mem:
        b = buffers(k, mem, h=[8, 256])
        channel_norm(k, x, b.h[:], 8, 1024, 1e-6, mod.scale2, mod.shift2)
        with buffers_scope(k, q=[16, 256], keys=[16, P], s=[16, P], work=[16, P], best1=[16, 16], cand=[HEADS, 256],
                           cand2=[HEADS, 256], best=[HEADS, 16], i12=[16, 16], pf=[2, HEADS, 16], hot=[HEADS, 16, 16],
                           e12=[2, HEADS, 16], row=[HEADS]) as s, \
                k.sbuf("idx1", [16, 16], U32) as idx1, k.sbuf("pos", [HEADS, 16], U32) as pos, \
                k.sbuf("posab", [2, HEADS, 16], U32) as posab:
            load(k, (s.keys[:], dram.sub_keys[l]))
            gemm(k, weight(dram.w_q[l], 8), lambda j: b.h[:, j, :], s.q[:], then)
            for tile in range(2):
                toks = slice(tile * P, tile * P + P)
                if tile == 1:
                    host_rows(k, job, hosted)
                with k.stage() as block:

                    @block.gpsimd
                    def _(pool):
                        fetch_rows(k, pool)

                    @block.tensor
                    def _(pe):
                        for n in range(16):
                            mm = pe.matmul(k.psum[:, n * P:n * P + P], s.q[:, n, toks], s.keys[:, n, :], start=True, stop=True)
                        mm.then_inc(k.multiplied.up(), 1)
                        for j in range(8):
                            mm = pe.transpose(k.psum[:, 2048 + j * P:2048 + j * P + P], b.h[:, j, toks], k.ident)
                        mm.then_inc(k.multiplied.up(), 1)

                    @block.scalar
                    def _(act):
                        act.wait_ge(k.multiplied.sem, k.multiplied.at(1))
                        act.activation(s.s[:], k.psum[:, 0:2048].rearrange("p (n c) -> p n c", n=16), ACT.Copy).then_inc(k.act_step.up(), 1)
                        act.wait_ge(k.multiplied.sem, k.multiplied.at(2))
                        act.activation(job.tok[:, tile, :], k.psum[:, 2048:3072], ACT.Copy).then_inc(k.act_step.up(), 1)

                    @block.vector
                    def _(dve):
                        chain = chained(k, dve)
                        if tile == 0:
                            chain(dve.tensor_copy(job.gate[:], mod.gate2))
                        dve.wait_ge(k.act_step.sem, k.act_step.at(1))
                        top16(k, dve, range(16), lambda n: s.s[:, n, :], lambda n: s.work[:, n, :], s.best1, idx1)
                        two = s.best1[:].rearrange("p (h c) j -> p h c j", c=2)
                        chain(dve.tensor_tensor(s.cand[:].rearrange("p h (a b) -> p h a b", b=16),
                                                two[:, :, 0, :].unsqueeze(3).broadcast_to([P, HEADS, 16, 16]),
                                                two[:, :, 1, :].unsqueeze(2).broadcast_to([P, HEADS, 16, 16]), ALU.add))
                        top16(k, dve, range(HEADS), lambda n: s.cand[:, n, :], lambda n: s.cand2[:, n, :], s.best, pos)
                        chain(dve.tensor_scalar(posab[:, 0], pos[:], 4, None, ALU.logical_shift_right))
                        chain(dve.tensor_scalar(posab[:, 1], pos[:], 15, None, ALU.bitwise_and))
                        chain(dve.tensor_copy(s.pf[:], posab[:]))
                        chain(dve.tensor_copy(s.i12[:], idx1[:]))
                        i2 = s.i12[:].rearrange("p (h c) j -> p h c j", c=2)
                        iota = k.iota16.unsqueeze(1).unsqueeze(1).broadcast_to([P, HEADS, 16, 16])
                        for c in range(2):
                            chain(dve.tensor_tensor(s.hot[:], s.pf[:, c].unsqueeze(3).broadcast_to([P, HEADS, 16, 16]), iota, ALU.is_equal))
                            chain(dve.tensor_tensor(s.hot[:], s.hot[:], i2[:, :, c, :].unsqueeze(2).broadcast_to([P, HEADS, 16, 16]), ALU.mult))
                            chain(dve.tensor_reduce(s.e12[:, c], s.hot[:], AXX, ALU.add))
                        chain(dve.scalar_tensor_tensor(s.e12[:, 0], s.e12[:, 0], float(KEYS), s.e12[:, 1], ALU.mult, ALU.add))
                        chain(dve.tensor_scalar(eidx[:, tile * SLOTS:(tile + 1) * SLOTS], s.e12[:, 0].rearrange("p h j -> p (h j)"), float(l * KEYS * KEYS), None, ALU.add))
                        if tile == 0:
                            chain(dve.tensor_copy(eidx[:, 2 * SLOTS:2 * SLOTS + RING], eidx[:, 0:RING]))
                        gw = job.gw[:, tile, :].rearrange("p (h j) -> p h j", j=16)
                        chain(dve.tensor_tensor(gw, s.best[:], s.best[:, :, 0:1].broadcast_to([P, HEADS, 16]), ALU.subtract))

                with k.stage() as block:

                    @block.scalar
                    def _(act):
                        act.activation(job.gw[:, tile, :], job.gw[:, tile, :], ACT.Exp).then_inc(k.act_step.up(), 1)

                    @block.vector
                    def _(dve):
                        chain = chained(k, dve)
                        dve.wait_ge(k.act_step.sem, k.act_step.at(1))
                        gw = job.gw[:, tile, :].rearrange("p (h j) -> p h j", j=16)
                        chain(dve.tensor_reduce(s.row[:], gw, AXX, ALU.add))
                        chain(dve.reciprocal(s.row[:], s.row[:]))
                        chain(dve.tensor_tensor(gw, gw, s.row[:].unsqueeze(2).broadcast_to([P, HEADS, 16]), ALU.mult))


def finish_experts(k, x, job):
    eidx, passes, done = job.eidx, PASSES[job.end // SLOTS:], job.end % SLOTS // (2 * RING)
    assert job.end % (2 * RING) == 0
    with_dots = passes[0][0] == "u"
    weights_done = 0 if with_dots else 2 * done
    weighted_first = sum(kind == "u" for kind, _ in passes)
    while job.row < job.end or not (job.weighted or with_dots):
        expert_weights(k)
        if job.row < job.end:
            with k.stage() as block:

                @block.vector
                def _(dve):
                    use_rows(k, dve, SLOTS)

                @block.gpsimd
                def _(pool):
                    fetch_rows(k, pool)
    k.job = None
    with ExitStack() as inner:
        r = buffers(k, inner, ring=[RING, 1024], dot8=[2, RING], act8=[2, RING])
        idx8 = [inner.enter_context(k.sbuf("expert_group", [RING], U32)) for _ in range(2)]
        groups = SLOTS // RING
        rounds = groups // 2
        with k.stage() as block:
            def turn(n, i, part):
                return i * 2 + (n * groups + part - 2 * done)

            @block.gpsimd
            def _(pool):
                for n, (kind, tile) in enumerate(passes):
                    table = job.tables[kind]

                    def gather(i, part, first=False):
                        g = turn(n, i, part)
                        pool.wait_ge(k.staged.sem, g + k.staged.at(1))
                        pool.sem_inc(k.slot_free.sem, 1)
                        for j in range(RING):
                            if not first:
                                pool.wait_ge(k.row_used.sem, g * RING + (k.row_used.at(1) + j - RING))
                                pool.sem_inc(k.slot_free.sem, 1)
                            pool.indirect_dma_start(
                                r.ring[:, j, :], None, table,
                                bass.IndirectOffsetOnAxis(ap=idx8[part][:, j:j + 1], axis=0),
                            ).then_inc(k.gathered[j].sem, 16)

                    start = 0
                    if n == 0:
                        gather(done, 0, True)
                        gather(done, 1)
                        start = done + 1
                    if start < rounds:
                        with pool.Fori(start, rounds) as i:
                            gather(i, 0)
                            gather(i, 1)

            @block.vector
            def _(dve):
                start = passes[0][1] * SLOTS + 2 * RING * done
                dve.tensor_copy(idx8[0][:], eidx[:, start:start + RING]).then_inc(k.staged.sem, 1)
                dve.wait_ge(k.row_used.sem, k.row_used.at(0))
                for n, (kind, tile) in enumerate(passes):
                    if kind == "v" and with_dots:
                        if tile == 0:
                            dve.wait_ge(k.dots_kept.sem, k.dots_kept.at(groups * weighted_first - 2 * done))
                            dve.memset(job.tok[:], 0.0).then_inc(k.weighted.up(), 1)
                        dve.wait_ge(k.act_step.sem, k.act_step.at(tile + 1))
                        dve.tensor_tensor(job.dots[:, tile, :], job.dots[:, tile, :], job.gw[:, tile, :], ALU.mult).then_inc(k.weighted.up(), 1)
                        dve.wait_ge(k.weighted.sem, k.weighted.count)

                    def use(i, part):
                        g = turn(n, i, part)
                        at = i * (2 * RING) + part * RING
                        dve.tensor_copy(idx8[1 - part][:], eidx[:, bass.ds(at + (tile * SLOTS + RING), RING)]).then_inc(k.staged.sem, 1)
                        if kind == "v":
                            dve.tensor_copy(r.act8[:, part, :], job.dots[:, tile, bass.ds(at, RING)]).then_inc(k.weights_staged.sem, 1)
                            dve.wait_ge(k.weights_staged.sem, i * 2 + (k.weights_staged.at(1) + (n - weighted_first) * groups + part - weights_done))
                        for j in range(RING):
                            dve.wait_ge(k.gathered[j].sem, g * 16 + k.gathered[j].at(16))
                            if kind == "u":
                                dve.tensor_tensor_reduce(r.ring[:, j, :], r.ring[:, j, :], job.tok[:, tile, :], 1.0, 0.0, ALU.mult,
                                                         ALU.add, r.dot8[:, part, j:j + 1]).then_inc(k.row_used.sem, 1)
                            else:
                                dve.wait_ge(k.row_used.sem, g * RING + (k.row_used.at(0) + j))
                                dve.scalar_tensor_tensor(job.tok[:, tile, :], r.ring[:, j, :], r.act8[:, part, j:j + 1],
                                                         job.tok[:, tile, :], ALU.mult, ALU.add).then_inc(k.row_used.sem, 1)
                        if kind == "u":
                            dve.wait_ge(k.row_used.sem, g * RING + k.row_used.at(RING))
                            dve.tensor_copy(job.dots[:, tile, bass.ds(at, RING)], r.dot8[:, part, :]).then_inc(k.dots_kept.sem, 1)

                    with dve.Fori(0 if n else done, rounds) as i:
                        use(i, 0)
                        use(i, 1)

            @block.scalar
            def _(act):
                for tile in range(2 if with_dots else 0):
                    if ("u", tile) in passes:
                        act.wait_ge(k.dots_kept.sem, k.dots_kept.at((passes.index(("u", tile)) + 1) * groups - 2 * done))
                    else:
                        act.wait_ge(k.row_used.sem, k.row_used.at(0))
                    act.activation(job.dots[:, tile, :], job.dots[:, tile, :], ACT.Gelu).then_inc(k.act_step.up(), 1)

            turns = len(passes) * groups - 2 * done
            k.staged.up(turns + 1)
            k.row_used.up(turns * RING)
            k.dots_kept.up(weighted_first * groups - 2 * done if with_dots else 0)
            k.weights_staged.up((len(passes) - weighted_first) * groups - weights_done)
            for j in range(RING):
                k.gathered[j].up(16 * turns)

        with k.stage() as block:

            @block.tensor
            def _(pe):
                for j in range(8):
                    for i in range(2):
                        mm = pe.transpose(k.psum[:, 256 * j + P * i:256 * j + P * i + P], job.tok[:, i, P * j:P * j + P], k.ident)
                mm.then_inc(k.multiplied.up(), 1)

            @block.vector
            def _(dve):
                dve.wait_ge(k.multiplied.sem, k.multiplied.at(1))
                for j in range(8):
                    dve.scalar_tensor_tensor(x[:, j, :], k.psum[:, 256 * j:256 * j + 256], job.gate[:, j:j + 1], x[:, j, :],
                                             ALU.mult, ALU.add).then_inc(k.vec_step.up(), 1)



DN_Q, DN_K, DN_V, DN_Z, CQ, CKV, KPE, GLA_Q, GLA_K, GLA_V, GLA_G, GLA_LR, FOX_Q, FOX_K, FOX_V, SMALL = (
    0, 2, 4, 6, 8, 10, 11, 12, 13, 14, 16, 18, 19, 21, 23, 25)
VECTORS2 = {"norm_mix_pre_2": 8, "norm_mix_post_2": 8, "norm_mlp_pre_2": 8, "norm_mlp_post_2": 8, "dn_conv_2": 24, "mla_q_norm_2": 2,
            "mla_kv_norm_2": 1, "gla_gate_bias_2": 1, "b_gate_2": 32, "dn_norm_2": 1, "gla_norm_2": 1}
ROWS2 = ("dn_dt_bias_2", "fox_f_bias_2", "dn_a_log_2")


def per_head(column, n):
    return column.unsqueeze(2).broadcast_to([P, 4, n])


def heads4(t):
    return t.rearrange("p (h c) -> p h c", h=4)


def for_heads(mask, n):
    return mask.unsqueeze(1).broadcast_to([P, n, mask.shape[1]])


def to_tokens(k, pairs):
    with k.stage() as block:

        @block.tensor
        def _(pe):
            for n, (src, _) in enumerate(pairs):
                for i in range(2):
                    mm = pe.transpose(k.psum[:, 256 * n + P * i:256 * n + P * i + P], src[:, P * i:P * i + P], k.ident)
            mm.then_inc(k.multiplied.up(), 1)

        @block.scalar
        def _(act):
            act.wait_ge(k.multiplied.sem, k.multiplied.at(1))
            for n, (_, dst) in enumerate(pairs):
                act.activation(dst, k.psum[:, 256 * n:256 * n + 256].rearrange("p (i c) -> p i c", i=2), ACT.Copy
                               ).then_inc(k.act_step.up(), 1)


def to_channels(k, y, out, gain=None, gate=None):
    with k.stage() as block:

        @block.tensor
        def _(pe):
            for j in range(2):
                for i in range(2):
                    mm = pe.transpose(k.psum[:, 256 * j + P * i:256 * j + P * i + P], y[:, i, P * j:P * j + P], k.ident)
            mm.then_inc(k.multiplied.up(), 1)

        @block.vector
        def _(dve):
            dve.wait_ge(k.multiplied.sem, k.multiplied.at(1))
            turned = k.psum[:, 0:512].rearrange("p (j t) -> p j t", j=2)
            if gate is None:
                dve.tensor_copy(out, turned).then_inc(k.vec_step.up(), 1)
            else:
                dve.scalar_tensor_tensor(out, turned, gain, gate, ALU.mult, ALU.mult).then_inc(k.vec_step.up(), 1)


def silu(k, t, tmp):
    with k.stage() as block:

        @block.scalar
        def _(act):
            act.activation(tmp, t, ACT.Sigmoid).then_inc(k.act_step.up(), 1)

        @block.vector
        def _(dve):
            dve.wait_ge(k.act_step.sem, k.act_step.at(1))
            dve.tensor_tensor(t, t, tmp, ALU.mult).then_inc(k.vec_step.up(), 1)


def softplus(k, y, tmp, out, scale):
    with k.stage() as block:

        @block.vector
        def _(dve):
            chain = chained(k, dve)
            chain(dve.scalar_tensor_tensor(tmp, y, -1.0, y, ALU.mult, ALU.min))
            dve.wait_ge(k.act_step.sem, k.act_step.at(2))
            chain(dve.scalar_tensor_tensor(out, y, 0.0, tmp, ALU.max, ALU.add))
            chain(dve.tensor_scalar(out, out, scale, None, ALU.mult))

        @block.scalar
        def _(act):
            act.wait_ge(k.vec_step.sem, k.vec_step.at(1))
            act.activation(tmp, tmp, ACT.Exp).then_inc(k.act_step.up(), 1)
            act.wait_ge(k.act_step.sem, k.act_step.at(1))
            act.activation(tmp, tmp, ACT.Ln, bias=1.0).then_inc(k.act_step.up(), 1)


def head_norm(k, y, squares, row):
    with k.stage() as block:
        marks = []

        @block.vector
        def _(dve):
            chain = chained(k, dve)
            chain(dve.tensor_tensor(squares, y, y, ALU.mult))
            chain(dve.tensor_reduce(row, squares, AXX, ALU.add))
            chain(dve.tensor_scalar(row, row, 1.0 / 64, 1e-6, ALU.mult, ALU.add))
            marks.append(k.vec_step.count)
            dve.wait_ge(k.act_step.sem, k.act_step.at(1))
            chain(dve.reciprocal(row, row))
            chain(dve.tensor_tensor(y, y, row.unsqueeze(2).broadcast_to([P, 8, 64]), ALU.mult))

        @block.scalar
        def _(act):
            act.wait_ge(k.vec_step.sem, marks[0])
            act.activation(row, row, ACT.Sqrt).then_inc(k.act_step.up(), 1)


def delta_branch(k, V, z, small, out):
    with buffers_scope(k, conv=[6, 256], tmp=[6, 256], ktok=[2, 256], vtok=[2, 256], km=[4, 256], qm=[4, 256], row=[8],
                       gcol=[2, 4], eg=[2, 4], bne=[2, 4], etail=[2, 4], eT=[2, 2, 4], D=[2, 4, P], L=[2, 4, P], Aq=[2, 4, P],
                       AqT=[2, 4, P], Ld=[2, 4, P], LdT=[2, 4, P], NT=[2, 4, P], E1=[2, 4, P], E2=[2, 4, P], E3=[2, 4, P],
                       X=[2, 4, P], TT=[2, 4, P], S=[2, P], R=[256], U=[2, 256], Y=[2, 256], inc=[2, P]) as b:
        beta, g = small.beta, small.g
        conv = b.conv
        with k.stage() as block:

            @block.vector
            def _(dve):
                chain = chained(k, dve)
                w = V.dn_conv_2.rearrange("p (r j) -> p r j", r=4)
                chain(dve.tensor_tensor(conv[:], z[:, 0:6, :], over_tokens(w[:, 3, :], 6, 256), ALU.mult))
                for r in range(3):
                    late = 3 - r
                    chain(dve.tensor_tensor(b.tmp[:, :, late:256], z[:, 0:6, 0:256 - late], over_tokens(w[:, r, :], 6, 256 - late), ALU.mult))
                    chain(dve.tensor_tensor(conv[:, :, late:256], conv[:, :, late:256], b.tmp[:, :, late:256], ALU.add))

        silu(k, conv[:], b.tmp[:])
        with k.stage() as block:

            @block.scalar
            def _(act):
                act.activation(b.tmp[:, 0:4, :], conv[:, 0:4, :], ACT.Square).then_inc(k.act_step.up(), 1)
                act.wait_ge(k.vec_step.sem, k.vec_step.at(1))
                act.activation(b.tmp[:, 0:4, :], b.tmp[:, 0:4, :], ACT.Sqrt).then_inc(k.act_step.up(), 1)

            @block.tensor
            def _(pe):
                pe.wait_ge(k.act_step.sem, k.act_step.at(1))
                for j in range(4):
                    mm = pe.matmul(k.psum[:, 256 * j:256 * j + 256], k.blocks64, b.tmp[:, j, :], start=True, stop=True)
                mm.then_inc(k.multiplied.up(), 1)

            @block.vector
            def _(dve):
                chain = chained(k, dve)
                dve.wait_ge(k.multiplied.sem, k.multiplied.at(1))
                t = b.tmp[:, 0:4, :]
                chain(dve.tensor_scalar(t, k.psum[:, 0:1024].rearrange("p (j t) -> p j t", j=4), 1e-6, None, ALU.add))
                dve.wait_ge(k.act_step.sem, k.act_step.at(2))
                chain(dve.reciprocal(t, t))
                chain(dve.tensor_tensor(conv[:, 0:4, :], conv[:, 0:4, :], t, ALU.mult))
                chain(dve.tensor_scalar(conv[:, 0:2, :], conv[:, 0:2, :], 64 ** -0.5, None, ALU.mult))
                for h in range(4):
                    chain(dve.tensor_scalar(b.qm[:, h, :], conv[:, h // 2, :], k.half_mask[h % 2], None, ALU.mult))
                    chain(dve.tensor_scalar(b.km[:, h, :], conv[:, 2 + h // 2, :], k.half_mask[h % 2], None, ALU.mult))
                chain(dve.memset(b.S[:], 0.0))

        to_tokens(k, [(conv[:, 2 + j, :], b.ktok[:, :, P * j:P * j + P]) for j in range(2)]
                  + [(conv[:, 4 + j, :], b.vtok[:, :, P * j:P * j + P]) for j in range(2)])
        for i in range(2):
            toks = slice(P * i, P * i + P)
            with k.stage() as block:

                @block.tensor
                def _(pe):
                    gi = g[:, i, :]
                    for n, m in enumerate((k.up_incl, k.blocks64, k.chunk0, k.chunk1)):
                        pe.matmul(k.bank(0)[:, 4 * n:4 * n + 4], m, gi, start=True, stop=True)
                    for h in range(4):
                        hs = slice(P * h, P * h + P)
                        pe.matmul(k.bank(1)[:, hs], g[:, i, h:h + 1].broadcast_to([P, P]), k.up_incl, start=True, stop=True)
                        pe.matmul(k.bank(2)[:, hs], b.km[:, h, toks], conv[:, 2 + h // 2, toks], start=True, stop=True)
                        mm = pe.matmul(k.bank(3)[:, hs], b.qm[:, h, toks], conv[:, 2 + h // 2, toks], start=True, stop=True)
                    mm.then_inc(k.multiplied.up(), 1)

                @block.vector
                def _(dve):
                    chain = chained(k, dve)
                    dve.wait_ge(k.multiplied.sem, k.multiplied.at(1))
                    sums = k.bank(0)
                    chain(dve.tensor_copy(b.gcol[:, i, :], sums[:, 0:4]))
                    chain(dve.tensor_tensor(b.etail[:, i, :], sums[:, 4:8], b.gcol[:, i, :], ALU.subtract))
                    chain(dve.tensor_copy(b.eT[:, i], sums[:, 8:16].rearrange("p (c h) -> p c h", c=2)))
                    for h in range(4):
                        chain(dve.tensor_scalar(b.D[:, i, h, :], k.bank(1)[:, P * h:P * h + P], -1.0, b.gcol[:, i, h:h + 1], ALU.mult, ALU.add))
                    chain(dve.tensor_tensor(b.D[:, i], b.D[:, i], for_heads(k.lo_incl, 4), ALU.mult))

            with k.stage() as block:

                @block.scalar
                def _(act):
                    act.activation(b.D[:, i], b.D[:, i], ACT.Exp).then_inc(k.act_step.up(), 1)
                    act.activation(b.eg[:, i, :], b.gcol[:, i, :], ACT.Exp).then_inc(k.act_step.up(), 1)
                    act.activation(b.etail[:, i, :], b.etail[:, i, :], ACT.Exp).then_inc(k.act_step.up(), 1)
                    act.activation(b.eT[:, i], b.eT[:, i], ACT.Exp).then_inc(k.act_step.up(), 1)

                @block.vector
                def _(dve):
                    chain = chained(k, dve)
                    dve.wait_ge(k.act_step.sem, k.act_step.at(4))
                    chain(dve.scalar_tensor_tensor(b.bne[:, i, :], b.eg[:, i, :], -1.0, beta[:, i, :], ALU.mult, ALU.mult))
                    chain(dve.tensor_tensor(b.D[:, i], b.D[:, i], for_heads(k.lo_incl, 4), ALU.mult))
                    chain(dve.scalar_tensor_tensor(b.L[:, i], heads4(k.bank(2)), -1.0, b.D[:, i], ALU.mult, ALU.mult))
                    chain(dve.tensor_tensor(b.L[:, i], b.L[:, i], for_heads(k.lo, 4), ALU.mult))
                    chain(dve.tensor_tensor(b.L[:, i], b.L[:, i], per_head(beta[:, i, :], P), ALU.mult))
                    chain(dve.tensor_tensor(b.Aq[:, i], heads4(k.bank(3)), b.D[:, i], ALU.mult))
                    chain(dve.tensor_tensor(b.Ld[:, i], b.L[:, i], for_heads(k.lo8, 4), ALU.mult))
                    chain(dve.tensor_tensor(heads4(b.vtok[:, i, :]), heads4(b.vtok[:, i, :]), per_head(beta[:, i, :], 64), ALU.mult))
                    chain(dve.tensor_tensor(heads4(b.ktok[:, i, :]), heads4(b.ktok[:, i, :]), per_head(b.etail[:, i, :], 64), ALU.mult))

            with k.stage() as block:

                @block.tensor
                def _(pe):
                    for h in range(4):
                        pe.transpose(k.bank(4)[:, P * h:P * h + P], b.L[:, i, h, :], k.ident)
                        mm = pe.transpose(k.bank(5)[:, P * h:P * h + P], b.Aq[:, i, h, :], k.ident)
                    mm.then_inc(k.multiplied.up(), 1)

                @block.vector
                def _(dve):
                    dve.wait_ge(k.multiplied.sem, k.multiplied.at(1))
                    dve.tensor_tensor(b.LdT[:, i], heads4(k.bank(4)), for_heads(k.up8, 4), ALU.mult).then_inc(k.vec_step.up(), 1)
                    dve.tensor_tensor(b.NT[:, i], heads4(k.bank(4)), for_heads(k.up_far, 4), ALU.mult).then_inc(k.vec_step.up(), 1)
                    dve.tensor_copy(b.AqT[:, i], heads4(k.bank(5))).then_inc(k.vec_step.up(), 1)

        with k.stage() as block:
            invert_unit_lower(k, block, 2, b.Ld, b.LdT, b.NT, (b.E1, b.E2, b.E3, b.X), b.TT)
        for i in range(2):
            toks = slice(P * i, P * i + P)
            bK, bQ, bU, bS, bY = (k.bank(n, 256) for n in range(5))
            y = b.Y[:, i, :]
            with k.stage() as block:
                marks = {}

                @block.vector
                def _(dve):
                    chain = chained(k, dve)
                    for c in range(2):
                        dve.wait_ge(k.multiplied.sem, k.multiplied.at(3 * c + 1))
                        chain(dve.tensor_tensor(heads4(b.R[:]), heads4(bK), per_head(b.bne[:, i, :], 64), ALU.mult))
                        chain(dve.tensor_tensor(b.R[:], b.R[:], b.vtok[:, i, :], ALU.add))
                        marks["R", c] = k.vec_step.count
                        if c == 0:
                            chain(dve.tensor_scalar(y, bQ, k.half_mask[0], None, ALU.mult))
                        else:
                            chain(dve.scalar_tensor_tensor(y, bQ, k.half_mask[1], y, ALU.mult, ALU.add))
                        dve.wait_ge(k.multiplied.sem, k.multiplied.at(3 * c + 2))
                        chain(dve.tensor_scalar(b.U[:, c, :], bU, k.half_mask[c], None, ALU.mult))
                        marks["U", c] = k.vec_step.count
                        dve.wait_ge(k.multiplied.sem, k.multiplied.at(3 * c + 3))
                        chain(dve.tensor_tensor(b.inc[:], bS.rearrange("p (j v) -> p j v", j=2), for_heads(k.blocks64, 2), ALU.mult))
                        S4 = b.S[:].rearrange("p j (h v) -> p (j h) v", h=2)
                        chain(dve.tensor_tensor(S4, S4, per_head(b.eT[:, i, c, :], 64), ALU.mult))
                        chain(dve.tensor_tensor(b.S[:], b.S[:], b.inc[:], ALU.add))
                        marks["S", c] = k.vec_step.count
                    chain(dve.tensor_tensor(heads4(y), heads4(y), per_head(b.eg[:, i, :], 64), ALU.mult))
                    chain(dve.tensor_tensor(b.U[:, 0, :], b.U[:, 0, :], b.U[:, 1, :], ALU.add))
                    marks["Usum"] = k.vec_step.count
                    dve.wait_ge(k.multiplied.sem, k.multiplied.at(7))
                    chain(dve.tensor_tensor(y, y, bY, ALU.add))

                @block.tensor
                def _(pe):
                    for c in range(2):
                        if c:
                            pe.wait_ge(k.vec_step.sem, marks["S", 0])
                        for j in range(2):
                            js = slice(P * j, P * j + P)
                            pe.matmul(bK[:, js], conv[:, 2 + j, toks], b.S[:, j, :], start=True, stop=True)
                            mm = pe.matmul(bQ[:, js], conv[:, j, toks], b.S[:, j, :], start=True, stop=True)
                        mm.then_inc(k.multiplied.up(), 1)
                        pe.wait_ge(k.vec_step.sem, marks["R", c])
                        for h in range(4):
                            hs = slice(64 * h, 64 * h + 64)
                            mm = pe.matmul(bU[:, hs], b.TT[:, i, h, :], b.R[:, hs], start=True, stop=True)
                        mm.then_inc(k.multiplied.up(), 1)
                        pe.wait_ge(k.vec_step.sem, marks["U", c])
                        for j in range(2):
                            js = slice(P * j, P * j + P)
                            mm = pe.matmul(bS[:, js], b.ktok[:, i, js], b.U[:, c, js], start=True, stop=True)
                        mm.then_inc(k.multiplied.up(), 1)
                    pe.wait_ge(k.vec_step.sem, marks["Usum"])
                    for h in range(4):
                        hs = slice(64 * h, 64 * h + 64)
                        mm = pe.matmul(bY[:, hs], b.AqT[:, i, h, :], b.U[:, 0, hs], start=True, stop=True)
                    mm.then_inc(k.multiplied.up(), 1)

        head_norm(k, b.Y[:].rearrange("p i (h v) -> p (i h) v", v=64), b.tmp[:, 0:2, :].rearrange("p i (h v) -> p (i h) v", v=64), b.row[:])
        silu(k, z[:, DN_Z:DN_Z + 2, :], b.tmp[:, 0:2, :])
        to_channels(k, b.Y, out, V.dn_norm_2, z[:, DN_Z:DN_Z + 2, :])


def gla_branch(k, V, z, gate_up, out):
    with buffers_scope(k, w=[256], tmp=[256], cum=[256], tot=[4], pc=[4], dist=[256], qin=[256], kin=[256], ktail=[256], qm=[4, 256],
                       ktok=[2, P], vtok=[2, 256], Vc=[2, 2, 256], AT=[2, 4, P], S=[256], inc=[256], Y=[2, 256], squares=[8, 64],
                       row=[8], tmp2=[2, 256]) as b:
        with k.stage() as block:

            @block.tensor
            def _(pe):
                pe.matmul(k.bank(0, 256), gate_up, z[0:16, GLA_LR, :], start=True, stop=True).then_inc(k.multiplied.up(), 1)

            @block.vector
            def _(dve):
                dve.wait_ge(k.multiplied.sem, k.multiplied.at(1))
                dve.tensor_scalar(b.w[:], k.bank(0, 256), V.gla_gate_bias_2, -1.0, ALU.add, ALU.mult).then_inc(k.vec_step.up(), 1)

        softplus(k, b.w[:], b.tmp[:], b.w[:], -1.0 / 16.0)
        with k.stage() as block:

            @block.vector
            def _(dve):
                chain = chained(k, dve)
                chain(dve.tensor_tensor_scan(b.cum[:], k.segments[:, 0:256], b.w[:], 0.0, ALU.mult, ALU.add))
                chain(dve.tensor_copy(b.tot[:], b.cum[:, 63::64]))
                chain(dve.tensor_tensor(b.dist[:].rearrange("p (c t) -> p c t", c=4), b.tot[:].unsqueeze(2).broadcast_to([P, 4, 64]),
                                        b.cum[:].rearrange("p (c t) -> p c t", c=4), ALU.subtract))
                dve.wait_ge(k.act_step.sem, k.act_step.at(4))
                chain(dve.scalar_tensor_tensor(b.qin[:], b.qin[:], 32 ** -0.5, z[:, GLA_Q, :], ALU.mult, ALU.mult))
                chain(dve.tensor_tensor(b.kin[:], b.kin[:], z[:, GLA_K, :], ALU.mult))
                chain(dve.tensor_tensor(b.ktail[:], b.dist[:], z[:, GLA_K, :], ALU.mult))
                for h in range(4):
                    chain(dve.tensor_scalar(b.qm[:, h, :], b.qin[:], k.quarter_mask[h], None, ALU.mult))
                chain(dve.memset(b.S[:], 0.0))
                chain(dve.memset(b.AT[:], 0.0))

            @block.scalar
            def _(act):
                act.wait_ge(k.vec_step.sem, k.vec_step.at(3))
                act.activation(b.qin[:], b.cum[:], ACT.Exp).then_inc(k.act_step.up(), 1)
                act.activation(b.kin[:], b.cum[:], ACT.Exp, scale=-1.0).then_inc(k.act_step.up(), 1)
                act.activation(b.pc[:], b.tot[:], ACT.Exp).then_inc(k.act_step.up(), 1)
                act.activation(b.dist[:], b.dist[:], ACT.Exp).then_inc(k.act_step.up(), 1)

        to_tokens(k, [(b.ktail[:], b.ktok[:])] + [(z[:, GLA_V + j, :], b.vtok[:, :, P * j:P * j + P]) for j in range(2)])
        with k.stage() as block:
            marks = {}

            @block.vector
            def _(dve):
                chain = chained(k, dve)
                for i in range(2):
                    for c in range(2):
                        chain(dve.tensor_scalar(b.Vc[:, i, c, :], b.vtok[:, i, :], k.half_mask[c], None, ALU.mult))
                marks["V"] = k.vec_step.count
                allowed = for_heads(k.up_incl, 4).bitcast(U32)
                for i in range(2):
                    dve.wait_ge(k.multiplied.sem, k.multiplied.at(i + 1))
                    chain(dve.copy_predicated(b.AT[:, i], allowed, heads4(k.bank(i))))
                marks["A"] = k.vec_step.count
                for n in range(4):
                    i, c = n // 2, n % 2
                    y = b.Y[:, i, :]
                    dve.wait_ge(k.multiplied.sem, k.multiplied.at(3 + n))
                    if c == 0:
                        chain(dve.tensor_scalar(y, k.bank(2, 256), k.half_mask[0], None, ALU.mult))
                    else:
                        chain(dve.scalar_tensor_tensor(y, k.bank(2, 256), k.half_mask[1], y, ALU.mult, ALU.add))
                    chain(dve.tensor_tensor(heads4(b.inc[:]), heads4(k.bank(3, 256)), per_head(k.quarters, 64), ALU.mult))
                    chain(dve.scalar_tensor_tensor(b.S[:], b.S[:], b.pc[:, n:n + 1], b.inc[:], ALU.mult, ALU.add))
                    marks["S", n] = k.vec_step.count
                dve.wait_ge(k.multiplied.sem, k.multiplied.at(7))
                chain(dve.tensor_tensor(b.Y[:], b.Y[:], k.bank(4).rearrange("p (i v) -> p i v", i=2), ALU.add))

            @block.tensor
            def _(pe):
                for i in range(2):
                    toks = slice(P * i, P * i + P)
                    pe.matmul(heads4(k.bank(i)), b.kin[:, toks], b.qm[:, :, toks], start=True, stop=True).then_inc(k.multiplied.up(), 1)
                pe.wait_ge(k.vec_step.sem, marks["V"])
                for n in range(4):
                    i, c = n // 2, n % 2
                    if n:
                        pe.wait_ge(k.vec_step.sem, marks["S", n - 1])
                    pe.matmul(k.bank(2, 256), b.qin[:, P * i:P * i + P], b.S[:], start=True, stop=True)
                    pe.matmul(k.bank(3, 256), b.ktok[:, i, :], b.Vc[:, i, c, :], start=True, stop=True).then_inc(k.multiplied.up(), 1)
                for i in range(2):
                    for h in range(4):
                        at = 256 * i + 64 * h
                        mm = pe.matmul(k.bank(4)[:, at:at + 64], b.AT[:, i, h, :], b.vtok[:, i, 64 * h:64 * h + 64], start=True, stop=True)
                mm.then_inc(k.multiplied.up(), 1)

        head_norm(k, b.Y[:].rearrange("p i (h v) -> p (i h) v", v=64), b.squares[:], b.row[:])
        silu(k, z[:, GLA_G:GLA_G + 2, :], b.tmp2[:])
        to_channels(k, b.Y, out, V.gla_norm_2, z[:, GLA_G:GLA_G + 2, :])


def attention(k, products, scale, mask, v, forget, out):
    with buffers_scope(k, vtok=[2, 256], F=[4, 256], lg=[4, 256], top=[4], total=[4], PT=[2, 4, P], Y=[2, 256]) as b:
        to_tokens(k, [(v[:, j, :], b.vtok[:, :, P * j:P * j + P]) for j in range(2)])
        if forget is not None:
            with k.stage() as block:

                @block.tensor
                def _(pe):
                    for h in range(4):
                        for m in range(2):
                            at = 256 * h + P * m
                            for i in range(m + 1):
                                mm = pe.matmul(k.psum[:, at:at + P], forget[:, i, h:h + 1].broadcast_to([P, P]),
                                               k.upto if i == m else k.ones, start=(i == 0), stop=(i == m))
                    mm.then_inc(k.multiplied.up(), 1)

                @block.vector
                def _(dve):
                    dve.wait_ge(k.multiplied.sem, k.multiplied.at(1))
                    dve.tensor_copy(b.F[:], heads4(k.psum[:, 0:1024])).then_inc(k.vec_step.up(), 1)

        for i in range(2):
            n = P * (i + 1)
            toks, keys = slice(P * i, n), slice(0, n)
            with k.stage() as block:
                logits = k.psum[:, 0:4 * 256].rearrange("p (h s) -> p h s", h=4)[:, :, 0:n]
                lg = b.lg[:, :, 0:n]
                marks = {}

                @block.vector
                def _(dve):
                    chain = chained(k, dve)
                    dve.wait_ge(k.multiplied.sem, k.multiplied.at(1))
                    if forget is None:
                        chain(dve.tensor_scalar(lg, logits, scale, None, ALU.mult))
                    else:
                        chain(dve.scalar_tensor_tensor(lg, logits, scale, b.F[:, :, 0:n], ALU.mult, ALU.subtract))
                    chain(dve.tensor_tensor(b.lg[:, :, toks], b.lg[:, :, toks], for_heads(mask, 4), ALU.add))
                    chain(dve.tensor_reduce(b.top[:], lg, AXX, ALU.max))
                    chain(dve.tensor_tensor(lg, lg, per_head(b.top[:], n), ALU.subtract))
                    marks["less"] = k.vec_step.count
                    dve.wait_ge(k.act_step.sem, k.act_step.at(1))
                    chain(dve.tensor_reduce(b.total[:], lg, AXX, ALU.add))
                    chain(dve.reciprocal(b.total[:], b.total[:]))
                    dve.wait_ge(k.multiplied.sem, k.multiplied.at(3))
                    y = heads4(b.Y[:, i, :])
                    chain(dve.tensor_tensor(y, heads4(k.bank(4, 256)), per_head(b.total[:], 64), ALU.mult))

                @block.scalar
                def _(act):
                    act.wait_ge(k.vec_step.sem, marks["less"])
                    act.activation(lg, lg, ACT.Exp).then_inc(k.act_step.up(), 1)
                    act.wait_ge(k.multiplied.sem, k.multiplied.at(2))
                    act.activation(b.PT[:, 0:i + 1], k.psum[:, 1024:1024 + 512 * (i + 1)].rearrange("p (m h t) -> p m h t", h=4, t=P),
                                   ACT.Copy).then_inc(k.act_step.up(), 1)

                @block.tensor
                def _(pe):
                    for h in range(4):
                        pairs = products(h, toks, keys)
                        for a, (q, kk) in enumerate(pairs):
                            mm = pe.matmul(logits[:, h, :], q, kk, start=(a == 0), stop=(a == len(pairs) - 1))
                    mm.then_inc(k.multiplied.up(), 1)
                    pe.wait_ge(k.act_step.sem, k.act_step.at(1))
                    for m in range(i + 1):
                        for h in range(4):
                            at = 1024 + 512 * m + P * h
                            mm = pe.transpose(k.psum[:, at:at + P], b.lg[:, h, P * m:P * m + P], k.ident)
                    mm.then_inc(k.multiplied.up(), 1)
                    pe.wait_ge(k.act_step.sem, k.act_step.at(2))
                    for h in range(4):
                        for m in range(i + 1):
                            mm = pe.matmul(k.bank(4)[:, 64 * h:64 * h + 64], b.PT[:, m, h, :], b.vtok[:, m, 64 * h:64 * h + 64],
                                           start=(m == 0), stop=(m == i))
                    mm.then_inc(k.multiplied.up(), 1)

        to_channels(k, b.Y, out)


def fox_branch(k, z, forget, out):
    with buffers_scope(k, qm=[4, 256]) as b:
        with k.stage() as block:

            @block.vector
            def _(dve):
                for h in range(4):
                    dve.tensor_scalar(b.qm[:, h, :], z[:, FOX_Q + h // 2, :], k.half_mask[h % 2], None, ALU.mult).then_inc(k.vec_step.up(), 1)

        attention(k, lambda h, toks, keys: [(b.qm[:, h, toks], z[:, FOX_K + h // 2, keys])], 64 ** -0.5, k.causal,
                  z[:, FOX_V:FOX_V + 2, :], forget, out)


def mla_branch(k, V, z, dram, gates, out):
    with buffers_scope(k, cq=[2, 256], ckv=[1, 256], q=[4, 256], kv=[4, 256], rot=[256], qm=[4, 256], qpm=[4, 256]) as b:
        channel_norm(k, z[:, CQ:CQ + 2, :], b.cq[:], 2, 256, 1e-6, V.mla_q_norm_2)
        channel_norm(k, z[:, CKV:CKV + 1, :], b.ckv[:], 1, 128, 1e-6, V.mla_kv_norm_2)
        gemm(k, weight(dram.mla_q_up, 2), lambda j: b.cq[:, j, :], b.q[:], weight(dram.mla_kv_up, 1))
        gemm(k, weight(dram.mla_kv_up, 1), lambda j: b.ckv[:, j, :], b.kv[:], gates[0])
        with k.stage() as block:

            @block.tensor
            def _(pe):
                pe.matmul(k.bank(0, 256), k.turn, b.q[:, 2, :], start=True, stop=True)
                pe.matmul(k.bank(1, 256), k.turn, z[:, KPE, :], start=True, stop=True).then_inc(k.multiplied.up(), 1)

            @block.vector
            def _(dve):
                chain = chained(k, dve)
                dve.wait_ge(k.multiplied.sem, k.multiplied.at(1))
                for n, t in enumerate((b.q[:, 2, :], z[:, KPE, :])):
                    chain(dve.tensor_tensor(b.rot[:], k.bank(n, 256), k.sin, ALU.mult))
                    chain(dve.tensor_tensor(t, t, k.cos, ALU.mult))
                    chain(dve.tensor_tensor(t, t, b.rot[:], ALU.add))
                for h in range(4):
                    chain(dve.tensor_scalar(b.qm[:, h, :], b.q[:, h // 2, :], k.half_mask[h % 2], None, ALU.mult))
                    chain(dve.tensor_scalar(b.qpm[:, h, :], b.q[:, 2, :], k.quarter_mask[h], None, ALU.mult))

        attention(k, lambda h, toks, keys: [(b.qm[:, h, toks], b.kv[:, h // 2, keys]), (b.qpm[:, h, toks], z[:, KPE, keys])],
                  96 ** -0.5, k.chunk_causal, b.kv[:, 2:4, :], None, out)


def second_block(k, dram, x):
    with ExitStack() as mem:
        lay = Layout(VECTORS2)
        c = buffers(k, mem, vec=[lay.width], rows=[12], gate_up=[P], h=[8, 256], branches=[4, 2, 256])
        load(k, (c.vec[:], dram.vectors2), (c.rows[:], dram.rows2), (c.gate_up[0:16, :], dram.gate_up))
        V = names(**{name: c.vec[:, a:z] for name, (a, z) in lay.at.items()})
        channel_norm(k, x[:], c.h[:], 8, 1024, 1e-6, V.norm_mix_pre_2)

        def rhs(t):
            return lambda j: t[:, j, :]

        gates = [weight(dram.w_gate_2[i], 8) for i in range(4)]
        ups = [weight(dram.w_branch_up_2[i], 2) for i in range(4)]
        w_out, w_mlp_in = weight(dram.w_out_2, 8), weight(dram.w_mlp_in_2, 8)
        with buffers_scope(k, z=[28, 256], rates=[2, 12], beta=[2, 4], y=[2, 8], tmp=[2, 8], ea=[4]) as s:
            gemm(k, weight(dram.w_in_2, 8), rhs(c.h), s.z[:], weight(dram.mla_q_up, 2))
            with k.stage() as block:

                @block.tensor
                def _(pe):
                    for i in range(2):
                        mm = pe.transpose(k.psum[:, P * i:P * i + P], s.z[:, SMALL, P * i:P * i + P], k.ident)
                    mm.then_inc(k.multiplied.up(), 1)

                @block.scalar
                def _(act):
                    act.wait_ge(k.vec_step.sem, k.vec_step.at(1))
                    turned = k.psum[:, 0:256].rearrange("p (i c) -> p i c", i=2)
                    act.activation(s.beta[:], turned[:, :, 0:4], ACT.Sigmoid).then_inc(k.act_step.up(), 1)
                    act.activation(s.ea[:], c.rows[:, 8:12], ACT.Exp).then_inc(k.act_step.up(), 1)

                @block.vector
                def _(dve):
                    chain = chained(k, dve)
                    dve.wait_ge(k.multiplied.sem, k.multiplied.at(1))
                    turned = k.psum[:, 0:256].rearrange("p (i c) -> p i c", i=2)
                    bias = c.rows[:, 0:8].unsqueeze(1).broadcast_to([P, 2, 8])
                    chain(dve.tensor_tensor(s.y[:], turned[:, :, 4:12], bias, ALU.add))
                    chain(dve.tensor_scalar(s.y[:, :, 4:8], s.y[:, :, 4:8], -1.0, None, ALU.mult))

            softplus(k, s.y[:], s.tmp[:], s.y[:], -1.0)
            with k.stage() as block:

                @block.vector
                def _(dve):
                    g = s.y[:, :, 0:4]
                    dve.tensor_tensor(g, g, s.ea[:].unsqueeze(1).broadcast_to([P, 2, 4]), ALU.mult).then_inc(k.vec_step.up(), 1)

            small = names(beta=s.beta, g=s.y[:, :, 0:4])
            delta_branch(k, V, s.z, small, c.branches[:, 0])
            mla_branch(k, V, s.z, dram, gates, c.branches[:, 1])
            gla_branch(k, V, s.z, c.gate_up[0:16, :], c.branches[:, 2])
            fox_branch(k, s.z, s.y[:, :, 4:8], c.branches[:, 3])
        with buffers_scope(k, merged=[8, 256], gate=[8, 256], up=[8, 256]) as s:
            def gated(dve, block):
                return dve.tensor_tensor(block(s.up if i else s.merged), block(s.gate), block(s.up), ALU.mult)

            def summed(dve, block):
                return dve.tensor_tensor(block(s.merged), block(s.merged), block(s.up), ALU.add)

            for i in range(4):
                gemm(k, gates[i], rhs(c.h), s.gate[:], ups[i], sigmoid=V.b_gate_2[:, 8 * i:8 * i + 8])
                gemm(k, ups[i], lambda j: c.branches[:, i, j, :], s.up[:], gates[i + 1] if i < 3 else w_out,
                     after=(gated, summed) if i else (gated,))
            gemm(k, w_out, rhs(s.merged), s.up[:], w_mlp_in)
            channel_norm(k, s.up[:], s.gate[:], 8, 1024, 1e-6, V.norm_mix_post_2)
            add_to(k, x[:], s.gate[:])
        channel_norm(k, x[:], c.h[:], 8, 1024, 1e-6, V.norm_mlp_pre_2)
        with buffers_scope(k, u=[32, 256], y=[8, 256], n=[8, 256]) as s:
            def relu_squared(dve, block):
                return dve.scalar_tensor_tensor(block(s.u), block(s.u), 0.0, block(s.u), ALU.max, ALU.mult)

            gemm(k, w_mlp_in, rhs(c.h), s.u[:], after=(relu_squared,))
            gemm(k, weight(dram.w_mlp_out_2, 32), rhs(s.u), s.y[:], own_ring=True)
            channel_norm(k, s.y[:], s.n[:], 8, 1024, 1e-6, V.norm_mlp_post_2)
            add_to(k, x[:], s.n[:])


def add_to(k, x, y):
    with k.stage() as block:

        @block.vector
        def _(dve):
            dve.tensor_tensor(x, x, y, ALU.add).then_inc(k.vec_step.up(), 1)


def layout_second(i):
    i = {n: a[0] for n, a in i.items() if n.endswith("_2")}
    a = {}
    at = np.cumsum([0, 768, 256, 4, 4, 256, 128, 32, 128, 128, 256, 256, 16, 256, 256, 256, 4])
    part = [i["w_in_2"][:, at[n]:at[n + 1]] for n in range(16)]
    qkv, dz, db, da, cq, ckv, kpe, gq, gk, gv, gg, lr, fq, fk, fv, ff = part
    w = np.concatenate([qkv, dz, cq, ckv, np.tile(kpe, (1, 4)), gq, gk, gv, gg, padded_to(lr, P), fq, fk, fv,
                        padded_to(np.concatenate([db, da, ff], axis=1), 3 * P)], axis=1)
    a["w_in_2"] = blocked(w, P)
    a["vectors2"] = np.concatenate([columns(np.tile(i[n], 2) if n in ("dn_norm_2", "gla_norm_2") else i[n]) for n in VECTORS2], axis=1)
    a["rows2"] = np.ascontiguousarray(np.broadcast_to(np.concatenate([i[n] for n in ROWS2])[None, :], (P, 12)))
    a["gate_up"] = i["gla_w_gate_up_2"]
    q = i["mla_w_q_up_2"].reshape(256, 4, 96)
    a["mla_q_up"] = blocked(padded_to(np.concatenate([q[:, :, :64].reshape(256, 256), q[:, :, 64:].reshape(256, 128)], axis=1), 4 * P), P)
    kv = i["mla_w_kv_up_2"].reshape(128, 4, 128)
    a["mla_kv_up"] = blocked(np.concatenate([kv[:, :, :64].reshape(128, 256), kv[:, :, 64:].reshape(128, 256)], axis=1), P)
    a["w_gate_2"] = np.stack([blocked(w, P) for w in i["w_gate_2"]])
    a["w_branch_up_2"] = np.stack([blocked(w, P) for w in i["w_branch_up_2"]])
    a["w_out_2"] = blocked(i["w_out_2"], P)
    a["w_mlp_in_2"] = blocked(i["w_mlp_in_2"], P)
    a["w_mlp_out_2"] = blocked(i["w_mlp_out_2"], P)
    return a


def constants(of_second=False):
    p, f = np.arange(P)[:, None], np.arange(P)[None, :]
    same, same8 = p // 64 == f // 64, p // 8 == f // 8
    t = np.arange(512)[None, :]
    freq = 1.0 / (10000.0 ** (np.arange(0, 32, 2, dtype=np.float32) / np.float32(32)))
    angle = (np.arange(256, dtype=np.float32)[:, None] * freq[None, :].astype(np.float32)).astype(np.float32)
    angle = np.concatenate([angle, angle], axis=1).T
    turn = np.zeros((P, P))
    for i in range(P):
        turn[i + 16 if i % 32 < 16 else i - 16, i] = -1.0 if i % 32 < 16 else 1.0
    table = {
        "ident": p == f, "ones": p * f >= 0, "blocks64": same,
        "up": same & (p < f), "lo": same & (p > f), "up_incl": same & (p <= f), "lo_incl": same & (p >= f),
        "up8": same8 & (p < f), "lo8": same8 & (p > f), "up_far": same & ~same8 & (p < f), "lo_far": same & ~same8 & (p > f),
        "halves": np.concatenate([p < 64, p >= 64], axis=1),
        "quarters": np.concatenate([p // 32 == i for i in range(4)], axis=1),
        "segments": np.broadcast_to(t % 64 != 0, (P, 512)), "iota16": np.broadcast_to(np.arange(16)[None, :], (P, 16)),
    }
    second = {
        "upto": p <= f, "chunk0": (p < 64) & (f >= 0), "chunk1": (p >= 64) & (f >= 0),
        "causal": np.where(f <= p, 0.0, -1e30), "chunk_causal": np.where(f // 64 <= p // 64, 0.0, -1e30),
        "turn": turn, "cos": np.tile(np.cos(angle), (4, 1)), "sin": np.tile(np.sin(angle), (4, 1)),
    }
    table = second if of_second else table
    return {n: np.asarray(a, np.float32) for n, a in table.items()}


class Layout:

    def __init__(self, widths):
        self.at, n = {}, 0
        for name, w in widths.items():
            self.at[name] = (n, n + w)
            n += w
        self.width = n


VECTORS = {"norm1_g": 8, "norm2_g": 8, "shift_mu": 56, "w0": 16, "a0": 16, "k_k": 8, "k_a": 8, "r_k": 8, "lnx_g": 8, "lnx_b": 8,
           "conv_w": 248, "cnorm_g": 8, "cnorm_b": 8, "gate_b": 16, "ada_b": 48}


def load_layer(k, mem, l, dram):
    lay = Layout(VECTORS)
    b = buffers(k, mem, vec=[lay.width], w2=[1024], a2=[1024])
    load(k, (b.vec[:], dram.vectors[l]), (b.w2[:], dram.w2[l]), (b.a2[:], dram.a2[l]))
    L = names(**{name: b.vec[:, a:z] for name, (a, z) in lay.at.items()})
    L.mu = L.shift_mu.rearrange("p (d j) -> p d j", d=2)
    L.w2, L.a2, L.g2 = b.w2, b.a2, dram.g2[l]
    return L


HOSTED_CONTEXT, HOSTED_FIRST, HOSTED_LAST = 336, 240, 0


def first_block(k, dram, x, xc):
    nc = k.nc
    with ExitStack() as mem:
        mods = buffers(k, mem, mods=[2, 48, 2]).mods
        with buffers_scope(k, c=[8, 2], sig=[8, 2]) as s:
            load(k, (s.c[:], dram.c))
            with k.stage() as block:

                @block.scalar
                def _(act):
                    act.activation(s.sig[:], s.c[:], ACT.Sigmoid).then_inc(k.act_step.up(), 1)

                @block.vector
                def _(dve):
                    dve.wait_ge(k.act_step.sem, k.act_step.at(1))
                    dve.tensor_tensor(s.c[:], s.c[:], s.sig[:], ALU.mult).then_inc(k.vec_step.up(), 1)

            modulation_rows(k, dram.ada_w, s.c, mods[:].rearrange("p l j c -> p (l j) c"))
        job = expert_job(k, mem, dram)
        states = [buffers(k, mem, state=[8, P]).state for d in range(2)]
        for l in range(2):
            with ExitStack() as layer_mem:
                L = load_layer(k, layer_mem, l, dram)
                m = buffers(k, layer_mem, mod=[2, 48])
                with k.stage() as block:

                    @block.vector
                    def _(dve):
                        chain = chained(k, dve)
                        for d in range(2):
                            chain(dve.memset(states[d][:], 0.0))
                        for c in range(2):
                            chain(dve.tensor_tensor(m.mod[:, c, :], mods[:, l, :, c], L.ada_b, ALU.add))
                            for at, gain in ((8, L.norm1_g), (32, L.norm2_g)):
                                part = m.mod[:, c, at:at + 8]
                                chain(dve.scalar_tensor_tensor(part, part, 1.0, gain, ALU.add, ALU.mult))


                def modulation(c):
                    shift1, scale1, gate1, shift2, scale2, gate2 = (m.mod[:, c, 8 * i:8 * i + 8] for i in range(6))
                    return names(shift1=shift1, scale1=scale1, gate1=gate1, shift2=shift2, scale2=scale2, gate2=gate2)

                last = l == 1
                mx, mc = modulation(0), modulation(1)
                w_q, w_mix = weight(dram.w_q[l], 8), weight(dram.w_in[l, 28:44], 8)
                token_mixer(k, L, l, dram, xc[:], mc, states, [(15, 0)] + [(r, r - 15) for r in range(31) if r != 15],
                            not last, w_mix if last else w_q)
                k.dump(f"xc_mix{l}", xc[:])
                if last:
                    finish_experts(k, x[:], job)
                    k.dump("x_peer0", x[:])
                else:
                    choose_experts(k, l, dram, xc[:], mc, job, HOSTED_CONTEXT, w_mix)
                token_mixer(k, L, l, dram, x[:], mx, states, [(15, 0)] + [(r, 64 * (r - 15)) for r in range(12, 19) if r != 15],
                            True, w_q)
                k.dump(f"x_mix{l}", x[:])
                if not last:
                    finish_experts(k, xc[:], job)
                choose_experts(k, l, dram, x[:], mx, job, HOSTED_LAST if last else HOSTED_FIRST, weight(dram.w_in_2, 8) if last else weight(dram.w_in[1, 8:28], 8))
                if last:
                    finish_experts(k, x[:], job)
                    k.dump("x_peer1", x[:])


def program(nc, dram, dump=None):
    with ExitStack() as ctx:
        k = Core(nc, ctx)
        k.dump = dump(k) if dump else lambda name, ap: None
        lay = Layout({n: a.shape[1] for n, a in constants().items()})
        table = ctx.enter_context(nc.sbuf_tensor("constants", [P, lay.width], F32))
        (k.ident, k.ones, k.blocks64, k.up, k.lo, k.up_incl, k.lo_incl, k.up8, k.lo8, k.up_far, k.lo_far,
         k.halves, k.quarters, k.segments, k.iota16) = (
            table[:, a:z] for a, z in lay.at.values())
        k.half_mask = [k.halves[:, i:i + 1] for i in range(2)]
        k.quarter_mask = [k.quarters[:, i:i + 1] for i in range(4)]
        k.ring = ctx.enter_context(k.sbuf("weight_ring", [SLOTS_W, 8 * P]))
        x = ctx.enter_context(nc.sbuf_tensor("x_tokens", [P, 8, 256], F32))
        with nc.sbuf_tensor("context_tokens", [P, 8, 256], F32) as xc:
            load(k, (table[:], dram.constants), (x[:], dram.x), (xc[:], dram.ctx))
            first_block(k, dram, x, xc)
        channel_norm(k, x[:], x[:], 8, 1024, 1e-6, k_final(k, ctx, dram))
        k.dump("x_first", x[:])
        lay2 = Layout({n: a.shape[1] for n, a in constants(of_second=True).items()})
        table2 = ctx.enter_context(nc.sbuf_tensor("constants_second", [P, lay2.width], F32))
        load(k, (table2[:], dram.constants_second))
        (k.upto, k.chunk0, k.chunk1, k.causal, k.chunk_causal, k.turn, k.cos, k.sin) = (table2[:, a:z] for a, z in lay2.at.values())
        second_block(k, dram, x)
        with buffers_scope(k, rows=[2, 1024]) as s, k.stage() as block:

            @block.tensor
            def _(pe):
                for i in range(2):
                    for j in range(8):
                        mm = pe.transpose(k.psum[:, 1024 * i + P * j:1024 * i + P * j + P], x[:, j, P * i:P * i + P], k.ident)
                mm.then_inc(k.multiplied.up(), 1)

            @block.scalar
            def _(act):
                act.wait_ge(k.multiplied.sem, k.multiplied.at(1))
                act.activation(s.rows[:], k.psum[:, 0:2048].rearrange("p (i c) -> p i c", i=2), ACT.Copy).then_inc(k.act_step.up(), 1)

            @block.sync
            def _(sp):
                sp.wait_ge(k.act_step.sem, k.act_step.at(1))
                sp.dma_start(dram.out.rearrange("b (i p) c -> p (b i) c", p=P), s.rows[:]).then_inc(k.stored.up(16), 16)
                sp.wait_ge(k.stored.sem, k.stored.count)


def k_final(k, ctx, dram):
    g = ctx.enter_context(k.nc.sbuf_tensor("final_g", [P, 8], F32))
    load(k, (g[:], dram.final_g))
    return g[:]




def columns(v):
    v = np.asarray(v)
    n = -(-v.shape[-1] // P) * P
    out = np.zeros((*v.shape[:-1], n), v.dtype)
    out[..., :v.shape[-1]] = v
    return np.ascontiguousarray(out.reshape(-1, P).T)


def blocked(w, cols):
    w = np.asarray(w)
    k, n = w.shape
    kt = -(-k // P)
    padded = np.zeros((kt * P, -(-n // cols) * cols), w.dtype)
    padded[:k, :n] = w
    return np.ascontiguousarray(padded.reshape(kt, P, -1, cols).transpose(2, 1, 0, 3).reshape(-1, P, kt * cols))


def padded_to(w, n):
    out = np.zeros((w.shape[0], n), w.dtype)
    out[:, :w.shape[1]] = w
    return out


def layout(i):
    i = {n: np.asarray(a) for n, a in i.items()}
    a = {}
    a["x"] = np.ascontiguousarray(i["x"][0].T.reshape(8, P, 256).transpose(1, 0, 2))
    a["ctx"] = np.ascontiguousarray(i["ctx"][0].T.reshape(8, P, 256).transpose(1, 0, 2))
    a["c"] = np.ascontiguousarray(np.stack([columns(i["c"][0]), columns(i["c_ctx"])], axis=2))
    a["constants"] = np.concatenate(list(constants().values()), axis=1)
    a["constants_second"] = np.concatenate(list(constants(of_second=True).values()), axis=1)
    a["final_g"] = columns(i["final_g"])
    a["vectors"] = np.stack([np.concatenate([columns(i[n][l].reshape(-1) if n == "r_k" else i[n][l]) for n in VECTORS], axis=1) for l in range(2)])
    a["ada_w"] = np.concatenate([blocked(i["ada_w"][l], 512) for l in range(2)])
    a["w_in"] = np.stack([np.concatenate([blocked(i["w_in"][l][:, :3488], P), blocked(i["w_in"][l][:, 3488:], P)]) for l in range(2)])
    a["w2"] = np.ascontiguousarray(i["w2"].reshape(2, P, 1024))
    a["a2"] = np.ascontiguousarray(i["a2"].reshape(2, P, 1024))
    g2 = np.zeros((2, 256, 1024), np.float32)
    g2[:, :160] = i["g2"]
    a["g2"] = np.ascontiguousarray(g2.reshape(2, 2, P, 1024).transpose(0, 2, 1, 3))
    for n in ("w_oA", "w_oB", "w_out", "w_q"):
        a[n] = np.stack([blocked(i[n][l], P) for l in range(2)])
    a["sub_keys"] = np.ascontiguousarray(i["sub_keys"].transpose(0, 4, 1, 2, 3).reshape(2, P, 16, P))
    a["peer_u"] = i["peer_u"].reshape(-1, 1024)
    a["peer_v"] = i["peer_v"].reshape(-1, 1024)
    a.update(layout_second(i))
    return a


def kernel(**inputs):
    import concourse.bacc as bacc
    from concourse.bass_utils import run_bass_kernel_spmd

    nc = bacc.Bacc("TRN2", target_bir_lowering=False, num_devices=1)
    arrays = {f"in_{n}": a for n, a in layout(inputs).items()}
    dram = names(**{n[3:]: nc.dram_tensor(n, a.shape, mybir.dt.from_np(a.dtype), kind="ExternalInput").ap()
                              for n, a in arrays.items()})
    dram.out = nc.dram_tensor("out_tokens", (1, 256, 1024), F32, kind="ExternalOutput").ap()
    program(nc, dram)
    return run_bass_kernel_spmd(nc, [arrays], core_ids=[0]).results[0]["out_tokens"]
```
